# Optimizing a Trainium2 kernel written in Bass

```python
import math
import jax, jax.numpy as jnp
from jax import lax
import numpy as np

D_MODEL = 1024
BATCH = 1
SEQ = 1024
DEPTH = 2

CHUNK = 64
MIX_WIDTH = D_MODEL
CONV_CH = MIX_WIDTH // 2
ATTN_WIDTH = MIX_WIDTH - CONV_CH
HEAD_DIM = 64
N_Q_HEADS = ATTN_WIDTH // HEAD_DIM
N_KV_HEADS = 2
GQA_GROUP = N_Q_HEADS // N_KV_HEADS
KV_WIDTH = N_KV_HEADS * HEAD_DIM
IN_WIDTH = 2 * CONV_CH + ATTN_WIDTH + 2 * KV_WIDTH
WINDOW = 128
WINDOW_CHUNKS = WINDOW // CHUNK
CONV_K = 31
FFN_CONV_K = 3
D_FF = 2816
ROT_DIM = HEAD_DIM // 4
ROPE_THETA = 500000.0
LN_EPS = 1e-5
DN_ALPHA = (2.0 * DEPTH) ** 0.25
DN_BETA = (8.0 * DEPTH) ** -0.25
NEG_INF = -1e30

kernel_name = "hybrid_conformer_swa_sink_deepnorm_block"

def layer_norm(x, g, b):
    xf = x.astype(jnp.float32)
    mu = jnp.mean(xf, axis=-1, keepdims=True)
    var = jnp.mean(jnp.square(xf - mu), axis=-1, keepdims=True)
    y = (xf - mu) * lax.rsqrt(var + LN_EPS)
    return (y * g.astype(jnp.float32) + b.astype(jnp.float32)).astype(x.dtype)

def causal_dwconv(x, w, b):
    k = w.shape[0]
    y = lax.conv_general_dilated(
        x, w[:, None, :].astype(x.dtype), window_strides=(1,), padding=[(k - 1, 0)],
        dimension_numbers=("NWC", "WIO", "NWC"), feature_group_count=x.shape[-1])
    return y + b.astype(x.dtype)

def rotary_tables(positions):
    inv_freq = ROPE_THETA ** (-jnp.arange(0, ROT_DIM, 2, dtype=jnp.float32) / ROT_DIM)
    ang = positions.astype(jnp.float32)[..., None] * inv_freq
    return jnp.cos(ang)[:, :, None, :], jnp.sin(ang)[:, :, None, :]

def partial_rotary(t, cos, sin):
    half = ROT_DIM // 2
    cos = cos.astype(t.dtype)
    sin = sin.astype(t.dtype)
    t1 = t[..., :half]
    t2 = t[..., half:ROT_DIM]
    return jnp.concatenate([t1 * cos - t2 * sin, t2 * cos + t1 * sin, t[..., ROT_DIM:]], axis=-1)

def adaln(c, w, b):
    mod = (c @ w + b)[:, None, :]
    shift, scale, gate = jnp.split(mod, 3, axis=-1)
    return shift, scale, gate

def swa_sink_attention(q, k, v, sinks):
    bsz, seq = q.shape[0], q.shape[1]
    n_chunks = seq // CHUNK
    q = q.reshape(bsz, n_chunks, CHUNK, N_KV_HEADS, GQA_GROUP, HEAD_DIM)
    k = k.reshape(bsz, n_chunks, CHUNK, N_KV_HEADS, HEAD_DIM)
    v = v.reshape(bsz, n_chunks, CHUNK, N_KV_HEADS, HEAD_DIM)
    pad = ((0, 0), (1, 0), (0, 0), (0, 0), (0, 0))
    k_band = jnp.concatenate([jnp.pad(k, pad)[:, :-1], k], axis=2)
    v_band = jnp.concatenate([jnp.pad(v, pad)[:, :-1], v], axis=2)
    scores = jnp.einsum("bnqhgd,bnkhd->bnhgqk", q, k_band).astype(jnp.float32)
    scores = scores * (HEAD_DIM ** -0.5)
    chunk_idx = jnp.arange(n_chunks)[:, None]
    key_idx = jnp.arange(WINDOW_CHUNKS * CHUNK)[None, :]
    valid = (chunk_idx > 0) | (key_idx >= CHUNK)
    scores = jnp.where(valid[None, :, None, None, None, :], scores, NEG_INF)
    sink = sinks.astype(jnp.float32).reshape(N_KV_HEADS, GQA_GROUP)[None, None, :, :, None, None]
    sink = jnp.broadcast_to(sink, scores.shape[:-1] + (1,))
    probs = jax.nn.softmax(jnp.concatenate([scores, sink], axis=-1), axis=-1)[..., :-1]
    out = jnp.einsum("bnhgqk,bnkhd->bnqhgd", probs.astype(v.dtype), v_band)
    return out.reshape(bsz, seq, ATTN_WIDTH)

def hybrid_mixer(u, w_in, conv_w, conv_b, conv_ln_g, conv_ln_b, sinks, w_out, cos, sin):
    bsz, seq = u.shape[0], u.shape[1]
    proj = u @ w_in
    a, g, q, k, v = jnp.split(
        proj, [CONV_CH, 2 * CONV_CH, 2 * CONV_CH + ATTN_WIDTH, 2 * CONV_CH + ATTN_WIDTH + KV_WIDTH], axis=-1)
    h = a * jax.nn.sigmoid(g)
    h = causal_dwconv(h, conv_w, conv_b)
    h = jax.nn.silu(layer_norm(h, conv_ln_g, conv_ln_b))
    q = partial_rotary(q.reshape(bsz, seq, N_Q_HEADS, HEAD_DIM), cos, sin)
    k = partial_rotary(k.reshape(bsz, seq, N_KV_HEADS, HEAD_DIM), cos, sin)
    v = v.reshape(bsz, seq, N_KV_HEADS, HEAD_DIM)
    o = swa_sink_attention(q, k, v, sinks)
    return jnp.concatenate([h, o], axis=-1) @ w_out

def conv_gated_mlp(u, w_up, ffn_conv_w, ffn_conv_b, w_down):
    val, gate = jnp.split(u @ w_up, 2, axis=-1)
    gate = causal_dwconv(gate, ffn_conv_w, ffn_conv_b)
    return (val * jax.nn.silu(gate)) @ w_down

def setup_inputs(seed: int = 0) -> dict:
    key = jax.random.key(seed)
    ks = jax.random.split(key, 24)
    f32 = jnp.float32
    nrm = lambda k, shape, s: jax.random.normal(k, shape, f32) * s
    L, D = DEPTH, D_MODEL
    positions = (jax.random.randint(ks[2], (BATCH, 1), 0, 4096, dtype=jnp.int32)
                 + jnp.arange(SEQ, dtype=jnp.int32)[None, :])
    return {
        "x": nrm(ks[0], (BATCH, SEQ, D), 1.0),
        "c": nrm(ks[1], (BATCH, D), 1.0),
        "positions": positions,
        "w_ada_mix": nrm(ks[3], (L, D, 3 * D), 0.1 * D ** -0.5),
        "b_ada_mix": nrm(ks[4], (L, 3 * D), 0.01),
        "w_in": nrm(ks[5], (L, D, IN_WIDTH), D ** -0.5),
        "conv_w": nrm(ks[6], (L, CONV_K, CONV_CH), CONV_K ** -0.5),
        "conv_b": nrm(ks[7], (L, CONV_CH), 0.01),
        "conv_ln_g": 1.0 + nrm(ks[8], (L, CONV_CH), 0.02),
        "conv_ln_b": nrm(ks[9], (L, CONV_CH), 0.01),
        "sinks": nrm(ks[10], (L, N_Q_HEADS), 0.5),
        "w_out": nrm(ks[11], (L, MIX_WIDTH, D), DN_BETA * MIX_WIDTH ** -0.5),
        "ln1_g": 1.0 + nrm(ks[12], (L, D), 0.02),
        "ln1_b": nrm(ks[13], (L, D), 0.01),
        "w_ada_ffn": nrm(ks[14], (L, D, 3 * D), 0.1 * D ** -0.5),
        "b_ada_ffn": nrm(ks[15], (L, 3 * D), 0.01),
        "w_up": nrm(ks[16], (L, D, 2 * D_FF), D ** -0.5),
        "ffn_conv_w": nrm(ks[17], (L, FFN_CONV_K, D_FF), FFN_CONV_K ** -0.5),
        "ffn_conv_b": nrm(ks[18], (L, D_FF), 0.01),
        "w_down": nrm(ks[19], (L, D_FF, D), DN_BETA * D_FF ** -0.5),
        "ln2_g": 1.0 + nrm(ks[20], (L, D), 0.02),
        "ln2_b": nrm(ks[21], (L, D), 0.01),
    }

def reference(x, c, positions, w_ada_mix, b_ada_mix, w_in, conv_w, conv_b, conv_ln_g, conv_ln_b,
              sinks, w_out, ln1_g, ln1_b, w_ada_ffn, b_ada_ffn, w_up, ffn_conv_w, ffn_conv_b,
              w_down, ln2_g, ln2_b):
    cos, sin = rotary_tables(positions)
    for l in range(DEPTH):
        shift, scale, gate = adaln(c, w_ada_mix[l], b_ada_mix[l])
        u = x * (1.0 + scale) + shift
        y = hybrid_mixer(u, w_in[l], conv_w[l], conv_b[l], conv_ln_g[l], conv_ln_b[l],
                         sinks[l], w_out[l], cos, sin)
        x = layer_norm(DN_ALPHA * x + (1.0 + gate) * y, ln1_g[l], ln1_b[l])
        shift, scale, gate = adaln(c, w_ada_ffn[l], b_ada_ffn[l])
        u = x * (1.0 + scale) + shift
        y = conv_gated_mlp(u, w_up[l], ffn_conv_w[l], ffn_conv_b[l], w_down[l])
        x = layer_norm(DN_ALPHA * x + (1.0 + gate) * y, ln2_g[l], ln2_b[l])
    return x


_drawn_inputs = setup_inputs


def setup_inputs(seed=0):
    import zlib

    import numpy as np

    out = dict(_drawn_inputs(seed))
    spreads = {}
    factors = {'b_ada_mix': 8.0,
     'conv_b': 8.0,
     'conv_ln_g': 8.0,
     'conv_ln_b': 38.312,
     'sinks': 8.0,
     'ln1_b': 3.714,
     'b_ada_ffn': 8.0,
     'ffn_conv_b': 8.0,
     'ln2_b': 3.797}
    for name, (base, spread) in spreads.items():
        noise = np.random.default_rng([zlib.crc32(name.encode()), seed]).standard_normal(out[name].shape)
        drawn = base * np.exp(spread * noise) if base else spread * noise
        out[name] = __import__('jax').numpy.asarray(drawn.astype(out[name].dtype))
    for name, factor in factors.items():
        out[name] = (out[name] * factor).astype(out[name].dtype)
    return out
```

```python
from contextlib import ExitStack

import numpy as np

import concourse.bass as bass
from concourse import mybir

ALU = mybir.AluOpType
ACT = mybir.ActivationFunctionType
AX = mybir.AxisListType
F32 = mybir.dt.float32
F32R = mybir.dt.float32r
I32 = mybir.dt.int32

P = 128
DEPTH = 2
D = 1024
SEQ = 1024
DT = D // P
NBLK = 2
T = SEQ // NBLK
CONV_CH = 512
CT = CONV_CH // P
CONV_K = 31
HIST = CONV_K - 1
HEAD = 64
HQ = 8
QT = 4
CHUNK = 64
NCH = T // CHUNK
Q0 = 2 * CONV_CH
K0 = Q0 + HQ * HEAD
V0 = K0 + 2 * HEAD
F = 2816
FT = F // P
GROUPS = 2
GT = FT // GROUPS
FK = 3
ROT = HEAD // 4
HALF = ROT // 2
THETA = 500000.0
EPS = 1e-5
ALPHA2 = (2.0 * DEPTH) ** 0.5
INV_ALPHA = (2.0 * DEPTH) ** -0.25
SCALE = HEAD ** -0.5
NEG = -1e30

CONV_PAIRS, QKV_PAIRS, OUT_PAIRS, DOWN_PAIRS = CT, 3, DT // 2, DT // 2
MIX_PAIRS = CONV_PAIRS + QKV_PAIRS + OUT_PAIRS
MLP_PAIRS = GROUPS * (GT + DOWN_PAIRS)
STAGES = [(l, m, b) for l in range(DEPTH) for m in (0, 1) for b in range(NBLK)]
FIRST = []
_n = 0
for _l, _m, _b in STAGES:
    FIRST.append(_n)
    _n += MLP_PAIRS if _m else MIX_PAIRS
N_PAIRS = _n
LAST = len(STAGES) - 1

ROWS1 = [("ln1_g", DT), ("ln1_b", DT), ("ln2_g", DT), ("ln2_b", DT), ("conv_b", CT), ("conv_ln_g", CT),
         ("conv_ln_b", CT), ("ffn_conv_b", FT), ("b_ada_mix", 3 * DT), ("b_ada_ffn", 3 * DT)]
N1 = sum(n for _, n in ROWS1)
N2 = CONV_K * CT
N3 = FK * FT
OFF = {}
_n = 0
for _name, _c in ROWS1:
    OFF[_name] = _n
    _n += _c


def chunked(t):
    return t.rearrange("p (n c) -> p n c", c=CHUNK)


class Step:

    def __init__(self, first, i, u):
        self.P = i * 2 + (first + u)
        self.half = i + (first + u) // 2
        self.par = (first + u) % 2
        self.m = i * 2 + u


def pairs(eng, first, n, straight=False):
    trips = 0 if straight or n < 4 else n // 2
    if trips:
        with eng.Fori(0, trips) as i:
            for u in (0, 1):
                yield Step(first, i, u)
    for m in range(2 * trips, n):
        yield Step(first, 0, m)


def number(names):
    at = {}
    for n, name in enumerate(names):
        assert name not in at
        at[name] = n + 1
    return at


NORMS = []
for _s, (_l, _m, _b) in enumerate(STAGES):
    if _s:
        NORMS.append((("x", _s - 1), DT))
    if not _m:
        NORMS.append((("c", _s), CT))
NORMS.append((("x", LAST), DT))
SMALL = 12


def norm_events():
    stat, dve, act, pool = [], [], [], []
    for b in range(NBLK):
        for k in range(DT):
            act += [("init", b, "u", k), ("init", b, "hi", k)]
            dve += [("init", b, "lo", k)]
    for s, (l, m, b) in enumerate(STAGES):
        here = []
        if s:
            here.append((("x", s - 1), DT))
        if not m:
            here.append((("c", s), CT))
        for name, n in here:
            add_norm(name, n, stat, dve, act, pool)
        pool += [("sum", s, k) for k in range(-1, DT)]
    add_norm(("x", LAST), DT, stat, dve, act, pool)
    return number(stat), number(dve), number(act), number(pool)


def add_norm(name, n, stat, dve, act, pool):
    stat += [(name, e) for e in ("mean", "var", "rstd")]
    if name[0] == "c":
        pool += [(name, "pre", k) for k in range(1, n)]
    dve += [(name, "center", k) for k in range(n)]
    act += [(name, "sq", k) for k in range(n)]
    pool += [(name, "sq", k) for k in range(1, n)]
    dve += [(name, "small", k) for k in range(SMALL)] + [(name, "diag", k) for k in range(T // P)]
    dve += [(name, "scale", k) for k in range(n)]
    if name[0] == "c":
        for k in range(n + 1):
            if k < n:
                act += [(name, "z", k), (name, "th", k)]
                dve += [(name, "m", k)]
            if k:
                act += [(name, "hi", k - 1)]
                dve += [(name, "lo", k - 1)]
    elif name[1] < LAST - 1:
        for k in range(n):
            act += [(name, "u", k), (name, "hi", k), (name, "x", k)]
            dve += [(name, "lo", k)]
    else:
        act += [(name, "x", k) for k in range(n)]


AT_STAT, AT_DVE, AT_ACT, AT_POOL = norm_events()
MIXERS = [s for s, (_, m, _) in enumerate(STAGES) if not m]


def attention_events():
    dve, act = [], []
    for s in MIXERS:
        for j in range(QT + 1):
            dve += [(s, "sin", j), (s, "cos", j), (s, "rope", j)] + ([(s, "rope2", j)] if j == QT else [])
        for n in range(NCH + 2):
            if n < NCH:
                dve += [(s, "mask", n)] if n == 0 and STAGES[s][2] == 0 else []
                dve += [(s, "max", n), (s, "negmax", n), (s, "sink", n)]
            if 1 <= n <= NCH:
                dve += [(s, e, n - 1) for e in ("den", "inv", "probs")]
            if n >= 2:
                dve += [(s, "lo", n - 2)]
        act += [(s, "v", 0), (s, "v", 1)]
        for n in range(NCH + 1):
            if n < NCH:
                act += [(s, "exp", n, i) for i in range(QT)] + [(s, "esink", n)]
            if n:
                act += [(s, "probsT", n - 1), (s, "hi", n - 1)]
    return number(dve), number(act)


AT_ADVE, AT_AACT = attention_events()
TAPS = CONV_K + 1
GATE = 6


def build(nc, a):
    ctx = ExitStack()
    with ctx:
        def sb(name, shape, dt=F32, stack=ctx):
            return stack.enter_context(nc.sbuf_tensor(name, shape, dt))

        def sem(name):
            return ctx.enter_context(nc.semaphore(name))

        x = sb("x", [P, DT, SEQ])
        u_hi = [sb(f"u_hi{b}", [P, DT, T], F32R) for b in range(NBLK)]
        u_lo = [sb(f"u_lo{b}", [P, DT, T], F32R) for b in range(NBLK)]
        raw = [[sb(f"raw{r}{s}", [P, GT, P]) for s in (0, 1)] for r in (0, 1)]
        w_hi = [sb(f"w_hi{s}", [P, GT, P], F32R) for s in (0, 1)]
        w_lo = [sb(f"w_lo{s}", [P, GT, P], F32R) for s in (0, 1)]
        tmp = sb("tmp", [P, 2, T])
        ssum = sb("ssum", [P, T])
        diag = sb("diag", [P, T // P, P])
        small = sb("small", [P, 3, T // P])
        const = sb("const", [P, 5 * P + 1])
        ident, rot, ones_d, ones_c, ones_1 = (const[:, i * P:(i + 1) * P] for i in range(5))
        inv_freq = const[:, 5 * P:5 * P + 1]
        par1 = sb("par1", [P, DEPTH, N1])
        par2 = sb("par2", [P, DEPTH, N2])
        par3 = sb("par3", [P, DEPTH, N3])
        ccol = sb("ccol", [P, DT])
        mod = sb("mod", [P, DEPTH, 2, 3 * DT])
        gain = sb("gain", [P, len(STAGES) // NBLK, DT])
        bias = sb("bias", [P, len(STAGES) // NBLK, DT])
        nsink = sb("nsink", [P, DEPTH, QT])
        ghist = sb("ghist", [P, FT, FK - 1])
        st = sb("st", [P, 2, 6, QT])

        with ExitStack() as region:
            rows1 = [sb(f"rows1{l}", [P, P], stack=region) for l in range(DEPTH)]
            rows2 = [sb(f"rows2{l}", [P, P], stack=region) for l in range(DEPTH)]
            rows3 = [sb(f"rows3{l}", [P, P], stack=region) for l in range(DEPTH)]
            rowsc = sb("rowsc", [DT, P], stack=region)
            pos = sb("pos", [P, SEQ], I32, stack=region)
            ang = sb("ang", [P, SEQ], stack=region)
            turns = sb("turns", [P, SEQ], stack=region)
            tabs = [sb(f"tab{i}", [P, SEQ], stack=region) for i in (0, 1)]
            stage_in = [sb(f"stage_in{i}", [P, D], stack=region) for i in (0, 1)]
            ada = [sb(f"ada{i}", [P, DT // 2, T], stack=region) for i in (0, 1)]
            ada_acc = [sb(f"ada_acc{i}", [P, T], stack=region) for i in (0, 1)]
        with ExitStack() as region:
            glu = sb("glu", [P, CT, HIST + T], stack=region)
            conv = sb("conv", [P, CT, T], stack=region)
            conv_odd = sb("conv_odd", [P, T], stack=region)
            tanh_g = sb("tanh_g", [P, T], stack=region)
            q = sb("q", [P, NCH, QT, CHUNK], stack=region)
            k_raw = sb("k_raw", [P, T], stack=region)
            kz = sb("kz", [P, 2, CHUNK + T], stack=region)
            v_t = sb("v_t", [P, CHUNK + T], stack=region)
            v = sb("v", [P, NCH, P], stack=region)
            probs = sb("probs", [P, 2, QT, P], stack=region)
            probs_t = sb("probs_t", [P, 2, QT * P], stack=region)
            cs = sb("cs", [P, 2, T], stack=region)
        with ExitStack() as region:
            h_hi = sb("h_hi", [P, GT, T], F32R, stack=region)
            h_lo = sb("h_lo", [P, GT, T], F32R, stack=region)
            gate = sb("gate", [P, FK - 1 + T], stack=region)
            gacc = sb("gacc", [P, T], stack=region)
            tanh_c = sb("tanh_c", [P, T], stack=region)
        with ExitStack() as region:
            stage_out = [sb(f"stage_out{i}", [P, D], stack=region) for i in (0, 1)]
        tab_dram = nc.dram_tensor("rope_tables", [2, P, SEQ], F32, kind="Internal").ap()

        bank = [[ctx.enter_context(nc.psum_tensor(f"bank{r}{s}", [P, T], F32)) for s in (0, 1)] for r in (0, 1)]
        sbank = [ctx.enter_context(nc.psum_tensor(f"sbank{i}", [P, QT, P], F32)) for i in (0, 1)]
        b6 = ctx.enter_context(nc.psum_tensor("b6", [P, T], F32))
        b7 = ctx.enter_context(nc.psum_tensor("b7", [P, T], F32))

        raw_in = [[sem(f"raw_in{r}{s}") for s in (0, 1)] for r in (0, 1)]
        hi_ready = [sem(f"hi_ready{s}") for s in (0, 1)]
        lo_ready = [sem(f"lo_ready{s}") for s in (0, 1)]
        slab_done = [sem(f"slab_done{s}") for s in (0, 1)]
        bank_free = [[sem(f"bank_free{r}{s}") for s in (0, 1)] for r in (0, 1)]
        stat_done = sem("stat_done")
        norm_dve = sem("norm_dve")
        norm_act = sem("norm_act")
        norm_pool = sem("norm_pool")
        conv_step = sem("conv_step")
        gate_step = sem("gate_step")
        ghist_clear = sem("ghist_clear")
        gate_act = sem("gate_act")
        hist_ready = sem("hist_ready")
        cs_in = sem("cs_in")
        rot_done = sem("rot_done")
        v_done = sem("v_done")
        scores_done = sem("scores_done")
        probs_t_done = sem("probs_t_done")
        pv_done = sem("pv_done")
        att_dve = sem("att_dve")
        att_act = sem("att_act")
        in_const = sem("in_const")
        in_pos = sem("in_pos")
        in_x = [sem("in_x0"), sem("in_x1")]
        in_ada = [sem("in_ada0"), sem("in_ada1")]
        tab_out = sem("tab_out")
        set_pe = sem("set_pe")
        set_dve = sem("set_dve")
        set_act = sem("set_act")
        x_t_done = sem("x_t_done")
        x_evac = [sem("x_evac0"), sem("x_evac1")]
        ada_add = sem("ada_add")
        ada_sum = sem("ada_sum")
        y_t_done = sem("y_t_done")
        y_evac = [sem("y_evac0"), sem("y_evac1")]
        y_out = [sem("y_out0"), sem("y_out1")]

        def qkv_copied(s, j):
            pair = FIRST[s] + CONV_PAIRS + j // 2
            return bank_free[pair % 2][j % 2], pair // 2 + 2

        TT = SEQ // P
        ADAS = [(l, m) for m in (0, 1) for l in range(DEPTH)]
        NCHUNK = 3 * D // T
        w_ada = {0: a["w_ada_mix"], 1: a["w_ada_ffn"]}

        block = ctx.enter_context(nc.Block())

        @block.sync
        def _(sp):
            sp.dma_start(const[:], a["consts"]).then_inc(in_const, 16)
            sp.dma_start(rowsc[:], a["c"].rearrange("o (t p) -> (o t) p", p=P)).then_inc(in_const, 16)
            for l in range(DEPTH):
                for name, n in ROWS1:
                    o = OFF[name]
                    sp.dma_start(rows1[l][o:o + n, :], a[name][l].rearrange("(t p) -> t p", p=P)).then_inc(in_const, 16)
                sp.dma_start(rows2[l][0:N2, :], a["conv_w"][l].rearrange("k (t p) -> (k t) p", p=P)).then_inc(in_const, 16)
                sp.dma_start(rows3[l][0:N3, :], a["ffn_conv_w"][l].rearrange("k (t p) -> (k t) p", p=P)).then_inc(in_const, 16)
                for s in (0, 1):
                    src = a["sinks"][l].rearrange("(o j s) -> s o j", o=1, s=2)[s]
                    with nc.allow_non_contiguous_dma(reason="eight numbers"):
                        sp.dma_start(nsink[s * CHUNK:(s + 1) * CHUNK, l, :], src.to_broadcast([CHUNK, QT])).then_inc(in_const, 16)
            sp.dma_start(pos[:], a["positions"].to_broadcast([P, SEQ])).then_inc(in_pos, 16)

            def load_ada(n):
                l, m = ADAS[n // NCHUNK]
                c = n % NCHUNK
                for half in (0, 1):
                    if n:
                        sp.wait_ge(ada_add, DT * (n - 1) + DT // 2 * (half + 1))
                    src = w_ada[m][l, half * D // 2:(half + 1) * D // 2, c * T:(c + 1) * T]
                    sp.dma_start(ada[half][:], src.rearrange("(k p) n -> p k n", p=P)).then_inc(in_ada[half], 16)

            def load_x(t):
                if t >= 2:
                    sp.wait_ge(x_t_done, 2 * (t - 1))
                sp.dma_start(stage_in[t % 2][:], a["x"][0, t * P:(t + 1) * P, :]).then_inc(in_x[t % 2], 16)

            def load(step, parts):
                if not isinstance(step.P, int) or step.P >= 2:
                    for s in (0, 1):
                        sp.wait_ge(lo_ready[s], step.P - 1)
                for s in (0, 1):
                    pieces = parts(s)
                    for n, (dst, src) in enumerate(pieces):
                        inc = 48 if len(pieces) == 1 else 16 if len(pieces) == 3 or n == 0 else 32
                        sp.dma_start(dst, src).then_inc(raw_in[step.par][s], inc)

            def columns(w, r0, nk, c0):
                return w[r0:r0 + nk * P, bass.ds(c0, P)].rearrange("(k p) m -> p k m", p=P)

            def mixer(s, l, b):
                first = FIRST[s]
                w = a["w_in"][l]
                for st_ in pairs(sp, first, CONV_PAIRS, straight=s == 0):
                    load(st_, lambda side: [(raw[st_.par][side][:, 0:DT, :],
                                             columns(w, 0, DT, st_.m * P + (CONV_CH if side == 0 else 0)))])
                for i in (0, 1):
                    sp.dma_start(cs[:, i, :], tab_dram[i, :, b * T:(b + 1) * T]).then_inc(cs_in, 16)
                for st_ in pairs(sp, first + CONV_PAIRS, QKV_PAIRS):
                    def parts(side):
                        j = 2 * st_.m + side
                        if j >= QT:
                            return [(raw[st_.par][side][:, 0:DT, :], columns(w, 0, DT, K0 + (j - QT) * P))]
                        return [(raw[st_.par][side][:, 0:DT, g * HEAD:(g + 1) * HEAD],
                                 w[:, Q0 + (g * QT + j) * HEAD:Q0 + (g * QT + j + 1) * HEAD].rearrange("(k p) m -> p k m", p=P))
                                for g in (0, 1)]
                    load(st_, parts)
                w = a["w_out"][l]
                for st_ in pairs(sp, first + CONV_PAIRS + QKV_PAIRS, OUT_PAIRS):
                    def parts(side):
                        c0 = (st_.m * 2 + side) * P
                        dst = raw[st_.par][side]
                        return [(dst[:, 0:CT, :], columns(w, 0, CT, c0))] + [
                            (dst[g * HEAD:(g + 1) * HEAD, CT:DT, :],
                             w[CONV_CH + g * QT * HEAD:CONV_CH + (g + 1) * QT * HEAD, bass.ds(c0, P)].rearrange("(j d) m -> d j m", d=HEAD))
                            for g in (0, 1)]
                    load(st_, parts)

            def mlp(s, l, b):
                first = FIRST[s]
                for g in range(GROUPS):
                    w = a["w_up"][l]
                    for st_ in pairs(sp, first, GT):
                        load(st_, lambda side: [(raw[st_.par][side][:, 0:DT, :],
                                                 columns(w, 0, DT, (st_.m + g * GT) * P + (F if side == 0 else 0)))])
                    first += GT
                    w = a["w_down"][l]
                    for st_ in pairs(sp, first, DOWN_PAIRS):
                        load(st_, lambda side: [(raw[st_.par][side][:], columns(w, g * GT * P, GT, (st_.m * 2 + side) * P))])
                    first += DOWN_PAIRS

            for t in range(TT):
                load_x(t)
                load_ada(t)
            for n in range(TT, len(ADAS) * NCHUNK):
                load_ada(n)
            sp.wait_ge(set_act, SET_ACT["table", 1])
            for i in (0, 1):
                sp.dma_start(tab_dram[i], tabs[i][:]).then_inc(tab_out, 16)
            sp.wait_ge(tab_out, 32)
            for s, (l, m, b) in enumerate(STAGES):
                (mlp if m else mixer)(s, l, b)
            for t in range(TT):
                sp.wait_ge(y_evac[0], t + 1)
                sp.wait_ge(y_evac[1], t + 1)
                sp.dma_start(a["out"][0, t * P:(t + 1) * P, :], stage_out[t % 2][:]).then_inc(y_out[t % 2], 16)
            for i in (0, 1):
                sp.wait_ge(y_out[i], 16 * TT // 2)

        @block.tensor
        def _(pe):
            pe.wait_ge(in_const, 16 * IN_CONST)
            srcs = [(rows1[l], N1) for l in range(DEPTH)] + [(rows2[l], N2) for l in range(DEPTH)]
            for i, (r, n) in enumerate(srcs):
                ins = pe.transpose(b6[:, i * P:i * P + n], r[0:n, :], ident[0:n, 0:n])
            ins.then_inc(set_pe, 1)
            for i, (r, n) in enumerate([(rows3[0], N3), (rows3[1], N3), (rowsc, DT)]):
                ins = pe.transpose(b7[:, i * P:i * P + n], r[0:n, :], ident[0:n, 0:n])
            ins.then_inc(set_pe, 1)
            def sum_ada(n):
                pe.wait_ge(ada_add, DT * (n + 1))
                for i in range(T // P):
                    col = n * (T // P) + i
                    ins = pe.matmul(b7[:, col:col + 1], ada_acc[n % 2][:, i * P:(i + 1) * P], ones_1[:, 0:1],
                                    start=True, stop=True)
                ins.then_inc(ada_sum, 1)

            pe.wait_ge(set_dve, SET_DVE["par", 1])
            for t in range(TT):
                pe.wait_ge(in_x[t % 2], 16 * (t // 2 + 1))
                for half in (0, 1):
                    if t >= 2:
                        pe.wait_ge(x_evac[half], t - 1)
                    for k in range(4):
                        ins = pe.transpose(bank[t % 2][half][:, k * P:(k + 1) * P],
                                           stage_in[t % 2][:, (half * 4 + k) * P:(half * 4 + k + 1) * P], ident)
                    ins.then_inc(x_t_done, 1)
                if t:
                    sum_ada(t - 1)
            for n in range(TT - 1, len(ADAS) * NCHUNK):
                sum_ada(n)

            def slab(step, side, nk, rhs, ready=None):
                pe.wait_ge(lo_ready[side], step.P + 1)
                pe.wait_ge(bank_free[step.par][side], step.half + 1)
                out = bank[step.par][side]
                for k in range(nk):
                    if ready:
                        ready(k)
                    hi, lo = rhs(k)
                    pe.matmul(out[:], w_hi[side][:, k, :], hi, start=k == 0, stop=False)
                    pe.matmul(out[:], w_hi[side][:, k, :], lo, start=False, stop=False)
                    ins = pe.matmul(out[:], w_lo[side][:, k, :], hi, start=False, stop=k == nk - 1)
                ins.then_inc(slab_done[side], 1)

            free7 = [set_dve, SET_DVE["mod", 1]]

            def take7(s, v):
                pe.wait_ge(*free7)
                free7[:] = s, v

            def stat(name, what):
                n = DT if name[0] == "x" else CT
                if what == "mean":
                    if name[0] == "x":
                        pe.wait_ge(norm_pool, AT_POOL["sum", name[1], DT - 1])
                    else:
                        pe.wait_ge(norm_pool, AT_POOL[name, "pre", n - 1])
                    take7(norm_dve, AT_DVE[name, "center", n - 1])
                    ins = pe.matmul(b7[:], ones_d if n == DT else ones_c, ssum[:], start=True, stop=True)
                elif what == "var":
                    pe.wait_ge(norm_pool, AT_POOL[name, "sq", n - 1])
                    take7(norm_dve, AT_DVE[name, "small", 0])
                    for i in range(T // P):
                        ins = pe.matmul(b7[:, i:i + 1], ssum[:, i * P:(i + 1) * P], (ones_d if n == DT else ones_c)[:, 0:1],
                                        start=True, stop=True)
                else:
                    pe.wait_ge(norm_dve, AT_DVE[name, "diag", T // P - 1])
                    take7(norm_dve, AT_DVE[name, "scale", n - 1])
                    ins = pe.matmul(b7[:], ones_1, diag[:].rearrange("p a b -> p (a b)"), start=True, stop=True)
                ins.then_inc(stat_done, 1)

            def mixer(s, l, b):
                first, mi = FIRST[s], MIXERS.index(s)
                for k in range(DT):
                    pe.wait_ge(norm_dve, need_u(s, k))
                for st_ in pairs(pe, first, CONV_PAIRS):
                    for side in (0, 1):
                        slab(st_, side, DT, lambda k: (u_hi[b][:, k, :], u_lo[b][:, k, :]))
                if s:
                    stat(("x", s - 1), "mean")
                for st_ in pairs(pe, first + CONV_PAIRS, QKV_PAIRS):
                    for side in (0, 1):
                        slab(st_, side, DT, lambda k: (u_hi[b][:, k, :], u_lo[b][:, k, :]))
                for j in range(QT + 1):
                    pe.wait_ge(*qkv_copied(s, j))
                    if j % 2:
                        take7(att_dve, AT_ADVE[s, "sin", j])
                    elif j:
                        pe.wait_ge(att_dve, AT_ADVE[s, "sin", j - 2])
                    elif mi:
                        pe.wait_ge(att_act, AT_AACT[MIXERS[mi - 1], "probsT", NCH - 1])
                    else:
                        pe.wait_ge(set_dve, SET_DVE["par", 0])
                    pe.matmul((b7 if j % 2 else b6)[:], rot, q[:, :, j, :] if j < QT else k_raw[:],
                              start=True, stop=True).then_inc(rot_done, 1)
                pe.wait_ge(*qkv_copied(s, QT + 1))
                pe.wait_ge(hist_ready, 2 * (mi + 1))
                for i in (0, 1):
                    for n in range(NCH // 2):
                        c = (i * NCH // 2 + n) * CHUNK
                        ins = pe.transpose(bank[0][i][:, n * P:(n + 1) * P], v_t[:, c:c + P], ident)
                    ins.then_inc(v_done, 1)
                if s:
                    stat(("x", s - 1), "var")

                def scores(n):
                    if n == 0:
                        pe.wait_ge(att_dve, AT_ADVE[s, "rope2", QT])
                    if n >= 2:
                        pe.wait_ge(att_act, AT_AACT[s, "exp", n - 2, QT - 1])
                    elif mi:
                        pe.wait_ge(att_act, AT_AACT[MIXERS[mi - 1], "exp", NCH - 2 + n, QT - 1])
                    for g in (0, 1):
                        for pr in (0, 1):
                            qq = q[:, n, 2 * pr:2 * pr + 2, :].rearrange("p j t -> p (j t)")
                            ins = pe.matmul(sbank[n % 2][:, 2 * g + pr, :], qq, kz[:, g, n * CHUNK:n * CHUNK + P],
                                            start=True, stop=True)
                    ins.then_inc(scores_done, 1)

                scores(0)
                scores(1)
                for n in range(NCH):
                    pe.wait_ge(att_dve, AT_ADVE[s, "probs", n])
                    if n == 0:
                        pe.wait_ge(att_dve, AT_ADVE[s, "sin", QT])
                    else:
                        pe.wait_ge(att_act, AT_AACT[s, "probsT", n - 1])
                    for i in range(QT):
                        ins = pe.transpose(b6[:, i * P:(i + 1) * P], probs[:, n % 2, i, :], ident)
                    ins.then_inc(probs_t_done, 1)
                    if n + 2 < NCH:
                        scores(n + 2)
                    pe.wait_ge(att_act, AT_AACT[s, "probsT", n])
                    if n == 0:
                        pe.wait_ge(att_act, AT_AACT[s, "v", 1])
                    take7(att_dve, AT_ADVE[s, "lo", n])
                    for g in (0, 1):
                        ins = pe.matmul(b7[g * HEAD:(g + 1) * HEAD, 0:2 * P], v[:, n, g * HEAD:(g + 1) * HEAD],
                                        probs_t[:, n % 2, g * 2 * P:(g + 1) * 2 * P], start=True, stop=True)
                    ins.then_inc(pv_done, 1)
                if s:
                    stat(("x", s - 1), "rstd")
                for what in ("mean", "var", "rstd"):
                    stat(("c", s), what)
                pe.wait_ge(norm_dve, AT_DVE[("c", s), "lo", CT - 1])
                for st_ in pairs(pe, first + CONV_PAIRS + QKV_PAIRS, OUT_PAIRS):
                    for side in (0, 1):
                        slab(st_, side, DT, lambda k: (u_hi[b][:, k, :], u_lo[b][:, k, :]))

            def mlp(s, l, b):
                first = FIRST[s]
                for k in range(DT):
                    pe.wait_ge(norm_dve, need_u(s, k))
                for g in range(GROUPS):
                    for st_ in pairs(pe, first, GT):
                        for side in (0, 1):
                            slab(st_, side, DT, lambda k: (u_hi[b][:, k, :], u_lo[b][:, k, :]))
                    first += GT
                    stat(("x", s - 1), ("mean", "rstd")[g])
                    done = hidden(s, g * GT)
                    for k in range(GT - 1):
                        pe.wait_ge(gate_step, done + GATE * (k + 1))
                    pe.wait_ge(gate_step, done + GATE * GT)
                    for st_ in pairs(pe, first, DOWN_PAIRS):
                        for side in (0, 1):
                            slab(st_, side, GT, lambda k: (h_hi[:, k, :], h_lo[:, k, :]))
                    first += DOWN_PAIRS
                    if g == 0:
                        stat(("x", s - 1), "var")

            for s, (l, m, b) in enumerate(STAGES):
                (mlp if m else mixer)(s, l, b)
            for what in ("mean", "var", "rstd"):
                stat(("x", LAST), what)
            for t in range(TT):
                for half in (0, 1):
                    if t == 0 and half == 0:
                        for k in range(DT):
                            pe.wait_ge(norm_act, AT_ACT[("x", LAST), "x", k])
                    if t >= 2:
                        pe.wait_ge(y_evac[half], t - 1)
                    for k in range(4):
                        ins = pe.transpose(bank[t % 2][half][:, k * P:(k + 1) * P],
                                           x[:, half * 4 + k, t * P:(t + 1) * P], ident)
                    ins.then_inc(y_t_done, 1)

        @block.scalar
        def _(act):
            for t in range(TT):
                act.wait_ge(x_t_done, 2 * t + 1)
                act.activation(x[:, 0:4, t * P:(t + 1) * P], bank[t % 2][0][:].rearrange("p (k n) -> p k n", k=4),
                               ACT.Copy).then_inc(x_evac[0], 1)
            for i in (0, 1):
                act.wait_ge(set_dve, SET_DVE["reduced", i])
                act.activation(tabs[i][:], tabs[i][:], ACT.Sin).then_inc(set_act, 1)
            act.wait_ge(set_dve, SET_DVE["fold", 1])

            def split_hi(step, side, nk):
                nxt = Step(0, step.half, step.par + 1)
                act.wait_ge(raw_in[1 - step.par][side], (nxt.half) * 48 + 48)
                act.wait_ge(slab_done[side], step.P + 1)
                act.activation(w_hi[side][:, 0:nk, :], raw[1 - step.par][side][:, 0:nk, :], ACT.Copy).then_inc(hi_ready[side], 1)

            def inputs(name, k, b, i, xk):
                act.activation(tmp[:, k % 2, :], xk, ACT.Identity, bias=bias[:, i, k:k + 1],
                               scale=gain[:, i, k:k + 1]).then_inc(norm_act, 1)
                act.wait_ge(norm_act, AT_ACT[(name, "u", k) if name[0] == "x" else (*name, "u", k)])
                act.activation(u_hi[b][:, k, :], tmp[:, k % 2, :], ACT.Copy).then_inc(norm_act, 1)

            for side in (0, 1):
                act.wait_ge(raw_in[0][side], 48)
                act.activation(w_hi[side][:, 0:DT, :], raw[0][side][:, 0:DT, :], ACT.Copy).then_inc(hi_ready[side], 1)
            for b in range(NBLK):
                for k in range(DT):
                    n = b * DT + k
                    if n >= 2:
                        act.wait_ge(norm_dve, AT_DVE["init", (n - 2) // DT, "lo", (n - 2) % DT])
                    if n == 0:
                        act.wait_ge(x_evac[0], TT)
                        act.wait_ge(x_evac[1], TT)
                    inputs(("init", b), k, b, 0, x[:, k, b * T:(b + 1) * T])

            def squares(name, xk):
                n = DT if name[0] == "x" else CT
                for k in range(n):
                    act.wait_ge(norm_dve, AT_DVE[name, "center", k])
                    if k >= 2:
                        act.wait_ge(norm_pool, AT_POOL[name, "sq", max(k - 2, 1)])
                    act.activation(tmp[:, k % 2, :], xk(k), ACT.Square).then_inc(norm_act, 1)

            def norm_out(s):
                l, m, b = STAGES[s]
                name = ("x", s)
                g0 = OFF["ln2_g" if m else "ln1_g"]
                b0 = OFF["ln2_b" if m else "ln1_b"]
                for k in range(DT):
                    xk = x[:, k, b * T:(b + 1) * T]
                    act.wait_ge(norm_dve, AT_DVE[name, "scale", k])
                    if s < LAST - 1:
                        if k >= 2:
                            act.wait_ge(norm_dve, AT_DVE[name, "lo", k - 2])
                        inputs(name, k, b, s // NBLK + 1, xk)
                    act.activation(xk, xk, ACT.Identity, bias=par1[:, l, b0 + k:b0 + k + 1],
                                   scale=par1[:, l, g0 + k:g0 + k + 1]).then_inc(norm_act, 1)

            def conv_norm_out(s):
                l, m, b = STAGES[s]
                name = ("c", s)
                g0, b0 = OFF["conv_ln_g"], OFF["conv_ln_b"]
                for k in range(CT + 1):
                    if k < CT:
                        act.wait_ge(norm_dve, AT_DVE[name, "scale", k])
                        act.activation(conv[:, k, :], conv[:, k, :], ACT.Identity, bias=par1[:, l, b0 + k:b0 + k + 1],
                                       scale=par1[:, l, g0 + k:g0 + k + 1]).then_inc(norm_act, 1)
                        act.wait_ge(norm_act, AT_ACT[name, "z", k])
                        if k >= 2:
                            act.wait_ge(norm_dve, AT_DVE[name, "lo", k - 2])
                        act.activation(tmp[:, k % 2, :], conv[:, k, :], ACT.Tanh, scale=0.5).then_inc(norm_act, 1)
                    if k:
                        act.wait_ge(norm_dve, AT_DVE[name, "m", k - 1])
                        act.activation(u_hi[b][:, k - 1, :], tmp[:, (k - 1) % 2, :], ACT.Copy, scale=0.5).then_inc(norm_act, 1)

            def mixer(s, l, b):
                first, mi = FIRST[s], MIXERS.index(s)
                for st_ in pairs(act, first, CONV_PAIRS):
                    act.wait_ge(slab_done[0], st_.P + 1)
                    act.wait_ge(bank_free[1 - st_.par][1], st_.half + (1 if st_.par == 0 else 2))
                    act.activation(tanh_g[:], bank[st_.par][0][:], ACT.Tanh, scale=0.5).then_inc(bank_free[st_.par][0], 1)
                    split_hi(st_, 0, DT)
                    split_hi(st_, 1, DT)
                for st_ in pairs(act, first + CONV_PAIRS, QKV_PAIRS):
                    for side in (0, 1):
                        j = 2 * st_.m + side
                        act.wait_ge(slab_done[side], st_.P + 1)
                        if j == QT + 1:
                            act.wait_ge(hist_ready, 2 * (mi + 1))
                        dst = q[:, :, j, :] if j < QT else k_raw[:] if j == QT else v_t[:, CHUNK:]
                        act.activation(dst, chunked(bank[st_.par][side][:]) if j < QT else bank[st_.par][side][:], ACT.Copy).then_inc(bank_free[st_.par][side], 1)
                        split_hi(st_, side, DT)
                if s:
                    squares(("x", s - 1), lambda k: x[:, k, (1 - b) * T:(2 - b) * T])
                for i in (0, 1):
                    act.wait_ge(v_done, 2 * mi + i + 1)
                    act.activation(v[:, i * NCH // 2:(i + 1) * NCH // 2, :], bank[0][i][:].rearrange("p (n f) -> p n f", f=P),
                                   ACT.Copy).then_inc(att_act, 1)
                for n in range(NCH + 1):
                    if n < NCH:
                        r = n % 2
                        act.wait_ge(att_dve, AT_ADVE[s, "sink", n])
                        for i in range(QT):
                            act.activation(probs[:, r, i, :], sbank[r][:, i, :], ACT.Exp, bias=st[:, r, 1, i:i + 1],
                                           scale=SCALE, accum_out=st[:, r, 3, i:i + 1]).then_inc(att_act, 1)
                        act.activation(st[:, r, 4, :], st[:, r, 2, :], ACT.Exp).then_inc(att_act, 1)
                    if n:
                        act.wait_ge(probs_t_done, mi * NCH + n)
                        act.activation(probs_t[:, (n - 1) % 2, :], b6[:], ACT.Copy).then_inc(att_act, 1)
                        act.wait_ge(pv_done, mi * NCH + n)
                        act.activation(u_hi[b][:, CT:DT, (n - 1) * CHUNK:n * CHUNK],
                                       b7[:, 0:QT * CHUNK].rearrange("p (j t) -> p j t", j=QT), ACT.Copy).then_inc(att_act, 1)
                if s:
                    norm_out(s - 1)
                squares(("c", s), lambda k: conv[:, k, :])
                conv_norm_out(s)
                for st_ in pairs(act, first + CONV_PAIRS + QKV_PAIRS, OUT_PAIRS):
                    split_hi(st_, 0, DT)
                    split_hi(st_, 1, DT)

            def mlp(s, l, b):
                first = FIRST[s]
                for g in range(GROUPS):
                    for st_ in pairs(act, first, GT):
                        f = st_.m + g * GT
                        n = f + FT * mlp_no(s)
                        nk = GT if isinstance(st_.m, int) and st_.m == GT - 1 else DT
                        act.wait_ge(slab_done[0], st_.P + 1)
                        act.wait_ge(gate_step, n * GATE + 1)
                        ps = bank[st_.par][0]
                        act.activation(gacc[:], ps[:], ACT.Identity, bias=par1[:, l, bass.ds(f + OFF["ffn_conv_b"], 1)],
                                       scale=par3[:, l, bass.ds(f + 2 * FT, 1)]).then_inc(gate_act, 1)
                        act.activation(gate[:, FK - 1:], ps[:], ACT.Copy).then_inc(bank_free[st_.par][0], 1)
                        split_hi(st_, 0, nk)
                        act.wait_ge(gate_step, n * GATE + 5)
                        act.activation(tanh_c[:], gacc[:], ACT.Tanh, scale=0.5).then_inc(gate_act, 1)
                        split_hi(st_, 1, nk)
                        act.wait_ge(bank_free[st_.par][1], st_.half + 2)
                        act.activation(h_hi[:, bass.ds(st_.m, 1), :], gacc[:].rearrange("p (o n) -> p o n", o=1), ACT.Copy).then_inc(gate_act, 1)
                    first += GT
                    if g == 0:
                        squares(("x", s - 1), lambda k: x[:, k, (1 - b) * T:(2 - b) * T])
                    else:
                        norm_out(s - 1)
                    last = s == LAST and g == GROUPS - 1
                    for st_ in pairs(act, first, DOWN_PAIRS, straight=last):
                        for side in (0, 1):
                            if not last or st_.m < DOWN_PAIRS - 1:
                                split_hi(st_, side, GT)
                    first += DOWN_PAIRS

            for s, (l, m, b) in enumerate(STAGES):
                (mlp if m else mixer)(s, l, b)
            squares(("x", LAST), lambda k: x[:, k, T:])
            norm_out(LAST)
            for t in range(TT):
                act.wait_ge(y_t_done, 2 * t + 1)
                if t >= 2:
                    act.wait_ge(y_out[t % 2], 16 * (t // 2))
                act.activation(stage_out[t % 2][:, 0:D // 2], bank[t % 2][0][:], ACT.Copy).then_inc(y_evac[0], 1)

        @block.vector
        def _(dve):
            setup = [0]

            def step(ins):
                ins.then_inc(set_dve, 1)
                setup[0] += 1
                dve.wait_ge(set_dve, setup[0])

            def done(name):
                assert SET_DVE[name] == setup[0], (name, setup[0])

            dve.wait_ge(set_pe, 1)
            step(dve.tensor_copy(par1[:], b6[:, 0:2 * P].rearrange("p (l n) -> p l n", l=DEPTH)[:, :, 0:N1]))
            step(dve.tensor_scalar(par2[:], b6[:, 2 * P:4 * P].rearrange("p (l n) -> p l n", l=DEPTH)[:, :, 0:N2], 0.5, None, ALU.mult))
            done(("par", 0))
            dve.wait_ge(set_pe, 2)
            step(dve.tensor_copy(par3[:], b7[:, 0:2 * P].rearrange("p (l n) -> p l n", l=DEPTH)[:, :, 0:N3]))
            step(dve.tensor_copy(ccol[:], b7[:, 2 * P:2 * P + DT]))
            done(("par", 1))
            step(dve.tensor_scalar(nsink[:], nsink[:], -1.0, None, ALU.mult))

            def evac_x(t):
                dve.wait_ge(x_t_done, 2 * t + 2)
                dve.tensor_copy(x[:, 4:8, t * P:(t + 1) * P],
                                bank[t % 2][1][:].rearrange("p (k n) -> p k n", k=4)).then_inc(x_evac[1], 1)

            def add_ada(n):
                acc = ada_acc[n % 2]
                if n >= 2:
                    dve.wait_ge(ada_sum, n - 1)
                for k in range(DT):
                    half = k // (DT // 2)
                    if k % (DT // 2) == 0:
                        dve.wait_ge(in_ada[half], 16 * (n + 1))
                    w = ada[half][:, k % (DT // 2), :]
                    if k == 0:
                        dve.tensor_scalar(acc[:], w, ccol[:, 0:1], None, ALU.mult).then_inc(ada_add, 1)
                    else:
                        dve.wait_ge(ada_add, n * DT + k)
                        dve.scalar_tensor_tensor(out=acc[:], in0=w, scalar=ccol[:, k:k + 1], in1=acc[:],
                                                 op0=ALU.mult, op1=ALU.add).then_inc(ada_add, 1)

            dve.wait_ge(in_pos, 16)
            step(dve.tensor_copy(ang[:], pos[:]))
            step(dve.tensor_scalar(ang[:], ang[:], inv_freq, None, ALU.mult))
            for i, (quarter, shift) in enumerate(((0.25, np.pi / 2), (0.0, 0.0))):
                step(dve.tensor_scalar(turns[:], ang[:], float(np.float32(0.5 / np.pi)), quarter, ALU.mult, ALU.add))
                step(dve.tensor_scalar(turns[:], turns[:], MAGIC, None, ALU.add))
                step(dve.tensor_scalar(turns[:], turns[:], -MAGIC, None, ALU.add))
                for n, part in enumerate(TWO_PI):
                    step(dve.scalar_tensor_tensor(out=tabs[i][:], in0=turns[:], scalar=-part, in1=(tabs[i] if n else ang)[:],
                                                  op0=ALU.mult, op1=ALU.add))
                step(dve.tensor_scalar(tabs[i][:], tabs[i][:], shift, PI_DOWN, ALU.add, ALU.min))
                step(dve.tensor_scalar(tabs[i][:], tabs[i][:], -PI_DOWN, None, ALU.max))
                done(("reduced", i))
            for t in range(TT):
                evac_x(t)
                add_ada(t)
            for n in range(TT, len(ADAS) * NCHUNK):
                add_ada(n)
            dve.wait_ge(ada_sum, len(ADAS) * NCHUNK)
            for i, m in enumerate((0, 1)):
                name = ("b_ada_mix", "b_ada_ffn")[m]
                o = OFF[name]
                step(dve.tensor_tensor(mod[:, :, m, :], b7[:, i * 6 * DT:(i + 1) * 6 * DT].rearrange("p (l n) -> p l n", l=DEPTH),
                                       par1[:, :, o:o + 3 * DT], ALU.add))
            done(("mod", 1))
            step(dve.tensor_scalar(mod[:, :, :, DT:2 * DT], mod[:, :, :, DT:2 * DT], 1.0, None, ALU.add))
            step(dve.tensor_scalar(mod[:, :, :, 2 * DT:], mod[:, :, :, 2 * DT:], 1.0, INV_ALPHA, ALU.add, ALU.mult))
            step(dve.tensor_copy(gain[:, 0, :], mod[:, 0, 0, DT:2 * DT]))
            step(dve.tensor_copy(bias[:, 0, :], mod[:, 0, 0, 0:DT]))
            for i in range(1, 2 * DEPTH):
                l, m = i // 2, i % 2
                pl, pm = (i - 1) // 2, (i - 1) % 2
                g0 = OFF["ln2_g" if pm else "ln1_g"]
                b0 = OFF["ln2_b" if pm else "ln1_b"]
                sc = mod[:, l, m, DT:2 * DT]
                step(dve.tensor_tensor(gain[:, i, :], par1[:, pl, g0:g0 + DT], sc, ALU.mult))
                step(dve.tensor_tensor(bias[:, i, :], par1[:, pl, b0:b0 + DT], sc, ALU.mult))
                step(dve.tensor_tensor(bias[:, i, :], bias[:, i, :], mod[:, l, m, 0:DT], ALU.add))
            done(("fold", 1))
            for r in (0, 1):
                for side in (0, 1):
                    dve.wait_ge(x_evac[side], TT)
                    dve.memset(small[:, 0, 2 * r + side:2 * r + side + 1], 0.0).then_inc(bank_free[r][side], 1)
            dve.memset(ghist[:], 0.0).then_inc(gate_step, 1)

            def split_lo(step_, side, nk):
                dve.wait_ge(hi_ready[side], step_.P + 2)
                dve.tensor_tensor(w_lo[side][:, 0:nk, :], raw[1 - step_.par][side][:, 0:nk, :],
                                  w_hi[side][:, 0:nk, :].bitcast(F32), ALU.subtract).then_inc(lo_ready[side], 1)

            def input_lo(b, k, hi_at):
                dve.wait_ge(norm_act, hi_at)
                dve.tensor_tensor(u_lo[b][:, k, :], tmp[:, k % 2, :], u_hi[b][:, k, :].bitcast(F32),
                                  ALU.subtract).then_inc(norm_dve, 1)

            for side in (0, 1):
                dve.wait_ge(hi_ready[side], 1)
                dve.tensor_tensor(w_lo[side][:, 0:DT, :], raw[0][side][:, 0:DT, :],
                                  w_hi[side][:, 0:DT, :].bitcast(F32), ALU.subtract).then_inc(lo_ready[side], 1)
            for b in range(NBLK):
                for k in range(DT):
                    input_lo(b, k, AT_ACT["init", b, "hi", k])

            def center(name, xk):
                dve.wait_ge(stat_done, AT_STAT[name, "mean"])
                for k in range(DT if name[0] == "x" else CT):
                    dve.tensor_tensor(xk(k), xk(k), b7[:], ALU.subtract).then_inc(norm_dve, 1)

            def rsqrt(name):
                eps = EPS / ALPHA2 if name[0] == "x" else EPS
                dve.wait_ge(stat_done, AT_STAT[name, "var"])
                var, y, t = small[:, 0, :], small[:, 1, :], small[:, 2, :]
                at = AT_DVE[name, "small", 0] - 1

                def small_step(n, ins):
                    ins.then_inc(norm_dve, 1)
                    dve.wait_ge(norm_dve, at + n + 1)

                small_step(0, dve.tensor_scalar(var, b7[:, 0:T // P], eps, None, ALU.add))
                small_step(1, dve.tensor_scalar(t.bitcast(I32), var.bitcast(I32), 1, None, ALU.logical_shift_right))
                small_step(2, dve.tensor_scalar(y.bitcast(I32), t.bitcast(I32), -1.0, 1597463007.0, ALU.mult, ALU.add))
                for i in range(3):
                    small_step(3 * i + 3, dve.tensor_tensor(t, y, y, ALU.mult))
                    small_step(3 * i + 4, dve.scalar_tensor_tensor(out=t, in0=t, scalar=-0.5, in1=var, op0=ALU.mult, op1=ALU.mult))
                    small_step(3 * i + 5, dve.scalar_tensor_tensor(out=y, in0=t, scalar=1.5, in1=y, op0=ALU.add, op1=ALU.mult))
                for i in range(T // P):
                    dve.tensor_scalar(diag[:, i, :], ident, y[:, i:i + 1], None, ALU.mult).then_inc(norm_dve, 1)

            def rescale(name, xk):
                dve.wait_ge(stat_done, AT_STAT[name, "rstd"])
                for k in range(DT if name[0] == "x" else CT):
                    dve.tensor_tensor(xk(k), xk(k), b7[:], ALU.mult).then_inc(norm_dve, 1)

            def inputs_lo(s):
                if s < LAST - 1:
                    for k in range(DT):
                        input_lo(STAGES[s][2], k, AT_ACT[("x", s), "hi", k])

            def residual(l, m, b, st_):
                for side in (0, 1):
                    k = st_.m * 2 + side
                    dve.wait_ge(slab_done[side], st_.P + 1)
                    xk = x[:, bass.ds(k, 1), b * T:(b + 1) * T]
                    dve.scalar_tensor_tensor(out=xk, in0=bank[st_.par][side][:].rearrange("p (o n) -> p o n", o=1),
                                             scalar=mod[:, l, m, bass.ds(k + 2 * DT, 1)],
                                             in1=xk, op0=ALU.mult, op1=ALU.add).then_inc(bank_free[st_.par][side], 1)

            def mixer(s, l, b):
                first, mi = FIRST[s], MIXERS.index(s)
                other = lambda k: x[:, k, (1 - b) * T:(2 - b) * T]
                dve.wait_ge(hist_ready, 2 * mi + 1)
                for st_ in pairs(dve, first, CONV_PAIRS):
                    j = st_.m
                    tap0 = (j + CT * mi) * TAPS
                    dve.wait_ge(slab_done[1], st_.P + 1)
                    dve.wait_ge(bank_free[st_.par][0], st_.half + 2)
                    dve.scalar_tensor_tensor(out=glu[:, bass.ds(j, 1), HIST:], in0=tanh_g[:].rearrange("p (o n) -> p o n", o=1),
                                             scalar=1.0, in1=bank[st_.par][1][:].rearrange("p (o n) -> p o n", o=1),
                                             op0=ALU.add, op1=ALU.mult).then_inc(bank_free[st_.par][1], 1)
                    dve.wait_ge(bank_free[st_.par][1], st_.half + 2)
                    even, odd = conv[:, bass.ds(j, 1), :], conv_odd[:].rearrange("p (o n) -> p o n", o=1)
                    for k in range(CONV_K):
                        src = glu[:, bass.ds(j, 1), k:k + T]
                        w = par2[:, l, bass.ds(j + k * CT, 1)]
                        if k == 0:
                            ins = dve.tensor_scalar(even, src, w, par1[:, l, bass.ds(j + OFF["conv_b"], 1)], ALU.mult, ALU.add)
                        elif k == 1:
                            ins = dve.tensor_scalar(odd, src, w, None, ALU.mult)
                        else:
                            dve.wait_ge(conv_step, tap0 + k - 1)
                            acc = odd if k % 2 else even
                            ins = dve.scalar_tensor_tensor(out=acc, in0=src, scalar=w, in1=acc, op0=ALU.mult, op1=ALU.add)
                        ins.then_inc(conv_step, 1)
                    dve.wait_ge(conv_step, tap0 + CONV_K)
                    dve.tensor_tensor(even, even, odd, ALU.add).then_inc(conv_step, 1)
                if s:
                    center(("x", s - 1), other)
                dve.wait_ge(cs_in, 32 * (mi + 1))
                cos, sin = cs[:, 0, :], cs[:, 1, :]
                for j in range(QT + 1):
                    shape = chunked if j < QT else lambda t: t
                    src = q[:, :, j, :] if j < QT else k_raw[:]
                    part = shape(conv_odd[:])
                    if j == 0:
                        dve.wait_ge(conv_step, CT * TAPS * (mi + 1))
                    else:
                        dve.wait_ge(att_dve, AT_ADVE[s, "rope", j - 1])
                    dve.wait_ge(rot_done, (QT + 1) * mi + j + 1)
                    dve.tensor_tensor(part, shape((b7 if j % 2 else b6)[:]), shape(sin), ALU.mult).then_inc(att_dve, 1)
                    dve.tensor_tensor(src, src, shape(cos), ALU.mult).then_inc(att_dve, 1)
                    dve.wait_ge(att_dve, AT_ADVE[s, "cos", j])
                    if j < QT:
                        dve.tensor_tensor(src, src, part, ALU.add).then_inc(att_dve, 1)
                    else:
                        dve.wait_ge(hist_ready, 2 * (mi + 1))
                        for g in (0, 1):
                            h = slice(g * HEAD, (g + 1) * HEAD)
                            dve.tensor_tensor(kz[h, g, CHUNK:], k_raw[h, :], conv_odd[h, :], ALU.add).then_inc(att_dve, 1)
                if s:
                    rsqrt(("x", s - 1))
                for n in range(NCH + 2):
                    if n < NCH:
                        r = n % 2
                        dve.wait_ge(scores_done, mi * NCH + n + 1)
                        if n == 0 and b == 0:
                            dve.memset(sbank[r][:, :, 0:CHUNK], NEG).then_inc(att_dve, 1)
                            dve.wait_ge(att_dve, AT_ADVE[s, "mask", n])
                        dve.tensor_reduce(st[:, r, 0, :], sbank[r][:], AX.X, ALU.max).then_inc(att_dve, 1)
                        dve.wait_ge(att_dve, AT_ADVE[s, "max", n])
                        dve.scalar_tensor_tensor(out=st[:, r, 1, :], in0=st[:, r, 0, :], scalar=-SCALE, in1=nsink[:, l, :],
                                                 op0=ALU.mult, op1=ALU.min).then_inc(att_dve, 1)
                        dve.wait_ge(att_dve, AT_ADVE[s, "negmax", n])
                        dve.tensor_tensor(st[:, r, 2, :], st[:, r, 1, :], nsink[:, l, :], ALU.subtract).then_inc(att_dve, 1)
                    if 1 <= n <= NCH:
                        r = (n - 1) % 2
                        dve.wait_ge(att_act, AT_AACT[s, "esink", n - 1])
                        dve.tensor_tensor(st[:, r, 5, :], st[:, r, 3, :], st[:, r, 4, :], ALU.add).then_inc(att_dve, 1)
                        dve.wait_ge(att_dve, AT_ADVE[s, "den", n - 1])
                        dve.reciprocal(st[:, r, 0, :], st[:, r, 5, :]).then_inc(att_dve, 1)
                        dve.wait_ge(att_dve, AT_ADVE[s, "inv", n - 1])
                        dve.tensor_tensor(probs[:, r, :, :], probs[:, r, :, :],
                                          st[:, r, 0, :].rearrange("p (i o) -> p i o", o=1).to_broadcast([P, QT, P]),
                                          ALU.mult).then_inc(att_dve, 1)
                    if n >= 2:
                        dve.wait_ge(att_act, AT_AACT[s, "hi", n - 2])
                        c = slice((n - 2) * CHUNK, (n - 1) * CHUNK)
                        dve.tensor_tensor(u_lo[b][:, CT:DT, c], b7[:, 0:QT * CHUNK].rearrange("p (j t) -> p j t", j=QT),
                                          u_hi[b][:, CT:DT, c].bitcast(F32), ALU.subtract).then_inc(att_dve, 1)
                if s:
                    rescale(("x", s - 1), other)
                    inputs_lo(s - 1)
                name, ck = ("c", s), lambda k: conv[:, k, :]
                center(name, ck)
                rsqrt(name)
                rescale(name, ck)
                for k in range(CT + 1):
                    if k < CT:
                        dve.wait_ge(norm_act, AT_ACT[name, "th", k])
                        t = tmp[:, k % 2, :]
                        dve.scalar_tensor_tensor(out=t, in0=t, scalar=1.0, in1=conv[:, k, :], op0=ALU.add,
                                                 op1=ALU.mult).then_inc(norm_dve, 1)
                    if k:
                        dve.wait_ge(norm_act, AT_ACT[name, "hi", k - 1])
                        dve.scalar_tensor_tensor(out=u_lo[b][:, k - 1, :], in0=tmp[:, (k - 1) % 2, :], scalar=0.5,
                                                 in1=u_hi[b][:, k - 1, :].bitcast(F32), op0=ALU.mult,
                                                 op1=ALU.subtract).then_inc(norm_dve, 1)
                if s:
                    wait_x(dve, s)
                for st_ in pairs(dve, first + CONV_PAIRS + QKV_PAIRS, OUT_PAIRS):
                    residual(l, 0, b, st_)

            def wait_x(eng, s):
                if s >= 2:
                    eng.wait_ge(norm_act, AT_ACT[("x", s - 2), "x", DT - 1])

            def mlp(s, l, b):
                first = FIRST[s]
                other = lambda k: x[:, k, (1 - b) * T:(2 - b) * T]
                if b == 0 and l:
                    dve.wait_ge(gate_step, hidden(s, 0))
                    dve.memset(ghist[:], 0.0).then_inc(ghist_clear, 1)
                    dve.wait_ge(ghist_clear, l)
                for g in range(GROUPS):
                    for st_ in pairs(dve, first, GT):
                        f = st_.m + g * GT
                        n = f + FT * mlp_no(s)
                        nk = GT if isinstance(st_.m, int) and st_.m == GT - 1 else DT
                        at = n * GATE + 1
                        hist = ghist[:, bass.ds(f, 1), :].rearrange("p o n -> p (o n)")
                        dve.wait_ge(slab_done[0], st_.P + 1)
                        dve.tensor_copy(gate[:, 0:FK - 1], hist).then_inc(gate_step, 1)
                        dve.wait_ge(bank_free[st_.par][0], st_.half + 2)
                        dve.wait_ge(gate_step, at + 1)
                        dve.scalar_tensor_tensor(out=gacc[:], in0=gate[:, 1:1 + T], scalar=par3[:, l, bass.ds(f + FT, 1)],
                                                 in1=gacc[:], op0=ALU.mult, op1=ALU.add).then_inc(gate_step, 1)
                        dve.tensor_copy(hist, gate[:, T:T + FK - 1]).then_inc(gate_step, 1)
                        dve.wait_ge(gate_step, at + 2)
                        dve.scalar_tensor_tensor(out=gacc[:], in0=gate[:, 0:T], scalar=par3[:, l, bass.ds(f, 1)],
                                                 in1=gacc[:], op0=ALU.mult, op1=ALU.add).then_inc(gate_step, 1)
                        split_lo(st_, 0, nk)
                        dve.wait_ge(gate_act, n * 3 + 2)
                        dve.scalar_tensor_tensor(out=tanh_c[:], in0=tanh_c[:], scalar=1.0, in1=gacc[:],
                                                 op0=ALU.add, op1=ALU.mult).then_inc(gate_step, 1)
                        dve.wait_ge(gate_step, at + 5)
                        dve.wait_ge(slab_done[1], st_.P + 1)
                        dve.scalar_tensor_tensor(out=gacc[:], in0=bank[st_.par][1][:], scalar=0.5, in1=tanh_c[:],
                                                 op0=ALU.mult, op1=ALU.mult).then_inc(bank_free[st_.par][1], 1)
                        dve.wait_ge(gate_act, n * 3 + 3)
                        o = lambda t: t.rearrange("p (o n) -> p o n", o=1)
                        dve.tensor_tensor(h_lo[:, bass.ds(st_.m, 1), :], o(gacc[:]),
                                          h_hi[:, bass.ds(st_.m, 1), :].bitcast(F32), ALU.subtract).then_inc(gate_step, 1)
                    first += GT
                    if g == 0:
                        center(("x", s - 1), other)
                    else:
                        rescale(("x", s - 1), other)
                        inputs_lo(s - 1)
                    if g == 0:
                        wait_x(dve, s)
                    last = s == LAST and g == GROUPS - 1
                    for st_ in pairs(dve, first, DOWN_PAIRS, straight=last):
                        if not last or st_.m < DOWN_PAIRS - 1:
                            split_lo(st_, 0, GT)
                        residual(l, 1, b, st_)
                    first += DOWN_PAIRS
                    if g == 0:
                        rsqrt(("x", s - 1))

            for s, (l, m, b) in enumerate(STAGES):
                (mlp if m else mixer)(s, l, b)
            lastx = lambda k: x[:, k, T:]
            center(("x", LAST), lastx)
            rsqrt(("x", LAST))
            rescale(("x", LAST), lastx)
            for t in range(TT):
                dve.wait_ge(y_t_done, 2 * t + 2)
                if t >= 2:
                    dve.wait_ge(y_out[t % 2], 16 * (t // 2))
                dve.tensor_copy(stage_out[t % 2][:, D // 2:], bank[t % 2][1][:]).then_inc(y_evac[1], 1)

        @block.gpsimd
        def _(pool):
            def split_lo(step_, side, nk):
                pool.wait_ge(hi_ready[side], step_.P + 2)
                pool.tensor_tensor(w_lo[side][:, 0:nk, :], raw[1 - step_.par][side][:, 0:nk, :],
                                   w_hi[side][:, 0:nk, :].bitcast(F32), ALU.subtract).then_inc(lo_ready[side], 1)

            def sum_squares(name):
                n = DT if name[0] == "x" else CT
                pool.wait_ge(stat_done, AT_STAT[name, "mean"])
                for k in range(1, n):
                    pool.wait_ge(norm_act, AT_ACT[name, "sq", k])
                    if k > 1:
                        pool.wait_ge(norm_pool, AT_POOL[name, "sq", k - 1])
                    pool.tensor_tensor(ssum[:], tmp[:, k % 2, :], (tmp[:, 0, :] if k == 1 else ssum[:]), ALU.add).then_inc(norm_pool, 1)

            def clear_sum(s):
                name = ("c", s) if s in MIXERS else ("x", s - 1)
                pool.wait_ge(stat_done, AT_STAT[name, "var"])
                pool.memset(ssum[:], 0.0).then_inc(norm_pool, 1)

            def add_residual(s, st_, side):
                k = st_.m * 2 + side
                b = STAGES[s][2]
                pool.wait_ge(norm_pool, k + AT_POOL["sum", s, -1])
                pool.wait_ge(bank_free[st_.par][side], st_.half + 2)
                pool.tensor_tensor(ssum[:].rearrange("p (o n) -> p o n", o=1), ssum[:].rearrange("p (o n) -> p o n", o=1),
                                   x[:, bass.ds(k, 1), b * T:(b + 1) * T], ALU.add).then_inc(norm_pool, 1)

            def mixer(s, l, b):
                first, mi = FIRST[s], MIXERS.index(s)
                if b == 0:
                    if s == 0:
                        pool.wait_ge(set_dve, SET_DVE["fold", 1])
                        pool.wait_ge(tab_out, 32)
                    else:
                        for side in (0, 1):
                            pool.wait_ge(slab_done[side], first)
                    pool.memset(glu[:, :, 0:HIST], 0.0).then_inc(hist_ready, 1)
                    pool.memset(v_t[:, 0:CHUNK], 0.0)
                    pool.memset(kz[:], 0.0).then_inc(hist_ready, 1)
                else:
                    pool.wait_ge(conv_step, CT * TAPS * mi)
                    pool.tensor_copy(glu[:, :, 0:HIST], glu[:, :, T:T + HIST]).then_inc(hist_ready, 1)
                    pool.tensor_copy(v_t[:, 0:CHUNK], v_t[:, T:T + CHUNK])
                    pool.tensor_copy(kz[:, :, 0:CHUNK], kz[:, :, T:T + CHUNK]).then_inc(hist_ready, 1)
                for st_ in pairs(pool, first, CONV_PAIRS):
                    for side in (0, 1):
                        split_lo(st_, side, DT)
                for st_ in pairs(pool, first + CONV_PAIRS, QKV_PAIRS):
                    for side in (0, 1):
                        split_lo(st_, side, DT)
                if s:
                    sum_squares(("x", s - 1))
                    pool.wait_ge(stat_done, AT_STAT[("x", s - 1), "var"])
                pool.wait_ge(conv_step, CT * TAPS * (mi + 1))
                for k in range(1, CT):
                    if k > 1:
                        pool.wait_ge(norm_pool, AT_POOL[("c", s), "pre", k - 1])
                    pool.tensor_tensor(ssum[:], conv[:, k, :], conv[:, 0, :] if k == 1 else ssum[:], ALU.add).then_inc(norm_pool, 1)
                sum_squares(("c", s))
                clear_sum(s)
                for st_ in pairs(pool, first + CONV_PAIRS + QKV_PAIRS, OUT_PAIRS):
                    for side in (0, 1):
                        split_lo(st_, side, DT)
                    for side in (0, 1):
                        add_residual(s, st_, side)

            def mlp(s, l, b):
                first = FIRST[s]
                for g in range(GROUPS):
                    for st_ in pairs(pool, first, GT):
                        nk = GT if isinstance(st_.m, int) and st_.m == GT - 1 else DT
                        split_lo(st_, 1, nk)
                    first += GT
                    if g == 0:
                        sum_squares(("x", s - 1))
                    else:
                        clear_sum(s)
                    last = s == LAST and g == GROUPS - 1
                    for st_ in pairs(pool, first, DOWN_PAIRS, straight=last):
                        if not last or st_.m < DOWN_PAIRS - 1:
                            split_lo(st_, 1, GT)
                        if g == GROUPS - 1:
                            for side in (0, 1):
                                add_residual(s, st_, side)
                    first += DOWN_PAIRS

            for s, (l, m, b) in enumerate(STAGES):
                (mlp if m else mixer)(s, l, b)
            sum_squares(("x", LAST))


def mlp_no(s):
    return sum(m for _, m, _ in STAGES[:s])


def hidden(s, f):
    return 1 + GATE * (f + FT * mlp_no(s))


def base_mixer(s):
    return max(t for t in MIXERS if t < s)


def need_u(s, k):
    if s < NBLK:
        return AT_DVE["init", s, "lo", k]
    return AT_DVE[("x", s - 2), "lo", k]


IN_CONST = 2 + DEPTH * (len(ROWS1) + 2 + 2)
MAGIC = 12582912.0
PI_DOWN = float(np.nextafter(np.float32(np.pi), np.float32(0.0)))


def two_pi_parts():
    rest, parts = 2 * np.pi, []
    for _ in range(3):
        e = 2.0 ** (np.floor(np.log2(rest)) - 7)
        parts.append(float(np.floor(rest / e) * e))
        rest -= parts[-1]
    return parts + [float(np.float32(rest))]


TWO_PI = two_pi_parts()
SET_DVE = {("par", 0): 2, ("par", 1): 4}
_n = 4 + 1 + 2
for _i in (0, 1):
    _n += 3 + len(TWO_PI) + 2
    SET_DVE["reduced", _i] = _n
_n += 2
SET_DVE["mod", 1] = _n
_n += 4 + 3 * (2 * DEPTH - 1)
SET_DVE["fold", 1] = _n
SET_ACT = {("table", 0): 1, ("table", 1): 2}


def constants():
    ident = np.eye(P, dtype=np.float32)
    rot = np.zeros((P, P), np.float32)
    freq = np.zeros((P, 1), np.float32)
    for g in range(P // HEAD):
        for j in range(HALF):
            lo, hi = g * HEAD + j, g * HEAD + HALF + j
            rot[hi, lo] = -1.0
            rot[lo, hi] = 1.0
            freq[lo, 0] = freq[hi, 0] = THETA ** (-2.0 * j / ROT)
    ones = np.ones((P, P), np.float32)
    return np.concatenate([ident, rot, ones * np.float32(1.0 / D), ones * np.float32(1.0 / CONV_CH), ones, freq], axis=1)


_INS = ["x", "c", "positions", "w_ada_mix", "b_ada_mix", "w_in", "conv_w", "conv_b", "conv_ln_g", "conv_ln_b",
        "sinks", "w_out", "ln1_g", "ln1_b", "w_ada_ffn", "b_ada_ffn", "w_up", "ffn_conv_w", "ffn_conv_b",
        "w_down", "ln2_g", "ln2_b"]


def kernel(**inputs):
    import concourse.bacc as _bacc
    from concourse.bass_utils import run_bass_kernel_spmd as _run

    nc = _bacc.Bacc("TRN2", target_bir_lowering=False, num_devices=1)
    arrays, args = {}, {}
    for name in _INS + ["consts"]:
        arr = constants() if name == "consts" else np.ascontiguousarray(inputs[name])
        arrays[f"in_{name}_dram"] = arr
        args[name] = nc.dram_tensor(f"in_{name}_dram", arr.shape, mybir.dt.from_np(arr.dtype), kind="ExternalInput").ap()
    args["out"] = nc.dram_tensor("out_dram", (1, SEQ, D), F32, kind="ExternalOutput").ap()
    build(nc, args)
    r = _run(nc, [arrays], core_ids=[0])
    return r.results[0]["out_dram"]
```

```python
from contextlib import ExitStack

import numpy as np

import concourse.bass as bass
from concourse import mybir

ALU = mybir.AluOpType
ACT = mybir.ActivationFunctionType
AX = mybir.AxisListType
F32 = mybir.dt.float32
F32R = mybir.dt.float32r
I32 = mybir.dt.int32

P = 128
DEPTH = 2
D = 1024
SEQ = 1024
DT = D // P
NBLK = 2
T = SEQ // NBLK
CONV_CH = 512
CT = CONV_CH // P
CONV_K = 31
HIST = CONV_K - 1
HEAD = 64
HQ = 8
QT = 4
CHUNK = 64
NCH = T // CHUNK
Q0 = 2 * CONV_CH
K0 = Q0 + HQ * HEAD
V0 = K0 + 2 * HEAD
F = 2816
FT = F // P
GROUP = [6, 5, 6, 5]
START = [sum(GROUP[:g]) for g in range(len(GROUP))]
LAST_G = len(GROUP) - 1
FK = 3
ROT = HEAD // 4
HALF = ROT // 2
THETA = 500000.0
FBLK = P // HALF
EPS = 1e-5
ALPHA2 = (2.0 * DEPTH) ** 0.5
INV_ALPHA = (2.0 * DEPTH) ** -0.25
SCALE = HEAD ** -0.5
NEG = -1e30

CONV_PAIRS, QKV_PAIRS, OUT_PAIRS, DOWN_PAIRS = CT, 3, DT // 2, DT // 2
MIX_PAIRS = CONV_PAIRS + QKV_PAIRS + OUT_PAIRS
MLP_PAIRS = FT + len(GROUP) * DOWN_PAIRS
STAGES = [(l, m, b) for l in range(DEPTH) for m in (0, 1) for b in range(NBLK)]
FIRST = []
_n = 0
for _l, _m, _b in STAGES:
    FIRST.append(_n)
    _n += MLP_PAIRS if _m else MIX_PAIRS
N_PAIRS = _n
LAST = len(STAGES) - 1

ROWS1 = [("ln1_g", DT), ("ln1_b", DT), ("ln2_g", DT), ("ln2_b", DT), ("conv_b", CT), ("conv_ln_g", CT),
         ("conv_ln_b", CT), ("ffn_conv_b", FT), ("b_ada_mix", 3 * DT), ("b_ada_ffn", 3 * DT)]
N1 = sum(n for _, n in ROWS1)
N2 = CONV_K * CT
N3 = FK * FT
OFF = {}
_n = 0
for _name, _c in ROWS1:
    OFF[_name] = _n
    _n += _c


def chunked(t):
    return t.rearrange("p (n c) -> p n c", c=CHUNK)


class Step:

    def __init__(self, first, i, u):
        self.P = i * 2 + (first + u)
        self.half = i + (first + u) // 2
        self.par = (first + u) % 2
        self.m = i * 2 + u
        self.trip, self.u = (u // 2, u % 2) if isinstance(i, int) else (i, u)


def pairs(eng, first, n, straight=False):
    trips = 0 if straight or n < 4 else n // 2
    if trips:
        with eng.Fori(0, trips) as i:
            for u in (0, 1):
                yield Step(first, i, u)
    for m in range(2 * trips, n):
        yield Step(first, 0, m)


def number(names):
    at = {}
    for n, name in enumerate(names):
        assert name not in at
        at[name] = n + 1
    return at


NORMS = []
for _s, (_l, _m, _b) in enumerate(STAGES):
    if _s:
        NORMS.append((("x", _s - 1), DT))
    if not _m:
        NORMS.append((("c", _s), CT))
NORMS.append((("x", LAST), DT))
SMALL = 12
PARTS = ("mean", "var", "read", "small", "rstd", "out")


def both(m):
    return (2 * m, 2 * m + 1)


def centered_by_pool(name):
    return name[0] == "x" and name[1] < LAST and not STAGES[name[1] + 1][1]



def norm_events():
    stat, dve, act, pool = [], [], [], []

    def init(b):
        for k in range(DT):
            act.extend([("init", b, "u", k), ("init", b, "hi", k)])
            dve.append(("init", b, "lo", k))

    init(0)
    for s, (l, m, b) in enumerate(STAGES):
        x_norm = norm_parts(("x", s - 1), DT) if s else None
        c_norm = norm_parts(("c", s), CT) if not m else None
        if x_norm and c_norm:
            order = [(x_norm, "mean"), (x_norm, "var"), (x_norm, "read"), (c_norm, "mean"), (c_norm, "var"),
                     (c_norm, "read"), (c_norm, "small"), (c_norm, "rstd"), (x_norm, "small"), (x_norm, "rstd"),
                     (c_norm, "out"), (x_norm, "out")]
        else:
            order = [(x_norm or c_norm, part) for part in PARTS]
        for norm, part in order:
            for events, new in zip((stat, dve, act, pool), norm[part]):
                events += new
        if s == 0:
            init(1)
        pool += [("sum", s, k) for k in range(-1, DT)]
    for part in PARTS:
        for events, new in zip((stat, dve, act, pool), norm_parts(("x", LAST), DT)[part]):
            events += new
    return number(stat), number(dve), number(act), number(pool)


def norm_parts(name, n):
    dve_out, act_out = [], []
    if name[0] == "c":
        for k in range(n + 1):
            if k < n:
                act_out += [(name, "z", k), (name, "th", k)]
                dve_out += [(name, "m", k)]
            if k:
                act_out += [(name, "hi", k - 1)]
                dve_out += [(name, "lo", k - 1)]
    elif name[1] < LAST - 1:
        for k in range(n):
            act_out += [(name, "u", k), (name, "hi", k), (name, "x", k)]
    else:
        act_out = [(name, "x", k) for k in range(n)]
    scales = [(name, "scale", k) for k in range(n)]
    if name[0] == "x" and name[1] < LAST - 1:
        dve_out = [(name, what, k) for m in range(n // 2) for what in ("scale", "lo") for k in both(m)]
    else:
        dve_out = scales + dve_out
    center = [(name, "center", k) for k in range(n)]
    dve_center, pool_center = ([], center) if centered_by_pool(name) else (center, [])
    return {
        "mean": ([(name, "mean")], dve_center,
                 ([(name, "copied")] if pool_center else []) + [(name, "sq", k) for k in range(n)],
                 pool_center + ([(name, "pre", k) for k in range(1, n)] if name[0] == "c" else []) + [(name, "sq", k) for k in range(1, n)]),
        "var": ([(name, "var")], [], [], []),
        "read": ([], [(name, "small", 0)], [], []),
        "small": ([], [(name, "small", k) for k in range(1, SMALL)] + [(name, "diag", k) for k in range(T // P)], [], []),
        "rstd": ([(name, "rstd")], [], [], []),
        "out": ([], dve_out, act_out, []),
    }


AT_STAT, AT_DVE, AT_ACT, AT_POOL = norm_events()
MIXERS = [s for s, (_, m, _) in enumerate(STAGES) if not m]


def attention_events():
    dve, act = [], []
    for s in MIXERS:
        for j in range(QT + 1):
            dve += [(s, "sin", j), (s, "rope", j)] + ([(s, "rope2", j)] if j == QT else [])
        for n in range(NCH + 3):
            if n < NCH:
                dve += [(s, "mask", n)] if n == 0 and STAGES[s][2] == 0 else []
                dve += [(s, "max", n), (s, "negmax", n), (s, "sink", n)]
            if 1 <= n <= NCH:
                dve += [(s, e, n - 1) for e in ("den", "inv", "probs")]
            if n >= 3:
                dve += [(s, "lo", n - 3)]
        act += [(s, "v", 0), (s, "v", 1)]
        for n in range(NCH + 2):
            if n < NCH:
                act += [(s, "exp", n, i) for i in range(QT)] + [(s, "esink", n)]
            if 1 <= n <= NCH:
                act += [(s, "probsT", n - 1)]
            if n >= 2:
                act += [(s, "hi", n - 2)]
    return number(dve), number(act)


AT_ADVE, AT_AACT = attention_events()
C_NORM_PE = {2: "var", 4: "rstd"}
C_NORM_ACT = {1: "squares", 6: 0, 7: 1, 8: 2, 9: 3}
C_NORM_DVE = {0: "center", 4: "small", 5: "x small", 6: "scale", 7: 0, 8: 1, 9: 2, 10: 3}
TAPS = CONV_K + 2
GATE = 6

NCHUNK = 3 * D // T
CHUNKS_BEFORE = 4
ADA_AT = {(0, "out"): (6, 1), (1, "out"): (10, 0.5)}
for _g in range(6):
    ADA_AT[2 + _g // 4, _g % 4] = (12 + 2 * _g, 0.5)
FOLD_AT = {0: [("ss", 0)], "out of 0": [("gate", 0)], 1: [("ss", 1)], 2: [("gate", 1)], 3: [("ss", 2), ("gate", 2)],
           4: [("ss", 3), ("gate", 3)]}
AT_FOLD = {}
_n = 0
for _s in FOLD_AT:
    for _what, _i in FOLD_AT[_s]:
        _n += 2 if _what == "gate" else 5 if _i else 3
        AT_FOLD[_what, _i] = _n


def ada_steps(s, phase, st_):
    if (s, phase) not in ADA_AT:
        return []
    first, rate = ADA_AT[s, phase]
    if rate == 1:
        return [(first, st_.m, (0, 1))]
    return [(first, st_.trip, (st_.u,))]


def build(nc, a):
    ctx = ExitStack()
    with ctx:
        def sb(name, shape, dt=F32, stack=ctx):
            return stack.enter_context(nc.sbuf_tensor(name, shape, dt))

        def sem(name):
            return ctx.enter_context(nc.semaphore(name))

        x = sb("x", [P, DT, SEQ])
        u_hi = [sb(f"u_hi{b}", [P, DT, T], F32R) for b in range(NBLK)]
        u_lo = [sb(f"u_lo{b}", [P, DT, T], F32R) for b in range(NBLK)]
        raw = [[sb(f"raw{r}{s}", [P, DT, P]) for s in (0, 1)] for r in (0, 1)]
        w_hi = [sb(f"w_hi{s}", [P, DT, P], F32R) for s in (0, 1)]
        w_lo = [sb(f"w_lo{s}", [P, DT, P], F32R) for s in (0, 1)]
        ada = [sb(f"ada{i}", [P, DT // 2, T]) for i in (0, 1)]
        ada_acc = sb("ada_acc", [P, T])
        tmp = sb("tmp", [P, 2, T])
        ssum = sb("ssum", [P, T])
        diag = sb("diag", [P, T // P, P])
        small = sb("small", [P, 2, 3, T // P])
        const = sb("const", [P, 5 * P + 1])
        ident, rot, ones_d, ones_c, ones_1 = (const[:, i * P:(i + 1) * P] for i in range(5))
        inv_freq = const[:, 5 * P:5 * P + 1]
        par1 = sb("par1", [P, DEPTH, N1])
        par2 = sb("par2", [P, DEPTH, N2])
        par3 = sb("par3", [P, DEPTH, N3])
        ccol = sb("ccol", [P, DT])
        mod = sb("mod", [P, DEPTH, 2, 3 * DT])
        gain = sb("gain", [P, len(STAGES) // NBLK, DT])
        bias = sb("bias", [P, len(STAGES) // NBLK, DT])
        nsink = sb("nsink", [P, DEPTH, QT])
        ghist = sb("ghist", [P, FT, FK - 1])
        st = sb("st", [P, 2, 7, QT])

        with ExitStack() as region:
            rows1, rows2, rows3 = (sb(f"rows{i}", [P, DEPTH, P], stack=region) for i in (1, 2, 3))
            rowsc = sb("rowsc", [DT, P], stack=region)
            stage_in = [sb(f"stage_in{i}", [P, D], stack=region) for i in (0, 1)]
            pos = sb("pos", [P, SEQ // FBLK], I32, stack=region)
            ang = sb("ang", [P, SEQ // FBLK], stack=region)
            turns = sb("turns", [P, SEQ // FBLK], stack=region)
            tabs = [sb(f"tab{i}", [P, SEQ // FBLK], stack=region) for i in (0, 1)]
        with ExitStack() as region:
            glu = sb("glu", [P, CT, HIST + T], stack=region)
            conv = sb("conv", [P, CT, T], stack=region)
            q = sb("q", [P, NCH, QT, CHUNK], stack=region)
            kz = sb("kz", [P, 2, CHUNK + T], stack=region)
            v_t = sb("v_t", [P, CHUNK + T], stack=region)
            v = sb("v", [P, NCH, P], stack=region)
            probs = sb("probs", [P, 2, QT, P], stack=region)
            probs_t = sb("probs_t", [P, 2, QT * P], stack=region)
            rot_part, k_raw = probs_t[:, 0, :], probs[:, 0, :, :].rearrange("p i n -> p (i n)")
            cs = sb("cs", [P, 2, T], stack=region)
        with ExitStack() as region:
            h_hi = sb("h_hi", [P, max(GROUP), T], F32R, stack=region)
            h_lo = sb("h_lo", [P, max(GROUP), T], F32R, stack=region)
            gate = sb("gate", [P, FK - 1 + T], stack=region)
            gacc = sb("gacc", [P, T], stack=region)
            tanh_c = sb("tanh_c", [P, T], stack=region)
        with ExitStack() as region:
            stage_out = [sb(f"stage_out{i}", [P, D], stack=region) for i in (0, 1)]
        tab_dram = nc.dram_tensor("rope_tables", [2, P, SEQ // FBLK], F32, kind="Internal").ap()

        bank = [[ctx.enter_context(nc.psum_tensor(f"bank{r}{s}", [P, T], F32)) for s in (0, 1)] for r in (0, 1)]
        sbank = [ctx.enter_context(nc.psum_tensor(f"sbank{i}", [P, QT, P], F32)) for i in (0, 1)]
        b6 = ctx.enter_context(nc.psum_tensor("b6", [P, T], F32))
        b7 = ctx.enter_context(nc.psum_tensor("b7", [P, T], F32))

        raw_in = [[sem(f"raw_in{r}{s}") for s in (0, 1)] for r in (0, 1)]
        hi_ready = [sem(f"hi_ready{s}") for s in (0, 1)]
        lo_ready = [sem(f"lo_ready{s}") for s in (0, 1)]
        slab_done = [sem(f"slab_done{s}") for s in (0, 1)]
        bank_free = [[sem(f"bank_free{r}{s}") for s in (0, 1)] for r in (0, 1)]
        stat_done = sem("stat_done")
        norm_dve = sem("norm_dve")
        norm_act = sem("norm_act")
        norm_pool = sem("norm_pool")
        conv_step = sem("conv_step")
        gate_step = sem("gate_step")
        ghist_clear = sem("ghist_clear")
        gate_act = sem("gate_act")
        hist_ready = sem("hist_ready")
        cs_in = sem("cs_in")
        rot_done = sem("rot_done")
        rope_cos = sem("rope_cos")
        v_done = sem("v_done")
        scores_done = sem("scores_done")
        probs_t_done = sem("probs_t_done")
        pv_done = sem("pv_done")
        att_dve = sem("att_dve")
        att_act = sem("att_act")
        in_const = sem("in_const")
        in_sinks = sem("in_sinks")
        in_pos = sem("in_pos")
        in_x = [sem("in_x0"), sem("in_x1")]
        in_ada = [sem("in_ada0"), sem("in_ada1")]
        tab_out = sem("tab_out")
        set_pe = sem("set_pe")
        set_dve = sem("set_dve")
        set_act = sem("set_act")
        x_t_done = sem("x_t_done")
        x_evac = [sem("x_evac0"), sem("x_evac1")]
        ada_add = sem("ada_add")
        ada_sum = sem("ada_sum")
        ada_copied = sem("ada_copied")
        fold_step = sem("fold_step")
        y_t_done = sem("y_t_done")
        y_evac = [sem("y_evac0"), sem("y_evac1")]
        y_out = [sem("y_out0"), sem("y_out1")]

        def centered(name, k):
            return (norm_pool, AT_POOL[name, "center", k]) if centered_by_pool(name) else (norm_dve, AT_DVE[name, "center", k])

        def rot_bank(j):
            return (bank[1][0][:], bank[1][1][:], b6[:], b7[:], sbank[0][:].rearrange("p i n -> p (i n)"))[j]

        def stat_bank(name, what):
            return bank[1][what == "var"] if name[0] == "c" else b7

        def diagonals(name):
            return ada_acc[:].rearrange("p (a b) -> p a b", b=P) if name[0] == "c" else diag[:]

        def qkv_copied(s, j):
            pair = FIRST[s] + CONV_PAIRS + j // 2
            return bank_free[pair % 2][j % 2], pair // 2 + 2

        TT = SEQ // P
        w_ada = {0: a["w_ada_mix"], 1: a["w_ada_ffn"]}

        block = ctx.enter_context(nc.Block())

        @block.sync
        def _(sp):
            def load_ada(base, more, half):
                l, m = base // NCHUNK // 2, base // NCHUNK % 2
                if not isinstance(more, int) or base + more:
                    sp.wait_ge(ada_add, more * DT + DT * (base - 1) + DT // 2 * (half + 1))
                src = w_ada[m][l, half * D // 2:(half + 1) * D // 2, bass.ds((more + base % NCHUNK) * T, T)]
                sp.dma_start(ada[half][:], src.rearrange("(k p) n -> p k n", p=P)).then_inc(in_ada[half], 16)

            def load_adas(s, phase, st_):
                for base, more, halves in ada_steps(s, phase, st_):
                    for half in halves:
                        load_ada(base, more, half)

            def load_x(t):
                if t >= 2:
                    sp.wait_ge(x_t_done, 2 * (t - 1))
                sp.dma_start(stage_in[t % 2][:], a["x"][0, t * P:(t + 1) * P, :]).then_inc(in_x[t % 2], 16)

            def load(step, parts):
                if not isinstance(step.P, int) or step.P >= 2:
                    for s in (0, 1):
                        sp.wait_ge(lo_ready[s], step.P - 1)
                for s in (0, 1):
                    pieces = parts(s)
                    for n, (dst, src) in enumerate(pieces):
                        inc = 48 if len(pieces) == 1 else 16 if len(pieces) == 3 or n == 0 else 32
                        sp.dma_start(dst, src).then_inc(raw_in[step.par][s], inc)

            def columns(w, r0, nk, c0):
                return w[r0:r0 + nk * P, bass.ds(c0, P)].rearrange("(k p) m -> p k m", p=P)

            def mixer(s, l, b):
                first = FIRST[s]
                w = a["w_in"][l]
                for st_ in pairs(sp, first, CONV_PAIRS, straight=s == 0):
                    load(st_, lambda side: [(raw[st_.par][side][:],
                                             columns(w, 0, DT, st_.m * P + (CONV_CH if side == 0 else 0)))])
                    if s == 0 and st_.m < 2:
                        for half in (0, 1):
                            load_ada(CHUNKS_BEFORE + st_.m, 0, half)
                if s == 0:
                    sp.wait_ge(tab_out, 32)
                for i in (0, 1):
                    table = tab_dram[i].rearrange("(f k) n -> f (k n)", k=FBLK)[:, b * T:(b + 1) * T]
                    for r in range(0, P, HEAD):
                        for r0 in (r, r + HALF):
                            sp.dma_start(cs[r0:r0 + HALF, i, :], table).then_inc(cs_in, 16)
                        sp.dma_start(cs[r + ROT:r + HEAD, i, :], a["plain"][i]).then_inc(cs_in, 16)
                for st_ in pairs(sp, first + CONV_PAIRS, QKV_PAIRS):
                    def parts(side):
                        j = 2 * st_.m + side
                        if j >= QT:
                            return [(raw[st_.par][side][:], columns(w, 0, DT, K0 + (j - QT) * P))]
                        return [(raw[st_.par][side][:, :, g * HEAD:(g + 1) * HEAD],
                                 w[:, Q0 + (g * QT + j) * HEAD:Q0 + (g * QT + j + 1) * HEAD].rearrange("(k p) m -> p k m", p=P))
                                for g in (0, 1)]
                    load(st_, parts)
                w = a["w_out"][l]
                for st_ in pairs(sp, first + CONV_PAIRS + QKV_PAIRS, OUT_PAIRS):
                    def parts(side):
                        c0 = (st_.m * 2 + side) * P
                        dst = raw[st_.par][side]
                        return [(dst[:, 0:CT, :], columns(w, 0, CT, c0))] + [
                            (dst[g * HEAD:(g + 1) * HEAD, CT:DT, :],
                             w[CONV_CH + g * QT * HEAD:CONV_CH + (g + 1) * QT * HEAD, bass.ds(c0, P)].rearrange("(j d) m -> d j m", d=HEAD))
                            for g in (0, 1)]
                    load(st_, parts)
                    load_adas(s, "out", st_)

            def mlp(s, l, b):
                first = FIRST[s]
                for g, n in enumerate(GROUP):
                    w = a["w_up"][l]
                    for st_ in pairs(sp, first, n):
                        load(st_, lambda side: [(raw[st_.par][side][:],
                                                 columns(w, 0, DT, (st_.m + START[g]) * P + (F if side == 0 else 0)))])
                    first += n
                    w = a["w_down"][l]
                    for st_ in pairs(sp, first, DOWN_PAIRS):
                        load(st_, lambda side: [(raw[st_.par][side][:, 0:n, :],
                                                 columns(w, START[g] * P, n, (st_.m * 2 + side) * P))])
                        load_adas(s, g, st_)
                    first += DOWN_PAIRS

            for t in range(TT):
                load_x(t)
                if t < CHUNKS_BEFORE:
                    for half in (0, 1):
                        load_ada(t, 0, half)
            sp.wait_ge(set_act, SET_ACT["table", 1])
            for i in (0, 1):
                sp.dma_start(tab_dram[i], tabs[i][:]).then_inc(tab_out, 16)
            for s, (l, m, b) in enumerate(STAGES):
                (mlp if m else mixer)(s, l, b)
            for t in range(TT):
                sp.wait_ge(y_evac[0], t + 1)
                sp.wait_ge(y_evac[1], t + 1)
                sp.dma_start(a["out"][0, t * P:(t + 1) * P, :], stage_out[t % 2][:]).then_inc(y_out[t % 2], 16)
            for i in (0, 1):
                sp.wait_ge(y_out[i], 16 * TT // 2)

        @block.tensor
        def _(pe):
            pe.wait_ge(in_const, 16 * IN_CONST)
            srcs = [(rows1[:, l, :], N1) for l in range(DEPTH)] + [(rows2[:, l, :], N2) for l in range(DEPTH)]
            for i, (r, n) in enumerate(srcs):
                ins = pe.transpose(b6[:, i * P:i * P + n], r[0:n, :], ident[0:n, 0:n])
            ins.then_inc(set_pe, 1)
            for i, (r, n) in enumerate([(rows3[:, 0, :], N3), (rows3[:, 1, :], N3), (rowsc, DT)]):
                ins = pe.transpose(b7[:, i * P:i * P + n], r[0:n, :], ident[0:n, 0:n])
            ins.then_inc(set_pe, 1)

            free6 = [set_dve, SET_DVE["par", 0]]
            free7 = [set_dve, SET_DVE["par", 1]]

            def take6(s, v):
                pe.wait_ge(*free6)
                free6[:] = s, v

            def take7(s, v):
                pe.wait_ge(*free7)
                free7[:] = s, v

            def sum_ada(base, more):
                pe.wait_ge(ada_add, more * DT + DT * (base + 1))
                pe.wait_ge(*free6)
                if not isinstance(more, int) or base + more:
                    pe.wait_ge(ada_copied, more + base)
                for i in range(T // P):
                    ins = pe.matmul(b6[:, i:i + 1], ada_acc[:, i * P:(i + 1) * P], ones_1[:, 0:1], start=True, stop=True)
                ins.then_inc(ada_sum, 1)

            def sum_adas(s, phase, st_):
                for base, more, halves in ada_steps(s, phase, st_):
                    if halves[-1] == 1:
                        sum_ada(base, more)

            def adas_summed(s, phase):
                if (s, phase) in ADA_AT:
                    n0, rate = ADA_AT[s, phase]
                    free6[:] = ada_copied, n0 + int(rate * DOWN_PAIRS)

            for t in range(TT):
                pe.wait_ge(in_x[t % 2], 16 * (t // 2 + 1))
                for half in (0, 1):
                    if t >= 2:
                        pe.wait_ge(x_evac[half], t - 1)
                    for k in range(4):
                        ins = pe.transpose(bank[t % 2][half][:, k * P:(k + 1) * P],
                                           stage_in[t % 2][:, (half * 4 + k) * P:(half * 4 + k + 1) * P], ident)
                    ins.then_inc(x_t_done, 1)
                if 1 <= t <= CHUNKS_BEFORE:
                    sum_ada(t - 1, 0)
            free6[:] = ada_copied, CHUNKS_BEFORE

            def slab(step, side, nk, rhs, ready=None):
                pe.wait_ge(lo_ready[side], step.P + 1)
                pe.wait_ge(bank_free[step.par][side], step.half + 1)
                out = bank[step.par][side]
                for k in range(nk):
                    if ready:
                        ready(k)
                    hi, lo = rhs(k)
                    pe.matmul(out[:], w_hi[side][:, k, :], hi, start=k == 0, stop=False)
                    pe.matmul(out[:], w_hi[side][:, k, :], lo, start=False, stop=False)
                    ins = pe.matmul(out[:], w_lo[side][:, k, :], hi, start=False, stop=k == nk - 1)
                ins.then_inc(slab_done[side], 1)

            def stat(name, what):
                n, ones = (DT, ones_d) if name[0] == "x" else (CT, ones_c)
                out = stat_bank(name, what)
                take = take7 if out is b7 else lambda s, v: None
                if what == "mean":
                    if name[0] == "x":
                        pe.wait_ge(norm_pool, AT_POOL["sum", name[1], DT - 1])
                    else:
                        pe.wait_ge(norm_pool, AT_POOL[name, "pre", n - 1])
                    take(*((norm_act, AT_ACT[name, "copied"]) if centered_by_pool(name) else centered(name, n - 1)))
                    ins = pe.matmul(out[:], ones, ssum[:], start=True, stop=True)
                elif what == "var":
                    pe.wait_ge(norm_pool, AT_POOL[name, "sq", n - 1])
                    take(norm_dve, AT_DVE[name, "small", 0])
                    for i in range(T // P):
                        ins = pe.matmul(out[:, i:i + 1], ssum[:, i * P:(i + 1) * P], ones[:, 0:1], start=True, stop=True)
                else:
                    pe.wait_ge(norm_dve, AT_DVE[name, "diag", T // P - 1])
                    take(norm_dve, AT_DVE[name, "scale", n - 1])
                    ins = pe.matmul(out[:], ones_1, diagonals(name).rearrange("p a b -> p (a b)"), start=True, stop=True)
                ins.then_inc(stat_done, 1)

            def mixer(s, l, b):
                first, mi = FIRST[s], MIXERS.index(s)
                for st_ in pairs(pe, first, CONV_PAIRS, straight=s == 0):
                    for side in (0, 1):
                        first_slab = s == 0 and st_.m == 0 and side == 0
                        if s and side == 0:
                            pe.wait_ge(norm_dve, need_u(s, DT - 1))
                        slab(st_, side, DT, lambda k: (u_hi[b][:, k, :], u_lo[b][:, k, :]),
                             (lambda k: pe.wait_ge(norm_dve, need_u(s, k))) if first_slab else None)
                    if s == 0 and st_.m < 2:
                        sum_ada(CHUNKS_BEFORE + st_.m, 0)
                if s == 0:
                    free6[:] = ada_copied, NCHUNK
                if s:
                    stat(("x", s - 1), "mean")
                for st_ in pairs(pe, first + CONV_PAIRS, QKV_PAIRS):
                    for side in (0, 1):
                        slab(st_, side, DT, lambda k: (u_hi[b][:, k, :], u_lo[b][:, k, :]))
                if s:
                    stat(("x", s - 1), "var")
                def rotate(j):
                    pe.wait_ge(*qkv_copied(s, j))
                    if j == 2:
                        take6(att_dve, AT_ADVE[s, "sin", j])
                    elif j == 3:
                        take7(att_dve, AT_ADVE[s, "sin", j])
                    elif j == QT:
                        pe.wait_ge(conv_step, CT * TAPS * (mi + 1))
                    elif j < 2:
                        for i in range(QT + 2):
                            pe.wait_ge(*qkv_copied(s, i))
                    pe.matmul(rot_bank(j), rot, q[:, :, j, :] if j < QT else k_raw,
                              start=True, stop=True).then_inc(rot_done, 1)

                for j in range(QT):
                    rotate(j)
                pe.wait_ge(*qkv_copied(s, QT + 1))
                pe.wait_ge(hist_ready, 2 * (mi + 1))
                for i in (0, 1):
                    for n in range(NCH // 2):
                        c = (i * NCH // 2 + n) * CHUNK
                        ins = pe.transpose(bank[0][i][:, n * P:(n + 1) * P], v_t[:, c:c + P], ident)
                    ins.then_inc(v_done, 1)
                rotate(QT)

                def scores(n):
                    if n == 0:
                        pe.wait_ge(att_dve, AT_ADVE[s, "rope2", QT])
                    if n >= 2:
                        pe.wait_ge(att_act, AT_AACT[s, "exp", n - 2, QT - 1])
                    else:
                        pe.wait_ge(conv_step, CT * TAPS * (mi + 1))
                    for g in (0, 1):
                        for pr in (0, 1):
                            qq = q[:, n, 2 * pr:2 * pr + 2, :].rearrange("p j t -> p (j t)")
                            ins = pe.matmul(sbank[n % 2][:, 2 * g + pr, :], qq, kz[:, g, n * CHUNK:n * CHUNK + P],
                                            start=True, stop=True)
                    ins.then_inc(scores_done, 1)

                scores(0)
                scores(1)
                stat(("c", s), "mean")
                for n in range(NCH):
                    if n + 2 < NCH:
                        scores(n + 2)
                    pe.wait_ge(att_dve, AT_ADVE[s, "probs", n])
                    (take7 if n % 2 else take6)(att_act, AT_AACT[s, "probsT", n])
                    for i in range(QT):
                        ins = pe.transpose((b7 if n % 2 else b6)[:, i * P:(i + 1) * P], probs[:, n % 2, i, :], ident)
                    ins.then_inc(probs_t_done, 1)
                    pe.wait_ge(att_act, AT_AACT[s, "probsT", n])
                    if n == 0:
                        pe.wait_ge(att_act, AT_AACT[s, "v", 1])
                    if n >= 2:
                        pe.wait_ge(att_dve, AT_ADVE[s, "lo", n - 2])
                    for g in (0, 1):
                        ins = pe.matmul(bank[0][n % 2][g * HEAD:(g + 1) * HEAD, 0:2 * P], v[:, n, g * HEAD:(g + 1) * HEAD],
                                        probs_t[:, n % 2, g * 2 * P:(g + 1) * 2 * P], start=True, stop=True)
                    ins.then_inc(pv_done, 1)
                    if n in C_NORM_PE:
                        stat(("c", s), C_NORM_PE[n])
                if s:
                    stat(("x", s - 1), "rstd")
                pe.wait_ge(norm_dve, AT_DVE[("c", s), "lo", CT - 1])
                pe.wait_ge(att_dve, AT_ADVE[s, "lo", NCH - 1])
                for st_ in pairs(pe, first + CONV_PAIRS + QKV_PAIRS, OUT_PAIRS):
                    for side in (0, 1):
                        slab(st_, side, DT, lambda k: (u_hi[b][:, k, :], u_lo[b][:, k, :]))
                    sum_adas(s, "out", st_)
                adas_summed(s, "out")

            def mlp(s, l, b):
                first = FIRST[s]
                for k in range(DT):
                    pe.wait_ge(norm_dve, need_u(s, k))
                for g, n in enumerate(GROUP):
                    for st_ in pairs(pe, first, n):
                        for side in (0, 1):
                            slab(st_, side, DT, lambda k: (u_hi[b][:, k, :], u_lo[b][:, k, :]))
                    first += n
                    if g < 2:
                        stat(("x", s - 1), ("mean", "rstd")[g])
                    done = hidden(s, START[g])
                    for st_ in pairs(pe, first, DOWN_PAIRS):
                        for side in (0, 1):
                            slab(st_, side, n, lambda k: (h_hi[:, k, :], h_lo[:, k, :]),
                                 lambda k: pe.wait_ge(gate_step, done + GATE * (k + 1)))
                        sum_adas(s, g, st_)
                    adas_summed(s, g)
                    first += DOWN_PAIRS
                    if g == 0:
                        stat(("x", s - 1), "var")

            for s, (l, m, b) in enumerate(STAGES):
                (mlp if m else mixer)(s, l, b)
            for what in ("mean", "var", "rstd"):
                stat(("x", LAST), what)
            for t in range(TT):
                for half in (0, 1):
                    if t == 0 and half == 0:
                        for k in range(DT):
                            pe.wait_ge(norm_act, AT_ACT[("x", LAST), "x", k])
                    if t >= 2:
                        pe.wait_ge(y_evac[half], t - 1)
                    for k in range(4):
                        ins = pe.transpose(bank[t % 2][half][:, k * P:(k + 1) * P],
                                           x[:, half * 4 + k, t * P:(t + 1) * P], ident)
                    ins.then_inc(y_t_done, 1)

        @block.scalar
        def _(act):
            def copy_ada(base, more):
                act.wait_ge(ada_sum, more + base + 1)
                l, m = base // NCHUNK // 2, base // NCHUNK % 2
                n = T // P
                act.activation(mod[:, l, m, bass.ds((more + base % NCHUNK) * n, n)], b6[:, 0:n], ACT.Copy).then_inc(ada_copied, 1)

            def copy_adas(s, phase, st_):
                for base, more, halves in ada_steps(s, phase, st_):
                    if halves[-1] == 1:
                        copy_ada(base, more)

            def load(dst, src):
                act.dma_start(dst, src).then_inc(in_const, 16)

            load(const[:], a["consts"])
            load(rowsc[:], a["c"].rearrange("o (t p) -> (o t) p", p=P))
            for name, n in ROWS1:
                load(rows1[OFF[name]:OFF[name] + n, :, :], a[name].rearrange("l (t p) -> t l p", p=P))
            for l in range(DEPTH):
                load(rows2[0:N2, l, :], a["conv_w"][l].rearrange("k (t p) -> (k t) p", p=P))
                load(rows3[0:N3, l, :], a["ffn_conv_w"][l].rearrange("k (t p) -> (k t) p", p=P))
            for l in range(DEPTH):
                for s in (0, 1):
                    src = a["sinks"][l].rearrange("(o j s) -> s o j", o=1, s=2)[s]
                    with nc.allow_non_contiguous_dma(reason="eight numbers"):
                        act.dma_start(nsink[s * CHUNK:(s + 1) * CHUNK, l, :], src.to_broadcast([CHUNK, QT])).then_inc(in_sinks, 16)
            for f in range(HALF):
                act.dma_start(pos[f * FBLK:(f + 1) * FBLK, :],
                              a["positions"].rearrange("o (k n) -> (o k) n", k=FBLK)).then_inc(in_pos, 16)

            for t in range(TT):
                act.wait_ge(x_t_done, 2 * t + 1)
                act.activation(x[:, 0:4, t * P:(t + 1) * P], bank[t % 2][0][:].rearrange("p (k n) -> p k n", k=4),
                               ACT.Copy).then_inc(x_evac[0], 1)
                if 1 <= t <= CHUNKS_BEFORE:
                    copy_ada(t - 1, 0)
                if t == 2:
                    for i in (0, 1):
                        act.wait_ge(set_dve, SET_DVE["reduced", i])
                        act.activation(tabs[i][:], tabs[i][:], ACT.Sin).then_inc(set_act, 1)
            def split_hi(step, side):
                nxt = Step(0, step.half, step.par + 1)
                act.wait_ge(raw_in[1 - step.par][side], (nxt.half) * 48 + 48)
                act.wait_ge(slab_done[side], step.P + 1)
                act.activation(w_hi[side][:], raw[1 - step.par][side][:], ACT.Copy).then_inc(hi_ready[side], 1)

            def inputs(name, k, b, i, xk):
                act.activation(tmp[:, k % 2, :], xk, ACT.Identity, bias=bias[:, i, k:k + 1],
                               scale=gain[:, i, k:k + 1]).then_inc(norm_act, 1)
                act.wait_ge(norm_act, AT_ACT[(name, "u", k) if name[0] == "x" else (*name, "u", k)])
                act.activation(u_hi[b][:, k, :], tmp[:, k % 2, :], ACT.Copy).then_inc(norm_act, 1)

            for side in (0, 1):
                act.wait_ge(raw_in[0][side], 48)
                act.activation(w_hi[side][:], raw[0][side][:], ACT.Copy).then_inc(hi_ready[side], 1)

            def first_inputs(b, tiles):
                act.wait_ge(x_evac[1], TT)
                act.wait_ge(x_evac[0], TT)
                act.wait_ge(fold_step, AT_FOLD["ss", 0])
                for k in tiles:
                    if k >= 2:
                        act.wait_ge(norm_dve, AT_DVE["init", b, "lo", k - 2])
                    inputs(("init", b), k, b, 0, x[:, k, b * T:(b + 1) * T])

            first_inputs(0, range(DT))

            def squares(name, xk, tiles):
                for k in tiles:
                    act.wait_ge(*centered(name, k))
                    if k >= 2:
                        act.wait_ge(norm_pool, AT_POOL[name, "sq", max(k - 2, 1)])
                    act.activation(tmp[:, k % 2, :], xk(k), ACT.Square).then_inc(norm_act, 1)

            def norm_out(s, tiles):
                l, m, b = STAGES[s]
                name = ("x", s)
                g0 = OFF["ln2_g" if m else "ln1_g"]
                b0 = OFF["ln2_b" if m else "ln1_b"]
                if s < 2 * DEPTH + 1 and ("ss", s // NBLK + 1) in AT_FOLD:
                    act.wait_ge(fold_step, AT_FOLD["ss", s // NBLK + 1])
                for k in tiles:
                    xk = x[:, k, b * T:(b + 1) * T]
                    act.wait_ge(norm_dve, AT_DVE[name, "scale", k])
                    if s < LAST - 1:
                        if k >= 2:
                            act.wait_ge(norm_dve, AT_DVE[name, "lo", k - 2])
                        inputs(name, k, b, s // NBLK + 1, xk)
                    act.activation(xk, xk, ACT.Identity, bias=par1[:, l, b0 + k:b0 + k + 1],
                                   scale=par1[:, l, g0 + k:g0 + k + 1]).then_inc(norm_act, 1)

            def conv_norm_out(s, k):
                l, m, b = STAGES[s]
                name = ("c", s)
                g0, b0 = OFF["conv_ln_g"], OFF["conv_ln_b"]
                if k < CT:
                    act.wait_ge(norm_dve, AT_DVE[name, "scale", k])
                    act.activation(conv[:, k, :], conv[:, k, :], ACT.Identity, bias=par1[:, l, b0 + k:b0 + k + 1],
                                   scale=par1[:, l, g0 + k:g0 + k + 1]).then_inc(norm_act, 1)
                    act.wait_ge(norm_act, AT_ACT[name, "z", k])
                    if k >= 2:
                        act.wait_ge(norm_dve, AT_DVE[name, "lo", k - 2])
                    act.activation(tmp[:, k % 2, :], conv[:, k, :], ACT.Tanh, scale=0.5).then_inc(norm_act, 1)
                if k:
                    act.wait_ge(norm_dve, AT_DVE[name, "m", k - 1])
                    act.activation(u_hi[b][:, k - 1, :], tmp[:, (k - 1) % 2, :], ACT.Copy, scale=0.5).then_inc(norm_act, 1)

            def mixer(s, l, b):
                first, mi = FIRST[s], MIXERS.index(s)
                if s == 0:
                    act.wait_ge(tab_out, 32)
                act.wait_ge(hist_ready, 2 * mi + 1)
                for st_ in pairs(act, first, CONV_PAIRS, straight=s == 0):
                    o = lambda t: t.rearrange("p (o n) -> p o n", o=1)
                    act.wait_ge(slab_done[0], st_.P + 1)
                    act.activation(conv[:, bass.ds(st_.m, 1), :], o(bank[st_.par][0][:]), ACT.Tanh,
                                   scale=0.5).then_inc(bank_free[st_.par][0], 1)
                    split_hi(st_, 0)
                    act.wait_ge(slab_done[1], st_.P + 1)
                    act.activation(glu[:, bass.ds(st_.m, 1), HIST:], o(bank[st_.par][1][:]),
                                   ACT.Copy).then_inc(bank_free[st_.par][1], 1)
                    split_hi(st_, 1)
                    if s == 0 and st_.m < 2:
                        copy_ada(CHUNKS_BEFORE + st_.m, 0)
                if s:
                    act.wait_ge(stat_done, AT_STAT[("x", s - 1), "mean"])
                    act.activation(diag[:].rearrange("p a b -> p (a b)"), b7[:], ACT.Copy).then_inc(norm_act, 1)
                for st_ in pairs(act, first + CONV_PAIRS, QKV_PAIRS):
                    for side in (0, 1):
                        j = 2 * st_.m + side
                        act.wait_ge(slab_done[side], st_.P + 1)
                        if j == QT + 1:
                            act.wait_ge(hist_ready, 2 * (mi + 1))
                        dst = q[:, :, j, :] if j < QT else k_raw if j == QT else v_t[:, CHUNK:]
                        act.activation(dst, chunked(bank[st_.par][side][:]) if j < QT else bank[st_.par][side][:], ACT.Copy).then_inc(bank_free[st_.par][side], 1)
                        split_hi(st_, side)
                if s:
                    squares(("x", s - 1), lambda k: x[:, k, (1 - b) * T:(2 - b) * T], range(DT))
                for i in (0, 1):
                    act.wait_ge(v_done, 2 * mi + i + 1)
                    act.activation(v[:, i * NCH // 2:(i + 1) * NCH // 2, :], bank[0][i][:].rearrange("p (n f) -> p n f", f=P),
                                   ACT.Copy).then_inc(att_act, 1)
                for n in range(NCH + 2):
                    if n < NCH:
                        r = n % 2
                        act.wait_ge(att_dve, AT_ADVE[s, "sink", n])
                        for i in range(QT):
                            act.activation(probs[:, r, i, :], sbank[r][:, i, :], ACT.Exp, bias=st[:, r, 1, i:i + 1],
                                           scale=SCALE, accum_out=st[:, r, 3, i:i + 1]).then_inc(att_act, 1)
                        act.activation(st[:, r, 4, :], st[:, r, 2, :], ACT.Exp).then_inc(att_act, 1)
                    if 1 <= n <= NCH:
                        act.wait_ge(probs_t_done, mi * NCH + n)
                        act.activation(probs_t[:, (n - 1) % 2, :], (b6 if n % 2 else b7)[:], ACT.Copy).then_inc(att_act, 1)
                    if n >= 2:
                        act.wait_ge(pv_done, mi * NCH + n - 1)
                        act.activation(u_hi[b][:, CT:DT, (n - 2) * CHUNK:(n - 1) * CHUNK],
                                       bank[0][n % 2][:, 0:QT * CHUNK].rearrange("p (j t) -> p j t", j=QT), ACT.Copy).then_inc(att_act, 1)
                    if n in C_NORM_ACT:
                        if C_NORM_ACT[n] == "squares":
                            squares(("c", s), lambda k: conv[:, k, :], range(CT))
                        else:
                            conv_norm_out(s, C_NORM_ACT[n])
                conv_norm_out(s, CT)
                for st_ in pairs(act, first + CONV_PAIRS + QKV_PAIRS, OUT_PAIRS, straight=True):
                    if s:
                        norm_out(s - 1, both(st_.m))
                    else:
                        act.wait_ge(norm_dve, AT_DVE[("c", s), "lo", CT - 1])
                        first_inputs(1, both(st_.m))
                    split_hi(st_, 0)
                    split_hi(st_, 1)
                    copy_adas(s, "out", st_)

            def mlp(s, l, b):
                first = FIRST[s]
                for g, size in enumerate(GROUP):
                    for st_ in pairs(act, first, size):
                        f = st_.m + START[g]
                        n = f + FT * mlp_no(s)
                        act.wait_ge(slab_done[0], st_.P + 1)
                        act.wait_ge(gate_step, n * GATE + 1)
                        ps = bank[st_.par][0]
                        act.activation(gacc[:], ps[:], ACT.Identity, bias=par1[:, l, bass.ds(f + OFF["ffn_conv_b"], 1)],
                                       scale=par3[:, l, bass.ds(f + 2 * FT, 1)]).then_inc(gate_act, 1)
                        act.activation(gate[:, FK - 1:], ps[:], ACT.Copy).then_inc(bank_free[st_.par][0], 1)
                        split_hi(st_, 0)
                        act.wait_ge(gate_step, n * GATE + 5)
                        act.activation(tanh_c[:], gacc[:], ACT.Tanh, scale=0.5).then_inc(gate_act, 1)
                        split_hi(st_, 1)
                        act.wait_ge(bank_free[st_.par][1], st_.half + 2)
                        act.activation(h_hi[:, bass.ds(st_.m, 1), :], gacc[:].rearrange("p (o n) -> p o n", o=1), ACT.Copy).then_inc(gate_act, 1)
                    first += size
                    last = s == LAST and g == LAST_G
                    for st_ in pairs(act, first, DOWN_PAIRS, straight=g < 2 or last):
                        if g == 0:
                            squares(("x", s - 1), lambda k: x[:, k, (1 - b) * T:(2 - b) * T], both(st_.m))
                        elif g == 1:
                            norm_out(s - 1, both(st_.m))
                        for side in (0, 1):
                            if not last or st_.m < DOWN_PAIRS - 1:
                                split_hi(st_, side)
                        copy_adas(s, g, st_)
                    first += DOWN_PAIRS

            for s, (l, m, b) in enumerate(STAGES):
                (mlp if m else mixer)(s, l, b)
            squares(("x", LAST), lambda k: x[:, k, T:], range(DT))
            norm_out(LAST, range(DT))
            for t in range(TT):
                act.wait_ge(y_t_done, 2 * t + 1)
                if t >= 2:
                    act.wait_ge(y_out[t % 2], 16 * (t // 2))
                act.activation(stage_out[t % 2][:, 0:D // 2], bank[t % 2][0][:], ACT.Copy).then_inc(y_evac[0], 1)

        @block.vector
        def _(dve):
            setup = [0]

            def step(ins):
                ins.then_inc(set_dve, 1)
                setup[0] += 1
                dve.wait_ge(set_dve, setup[0])

            def done(name):
                assert SET_DVE[name] == setup[0], (name, setup[0])

            dve.wait_ge(set_pe, 1)
            step(dve.tensor_copy(par1[:], b6[:, 0:2 * P].rearrange("p (l n) -> p l n", l=DEPTH)[:, :, 0:N1]))
            step(dve.tensor_scalar(par2[:], b6[:, 2 * P:4 * P].rearrange("p (l n) -> p l n", l=DEPTH)[:, :, 0:N2], 0.5, None, ALU.mult))
            done(("par", 0))
            dve.wait_ge(set_pe, 2)
            step(dve.tensor_copy(par3[:], b7[:, 0:2 * P].rearrange("p (l n) -> p l n", l=DEPTH)[:, :, 0:N3]))
            step(dve.tensor_copy(ccol[:], b7[:, 2 * P:2 * P + DT]))
            done(("par", 1))
            dve.wait_ge(in_sinks, 16 * 2 * DEPTH)
            step(dve.tensor_scalar(nsink[:], nsink[:], -1.0, None, ALU.mult))

            def evac_x(t):
                dve.wait_ge(x_t_done, 2 * t + 2)
                dve.tensor_copy(x[:, 4:8, t * P:(t + 1) * P],
                                bank[t % 2][1][:].rearrange("p (k n) -> p k n", k=4)).then_inc(x_evac[1], 1)

            def add_ada(base, more, half):
                dve.wait_ge(in_ada[half], more * 16 + 16 * (base + 1))
                for k in range(half * DT // 2, (half + 1) * DT // 2):
                    w = ada[half][:, k % (DT // 2), :]
                    if k == 0:
                        if not isinstance(more, int) or base + more:
                            dve.wait_ge(ada_sum, more + base)
                        dve.tensor_scalar(ada_acc[:], w, ccol[:, 0:1], None, ALU.mult).then_inc(ada_add, 1)
                    else:
                        dve.wait_ge(ada_add, more * DT + base * DT + k)
                        dve.scalar_tensor_tensor(out=ada_acc[:], in0=w, scalar=ccol[:, k:k + 1], in1=ada_acc[:],
                                                 op0=ALU.mult, op1=ALU.add).then_inc(ada_add, 1)

            def add_adas(s, phase, st_):
                for base, more, halves in ada_steps(s, phase, st_):
                    for half in halves:
                        add_ada(base, more, half)

            folds = [0]

            def fold(what, i):
                def fold_one(ins):
                    ins.then_inc(fold_step, 1)
                    folds[0] += 1
                    dve.wait_ge(fold_step, folds[0])

                l, m = i // 2, i % 2
                o = OFF["b_ada_ffn" if m else "b_ada_mix"]
                dve.wait_ge(ada_copied, NCHUNK * i + (4 if what == "ss" else 6))
                if what == "gate":
                    g = mod[:, l, m, 2 * DT:]
                    fold_one(dve.tensor_tensor(g, g, par1[:, l, o + 2 * DT:o + 3 * DT], ALU.add))
                    fold_one(dve.tensor_scalar(g, g, 1.0, INV_ALPHA, ALU.add, ALU.mult))
                else:
                    shift, scale = mod[:, l, m, 0:DT], mod[:, l, m, DT:2 * DT]
                    both = mod[:, l, m, 0:2 * DT]
                    fold_one(dve.tensor_tensor(both, both, par1[:, l, o:o + 2 * DT], ALU.add))
                    if i == 0:
                        fold_one(dve.tensor_scalar(gain[:, 0, :], scale, 1.0, None, ALU.add))
                        fold_one(dve.tensor_copy(bias[:, 0, :], shift))
                    else:
                        pl, pm = (i - 1) // 2, (i - 1) % 2
                        g0, b0 = (OFF["ln2_g"], OFF["ln2_b"]) if pm else (OFF["ln1_g"], OFF["ln1_b"])
                        fold_one(dve.tensor_scalar(scale, scale, 1.0, None, ALU.add))
                        fold_one(dve.tensor_tensor(gain[:, i, :], par1[:, pl, g0:g0 + DT], scale, ALU.mult))
                        fold_one(dve.tensor_tensor(bias[:, i, :], par1[:, pl, b0:b0 + DT], scale, ALU.mult))
                        fold_one(dve.tensor_tensor(bias[:, i, :], bias[:, i, :], shift, ALU.add))
                assert AT_FOLD[what, i] == folds[0]

            def angles():
                dve.wait_ge(in_pos, 16 * HALF)
                step(dve.tensor_copy(ang[:], pos[:]))
                step(dve.tensor_scalar(ang[:], ang[:], inv_freq, None, ALU.mult))
                for i, (quarter, shift) in enumerate(((0.25, np.pi / 2), (0.0, 0.0))):
                    step(dve.tensor_scalar(turns[:], ang[:], float(np.float32(0.5 / np.pi)), quarter, ALU.mult, ALU.add))
                    step(dve.tensor_scalar(turns[:], turns[:], MAGIC, None, ALU.add))
                    step(dve.tensor_scalar(turns[:], turns[:], -MAGIC, None, ALU.add))
                    for n, part in enumerate(TWO_PI):
                        step(dve.scalar_tensor_tensor(out=tabs[i][:], in0=turns[:], scalar=-part, in1=(tabs[i] if n else ang)[:],
                                                      op0=ALU.mult, op1=ALU.add))
                    step(dve.tensor_scalar(tabs[i][:], tabs[i][:], shift, PI_DOWN, ALU.add, ALU.min))
                    step(dve.tensor_scalar(tabs[i][:], tabs[i][:], -PI_DOWN, None, ALU.max))
                    done(("reduced", i))

            for t in range(TT):
                evac_x(t)
                if t < CHUNKS_BEFORE:
                    for half in (0, 1):
                        add_ada(t, 0, half)
                if t == 0:
                    angles()
            for r in (0, 1):
                for side in (0, 1):
                    dve.wait_ge(x_evac[side], TT)
                    dve.memset(small[:, 0, 0, 2 * r + side:2 * r + side + 1], 0.0).then_inc(bank_free[r][side], 1)
            dve.memset(ghist[:], 0.0).then_inc(gate_step, 1)

            def split_lo(step_, side):
                dve.wait_ge(hi_ready[side], step_.P + 2)
                dve.tensor_tensor(w_lo[side][:], raw[1 - step_.par][side][:], w_hi[side][:].bitcast(F32),
                                  ALU.subtract).then_inc(lo_ready[side], 1)

            def input_lo(b, k, hi_at):
                dve.wait_ge(norm_act, hi_at)
                dve.tensor_tensor(u_lo[b][:, k, :], tmp[:, k % 2, :], u_hi[b][:, k, :].bitcast(F32),
                                  ALU.subtract).then_inc(norm_dve, 1)

            for what in FOLD_AT[0]:
                fold(*what)
            for side in (0, 1):
                dve.wait_ge(hi_ready[side], 1)
                dve.tensor_tensor(w_lo[side][:], raw[0][side][:],
                                  w_hi[side][:].bitcast(F32), ALU.subtract).then_inc(lo_ready[side], 1)
            for k in range(DT):
                input_lo(0, k, AT_ACT["init", 0, "hi", k])

            def center(name, xk, tiles):
                dve.wait_ge(stat_done, AT_STAT[name, "mean"])
                for k in tiles:
                    dve.tensor_tensor(xk(k), xk(k), stat_bank(name, "mean")[:], ALU.subtract).then_inc(norm_dve, 1)

            def small_step(name, n, ins):
                ins.then_inc(norm_dve, 1)
                dve.wait_ge(norm_dve, AT_DVE[name, "small", n])

            def read_var(name):
                eps = EPS / ALPHA2 if name[0] == "x" else EPS
                dve.wait_ge(stat_done, AT_STAT[name, "var"])
                small_step(name, 0, dve.tensor_scalar(small[:, name[0] == "c", 0, :], stat_bank(name, "var")[:, 0:T // P],
                                                      eps, None, ALU.add))

            def rsqrt(name):
                var, y, t = (small[:, name[0] == "c", i, :] for i in range(3))
                small_step(name, 1, dve.tensor_scalar(t.bitcast(I32), var.bitcast(I32), 1, None, ALU.logical_shift_right))
                small_step(name, 2, dve.tensor_scalar(y.bitcast(I32), t.bitcast(I32), -1.0, 1597463007.0, ALU.mult, ALU.add))
                for i in range(3):
                    small_step(name, 3 * i + 3, dve.tensor_tensor(t, y, y, ALU.mult))
                    small_step(name, 3 * i + 4, dve.scalar_tensor_tensor(out=t, in0=t, scalar=-0.5, in1=var, op0=ALU.mult, op1=ALU.mult))
                    small_step(name, 3 * i + 5, dve.scalar_tensor_tensor(out=y, in0=t, scalar=1.5, in1=y, op0=ALU.add, op1=ALU.mult))
                for i in range(T // P):
                    dve.tensor_scalar(diagonals(name)[:, i, :], ident, y[:, i:i + 1], None, ALU.mult).then_inc(norm_dve, 1)

            def rescale(name, xk, tiles):
                dve.wait_ge(stat_done, AT_STAT[name, "rstd"])
                for k in tiles:
                    dve.tensor_tensor(xk(k), xk(k), stat_bank(name, "rstd")[:], ALU.mult).then_inc(norm_dve, 1)

            def inputs_lo(s, tiles):
                if s < LAST - 1:
                    for k in tiles:
                        input_lo(STAGES[s][2], k, AT_ACT[("x", s), "hi", k])

            def residual(l, m, b, st_):
                for side in (0, 1):
                    k = st_.m * 2 + side
                    dve.wait_ge(slab_done[side], st_.P + 1)
                    xk = x[:, bass.ds(k, 1), b * T:(b + 1) * T]
                    dve.scalar_tensor_tensor(out=xk, in0=bank[st_.par][side][:].rearrange("p (o n) -> p o n", o=1),
                                             scalar=mod[:, l, m, bass.ds(k + 2 * DT, 1)],
                                             in1=xk, op0=ALU.mult, op1=ALU.add).then_inc(bank_free[st_.par][side], 1)

            def conv_norm(s, part):
                name, ck = ("c", s), lambda k: conv[:, k, :]
                b = STAGES[s][2]
                if part == "center":
                    center(name, ck, range(CT))
                elif part == "small":
                    read_var(name)
                    rsqrt(name)
                elif part == "x small":
                    if s:
                        rsqrt(("x", s - 1))
                elif part == "scale":
                    rescale(name, ck, range(CT))
                else:
                    k = part
                    if k < CT:
                        dve.wait_ge(norm_act, AT_ACT[name, "th", k])
                        t = tmp[:, k % 2, :]
                        dve.scalar_tensor_tensor(out=t, in0=t, scalar=1.0, in1=conv[:, k, :], op0=ALU.add,
                                                 op1=ALU.mult).then_inc(norm_dve, 1)
                    if k:
                        dve.wait_ge(norm_act, AT_ACT[name, "hi", k - 1])
                        dve.scalar_tensor_tensor(out=u_lo[b][:, k - 1, :], in0=tmp[:, (k - 1) % 2, :], scalar=0.5,
                                                 in1=u_hi[b][:, k - 1, :].bitcast(F32), op0=ALU.mult,
                                                 op1=ALU.subtract).then_inc(norm_dve, 1)

            def mixer(s, l, b):
                first, mi = FIRST[s], MIXERS.index(s)
                other = lambda k: x[:, k, (1 - b) * T:(2 - b) * T]
                if s == 0:
                    for n in (CHUNKS_BEFORE, CHUNKS_BEFORE + 1):
                        for half in (0, 1):
                            add_ada(n, 0, half)
                dve.wait_ge(hist_ready, 2 * mi + 1)
                for st_ in pairs(dve, first, CONV_PAIRS):
                    j = st_.m
                    tap0 = (j + CT * mi) * TAPS + 1
                    dve.wait_ge(bank_free[st_.par][0], st_.half + 2)
                    dve.wait_ge(bank_free[st_.par][1], st_.half + 2)
                    value = glu[:, bass.ds(j, 1), HIST:]
                    dve.scalar_tensor_tensor(out=value, in0=conv[:, bass.ds(j, 1), :], scalar=1.0, in1=value,
                                             op0=ALU.add, op1=ALU.mult).then_inc(conv_step, 1)
                    dve.wait_ge(conv_step, tap0)
                    total = conv[:, bass.ds(j, 1), :]
                    even, odd = (sbank[i][:].rearrange("p i (o n) -> p o (i n)", o=1) for i in (0, 1))
                    for k in range(CONV_K):
                        src = glu[:, bass.ds(j, 1), k:k + T]
                        w = par2[:, l, bass.ds(j + k * CT, 1)]
                        if k == 0:
                            ins = dve.tensor_scalar(even, src, w, par1[:, l, bass.ds(j + OFF["conv_b"], 1)], ALU.mult, ALU.add)
                        elif k == 1:
                            ins = dve.tensor_scalar(odd, src, w, None, ALU.mult)
                        else:
                            dve.wait_ge(conv_step, tap0 + k - 1)
                            acc = odd if k % 2 else even
                            out = total if k == CONV_K - 2 else acc
                            ins = dve.scalar_tensor_tensor(out=out, in0=src, scalar=w, in1=acc, op0=ALU.mult, op1=ALU.add)
                        ins.then_inc(conv_step, 1)
                    dve.wait_ge(conv_step, tap0 + CONV_K)
                    dve.tensor_tensor(total, total, even, ALU.add).then_inc(conv_step, 1)
                if s:
                    read_var(("x", s - 1))
                dve.wait_ge(cs_in, CS_IN * (mi + 1))
                sin = cs[:, 1, :]
                for j in range(QT + 1):
                    shape = chunked if j < QT else lambda t: t
                    src = q[:, :, j, :] if j < QT else k_raw
                    part = shape(rot_part)
                    if j:
                        dve.wait_ge(att_dve, AT_ADVE[s, "rope", j - 1])
                    dve.wait_ge(rot_done, (QT + 1) * mi + j + 1)
                    dve.tensor_tensor(part, shape(rot_bank(j)), shape(sin), ALU.mult).then_inc(att_dve, 1)
                    dve.wait_ge(att_dve, AT_ADVE[s, "sin", j])
                    dve.wait_ge(rope_cos, (QT + 1) * mi + j + 1)
                    if j < QT:
                        dve.tensor_tensor(src, src, part, ALU.add).then_inc(att_dve, 1)
                    else:
                        dve.wait_ge(hist_ready, 2 * (mi + 1))
                        for g in (0, 1):
                            h = slice(g * HEAD, (g + 1) * HEAD)
                            dve.tensor_tensor(kz[h, g, CHUNK:], k_raw[h, :], rot_part[h, :], ALU.add).then_inc(att_dve, 1)
                for n in range(NCH + 3):
                    if n < NCH:
                        r = n % 2
                        dve.wait_ge(scores_done, mi * NCH + n + 1)
                        if n == 0 and b == 0:
                            dve.memset(sbank[r][:, :, 0:CHUNK], NEG).then_inc(att_dve, 1)
                            dve.wait_ge(att_dve, AT_ADVE[s, "mask", n])
                        dve.tensor_reduce(st[:, r, 0, :], sbank[r][:], AX.X, ALU.max).then_inc(att_dve, 1)
                        dve.wait_ge(att_dve, AT_ADVE[s, "max", n])
                        dve.scalar_tensor_tensor(out=st[:, r, 1, :], in0=st[:, r, 0, :], scalar=-SCALE, in1=nsink[:, l, :],
                                                 op0=ALU.mult, op1=ALU.min).then_inc(att_dve, 1)
                        dve.wait_ge(att_dve, AT_ADVE[s, "negmax", n])
                        dve.tensor_tensor(st[:, r, 2, :], st[:, r, 1, :], nsink[:, l, :], ALU.subtract).then_inc(att_dve, 1)
                    if 1 <= n <= NCH:
                        r = (n - 1) % 2
                        dve.wait_ge(att_act, AT_AACT[s, "esink", n - 1])
                        dve.tensor_tensor(st[:, r, 5, :], st[:, r, 3, :], st[:, r, 4, :], ALU.add).then_inc(att_dve, 1)
                        dve.wait_ge(att_dve, AT_ADVE[s, "den", n - 1])
                        dve.reciprocal(st[:, r, 6, :], st[:, r, 5, :]).then_inc(att_dve, 1)
                        dve.wait_ge(att_dve, AT_ADVE[s, "inv", n - 1])
                        dve.tensor_tensor(probs[:, r, :, :], probs[:, r, :, :],
                                          st[:, r, 6, :].rearrange("p (i o) -> p i o", o=1).to_broadcast([P, QT, P]),
                                          ALU.mult).then_inc(att_dve, 1)
                    if n >= 3:
                        dve.wait_ge(att_act, AT_AACT[s, "hi", n - 3])
                        c = slice((n - 3) * CHUNK, (n - 2) * CHUNK)
                        dve.tensor_tensor(u_lo[b][:, CT:DT, c], bank[0][(n - 3) % 2][:, 0:QT * CHUNK].rearrange("p (j t) -> p j t", j=QT),
                                          u_hi[b][:, CT:DT, c].bitcast(F32), ALU.subtract).then_inc(att_dve, 1)
                    if n in C_NORM_DVE:
                        conv_norm(s, C_NORM_DVE[n])
                conv_norm(s, CT)
                if s == 0:
                    fold("gate", 0)
                wait_x(dve, s)
                for st_ in pairs(dve, first + CONV_PAIRS + QKV_PAIRS, OUT_PAIRS, straight=True):
                    if s:
                        rescale(("x", s - 1), other, both(st_.m))
                        inputs_lo(s - 1, both(st_.m))
                    else:
                        for k in both(st_.m):
                            input_lo(1, k, AT_ACT["init", 1, "hi", k])
                    add_adas(s, "out", st_)
                    residual(l, 0, b, st_)

            def wait_x(eng, s):
                if s >= 2:
                    eng.wait_ge(norm_act, AT_ACT[("x", s - 2), "x", DT - 1])

            def mlp(s, l, b):
                first = FIRST[s]
                other = lambda k: x[:, k, (1 - b) * T:(2 - b) * T]
                if b == 0 and l:
                    dve.wait_ge(gate_step, hidden(s, 0))
                    dve.memset(ghist[:], 0.0).then_inc(ghist_clear, 1)
                    dve.wait_ge(ghist_clear, l)
                for g, size in enumerate(GROUP):
                    for st_ in pairs(dve, first, size):
                        f = st_.m + START[g]
                        n = f + FT * mlp_no(s)
                        at = n * GATE + 1
                        hist = ghist[:, bass.ds(f, 1), :].rearrange("p o n -> p (o n)")
                        dve.wait_ge(slab_done[0], st_.P + 1)
                        dve.tensor_copy(gate[:, 0:FK - 1], hist).then_inc(gate_step, 1)
                        dve.wait_ge(bank_free[st_.par][0], st_.half + 2)
                        dve.wait_ge(gate_step, at + 1)
                        dve.scalar_tensor_tensor(out=gacc[:], in0=gate[:, 1:1 + T], scalar=par3[:, l, bass.ds(f + FT, 1)],
                                                 in1=gacc[:], op0=ALU.mult, op1=ALU.add).then_inc(gate_step, 1)
                        dve.tensor_copy(hist, gate[:, T:T + FK - 1]).then_inc(gate_step, 1)
                        dve.wait_ge(gate_step, at + 2)
                        dve.scalar_tensor_tensor(out=gacc[:], in0=gate[:, 0:T], scalar=par3[:, l, bass.ds(f, 1)],
                                                 in1=gacc[:], op0=ALU.mult, op1=ALU.add).then_inc(gate_step, 1)
                        split_lo(st_, 0)
                        dve.wait_ge(gate_act, n * 3 + 2)
                        dve.scalar_tensor_tensor(out=tanh_c[:], in0=tanh_c[:], scalar=1.0, in1=gacc[:],
                                                 op0=ALU.add, op1=ALU.mult).then_inc(gate_step, 1)
                        dve.wait_ge(gate_step, at + 5)
                        dve.wait_ge(slab_done[1], st_.P + 1)
                        dve.scalar_tensor_tensor(out=gacc[:], in0=bank[st_.par][1][:], scalar=0.5, in1=tanh_c[:],
                                                 op0=ALU.mult, op1=ALU.mult).then_inc(bank_free[st_.par][1], 1)
                        dve.wait_ge(gate_act, n * 3 + 3)
                        o = lambda t: t.rearrange("p (o n) -> p o n", o=1)
                        dve.tensor_tensor(h_lo[:, bass.ds(st_.m, 1), :], o(gacc[:]),
                                          h_hi[:, bass.ds(st_.m, 1), :].bitcast(F32), ALU.subtract).then_inc(gate_step, 1)
                    first += size
                    if g == 0:
                        wait_x(dve, s)
                    last = s == LAST and g == LAST_G
                    for st_ in pairs(dve, first, DOWN_PAIRS, straight=g < 2 or last):
                        if g == 0:
                            center(("x", s - 1), other, both(st_.m))
                        elif g == 1:
                            rescale(("x", s - 1), other, both(st_.m))
                            inputs_lo(s - 1, both(st_.m))
                        add_adas(s, g, st_)
                        if not last or st_.m < DOWN_PAIRS - 1:
                            split_lo(st_, 0)
                        residual(l, 1, b, st_)
                    first += DOWN_PAIRS
                    if g == 0:
                        read_var(("x", s - 1))
                        rsqrt(("x", s - 1))

            for s, (l, m, b) in enumerate(STAGES):
                if s:
                    for what in FOLD_AT.get(s, []):
                        fold(*what)
                (mlp if m else mixer)(s, l, b)
            lastx = lambda k: x[:, k, T:]
            center(("x", LAST), lastx, range(DT))
            read_var(("x", LAST))
            rsqrt(("x", LAST))
            rescale(("x", LAST), lastx, range(DT))
            for t in range(TT):
                dve.wait_ge(y_t_done, 2 * t + 2)
                if t >= 2:
                    dve.wait_ge(y_out[t % 2], 16 * (t // 2))
                dve.tensor_copy(stage_out[t % 2][:, D // 2:], bank[t % 2][1][:]).then_inc(y_evac[1], 1)

        @block.gpsimd
        def _(pool):
            def split_lo(step_, side):
                pool.wait_ge(hi_ready[side], step_.P + 2)
                pool.tensor_tensor(w_lo[side][:], raw[1 - step_.par][side][:], w_hi[side][:].bitcast(F32),
                                   ALU.subtract).then_inc(lo_ready[side], 1)

            def center(name, tiles, b):
                pool.wait_ge(norm_act, AT_ACT[name, "copied"])
                mean = diag[:].rearrange("p a b -> p (a b)")
                for k in tiles:
                    xk = x[:, k, b * T:(b + 1) * T]
                    pool.tensor_tensor(xk, xk, mean, ALU.subtract).then_inc(norm_pool, 1)

            def sum_squares(name, tiles):
                pool.wait_ge(stat_done, AT_STAT[name, "mean"])
                for k in tiles:
                    if k == 0:
                        continue
                    pool.wait_ge(norm_act, AT_ACT[name, "sq", k])
                    if k > 1:
                        pool.wait_ge(norm_pool, AT_POOL[name, "sq", k - 1])
                    pool.tensor_tensor(ssum[:], tmp[:, k % 2, :], (tmp[:, 0, :] if k == 1 else ssum[:]), ALU.add).then_inc(norm_pool, 1)

            def clear_sum(s):
                name = ("c", s) if s in MIXERS else ("x", s - 1)
                pool.wait_ge(stat_done, AT_STAT[name, "var"])
                pool.memset(ssum[:], 0.0).then_inc(norm_pool, 1)

            def add_residual(s, st_, side):
                k = st_.m * 2 + side
                b = STAGES[s][2]
                pool.wait_ge(norm_pool, k + AT_POOL["sum", s, -1])
                pool.wait_ge(bank_free[st_.par][side], st_.half + 2)
                pool.tensor_tensor(ssum[:].rearrange("p (o n) -> p o n", o=1), ssum[:].rearrange("p (o n) -> p o n", o=1),
                                   x[:, bass.ds(k, 1), b * T:(b + 1) * T], ALU.add).then_inc(norm_pool, 1)

            def mixer(s, l, b):
                first, mi = FIRST[s], MIXERS.index(s)
                if b == 0:
                    if s == 0:
                        pool.wait_ge(fold_step, AT_FOLD["ss", 0])
                        pool.wait_ge(tab_out, 32)
                    else:
                        for side in (0, 1):
                            pool.wait_ge(slab_done[side], first)
                    pool.memset(glu[:, :, 0:HIST], 0.0).then_inc(hist_ready, 1)
                    pool.memset(v_t[:, 0:CHUNK], 0.0)
                    pool.memset(kz[:], 0.0).then_inc(hist_ready, 1)
                else:
                    pool.wait_ge(conv_step, CT * TAPS * mi)
                    pool.tensor_copy(glu[:, :, 0:HIST], glu[:, :, T:T + HIST]).then_inc(hist_ready, 1)
                    pool.tensor_copy(v_t[:, 0:CHUNK], v_t[:, T:T + CHUNK])
                    pool.tensor_copy(kz[:, :, 0:CHUNK], kz[:, :, T:T + CHUNK]).then_inc(hist_ready, 1)
                for st_ in pairs(pool, first, CONV_PAIRS):
                    for side in (0, 1):
                        split_lo(st_, side)
                for st_ in pairs(pool, first + CONV_PAIRS, QKV_PAIRS, straight=True):
                    for side in (0, 1):
                        split_lo(st_, side)
                    if s:
                        center(("x", s - 1), range(3 * st_.m, min(3 * st_.m + 3, DT)), 1 - b)
                if s:
                    sum_squares(("x", s - 1), range(DT))
                pool.wait_ge(cs_in, CS_IN * (mi + 1))
                for j in range(QT + 1):
                    pool.wait_ge(rot_done, (QT + 1) * mi + j + 1)
                    src, cos = (q[:, :, j, :], chunked(cs[:, 0, :])) if j < QT else (k_raw, cs[:, 0, :])
                    pool.tensor_tensor(src, src, cos, ALU.mult).then_inc(rope_cos, 1)
                if s:
                    pool.wait_ge(stat_done, AT_STAT[("x", s - 1), "var"])
                for k in range(1, CT):
                    pool.wait_ge(conv_step, CT * TAPS * mi + TAPS * (k + 1))
                    if k > 1:
                        pool.wait_ge(norm_pool, AT_POOL[("c", s), "pre", k - 1])
                    pool.tensor_tensor(ssum[:], conv[:, k, :], conv[:, 0, :] if k == 1 else ssum[:], ALU.add).then_inc(norm_pool, 1)
                sum_squares(("c", s), range(CT))
                clear_sum(s)
                for st_ in pairs(pool, first + CONV_PAIRS + QKV_PAIRS, OUT_PAIRS):
                    for side in (0, 1):
                        split_lo(st_, side)
                    for side in (0, 1):
                        add_residual(s, st_, side)

            def mlp(s, l, b):
                first = FIRST[s]
                for g, size in enumerate(GROUP):
                    for st_ in pairs(pool, first, size):
                        split_lo(st_, 1)
                    first += size
                    if g == LAST_G:
                        clear_sum(s)
                    last = s == LAST and g == LAST_G
                    for st_ in pairs(pool, first, DOWN_PAIRS, straight=g == 0 or last):
                        if g == 0:
                            sum_squares(("x", s - 1), both(st_.m))
                        if not last or st_.m < DOWN_PAIRS - 1:
                            split_lo(st_, 1)
                        if g == LAST_G:
                            for side in (0, 1):
                                add_residual(s, st_, side)
                    first += DOWN_PAIRS

            for s, (l, m, b) in enumerate(STAGES):
                (mlp if m else mixer)(s, l, b)
            sum_squares(("x", LAST), range(DT))


def mlp_no(s):
    return sum(m for _, m, _ in STAGES[:s])


def hidden(s, f):
    return 1 + GATE * (f + FT * mlp_no(s))


def need_u(s, k):
    if s < NBLK:
        return AT_DVE["init", s, "lo", k]
    return AT_DVE[("x", s - 2), "lo", k]


CS_IN = 16 * 2 * 3 * (P // HEAD)
IN_CONST = 2 + len(ROWS1) + 2 * DEPTH
MAGIC = 12582912.0
PI_DOWN = float(np.nextafter(np.float32(np.pi), np.float32(0.0)))


def two_pi_parts():
    rest, parts = 2 * np.pi, []
    for _ in range(3):
        e = 2.0 ** (np.floor(np.log2(rest)) - 7)
        parts.append(float(np.floor(rest / e) * e))
        rest -= parts[-1]
    return parts + [float(np.float32(rest))]


TWO_PI = two_pi_parts()
SET_DVE = {("par", 0): 2, ("par", 1): 4}
for _i in (0, 1):
    SET_DVE["reduced", _i] = 4 + 1 + 2 + (_i + 1) * (3 + len(TWO_PI) + 2)
SET_ACT = {("table", 0): 1, ("table", 1): 2}


def constants():
    ident = np.eye(P, dtype=np.float32)
    rot = np.zeros((P, P), np.float32)
    freq = np.float32(THETA ** (-2.0 * (np.arange(P)[:, None] // FBLK) / ROT))
    for g in range(P // HEAD):
        for j in range(HALF):
            lo, hi = g * HEAD + j, g * HEAD + HALF + j
            rot[hi, lo] = -1.0
            rot[lo, hi] = 1.0
    ones = np.ones((P, P), np.float32)
    return np.concatenate([ident, rot, ones * np.float32(1.0 / D), ones * np.float32(1.0 / CONV_CH), ones, freq], axis=1)


def plain():
    return np.stack([np.full((HEAD - ROT, T), v, np.float32) for v in (1.0, 0.0)])


_INS = ["x", "c", "positions", "w_ada_mix", "b_ada_mix", "w_in", "conv_w", "conv_b", "conv_ln_g", "conv_ln_b",
        "sinks", "w_out", "ln1_g", "ln1_b", "w_ada_ffn", "b_ada_ffn", "w_up", "ffn_conv_w", "ffn_conv_b",
        "w_down", "ln2_g", "ln2_b"]


def kernel(**inputs):
    import concourse.bacc as _bacc
    from concourse.bass_utils import run_bass_kernel_spmd as _run

    nc = _bacc.Bacc("TRN2", target_bir_lowering=False, num_devices=1)
    arrays, args = {}, {}
    made = {"consts": constants(), "plain": plain()}
    for name in _INS + list(made):
        arr = made[name] if name in made else np.ascontiguousarray(inputs[name])
        arrays[f"in_{name}_dram"] = arr
        args[name] = nc.dram_tensor(f"in_{name}_dram", arr.shape, mybir.dt.from_np(arr.dtype), kind="ExternalInput").ap()
    args["out"] = nc.dram_tensor("out_dram", (1, SEQ, D), F32, kind="ExternalOutput").ap()
    build(nc, args)
    r = _run(nc, [arrays], core_ids=[0])
    return r.results[0]["out_dram"]
```

```python
from contextlib import ExitStack

import numpy as np

import concourse.bass as bass
from concourse import mybir

ALU = mybir.AluOpType
ACT = mybir.ActivationFunctionType
AX = mybir.AxisListType
F32 = mybir.dt.float32
F32R = mybir.dt.float32r
I32 = mybir.dt.int32

P = 128
DEPTH = 2
D = 1024
SEQ = 1024
DT = D // P
NBLK = 2
T = SEQ // NBLK
CONV_CH = 512
CT = CONV_CH // P
CONV_K = 31
HIST = CONV_K - 1
HEAD = 64
HQ = 8
QT = 4
CHUNK = 64
NCH = T // CHUNK
Q0 = 2 * CONV_CH
K0 = Q0 + HQ * HEAD
F = 2816
FT = F // P
GROUP = [6, 5, 6, 5]
START = [sum(GROUP[:g]) for g in range(len(GROUP))]
LAST_G = len(GROUP) - 1
FK = 3
ROT = HEAD // 4
HALF = ROT // 2
THETA = 500000.0
FBLK = P // HALF
EPS = 1e-5
ALPHA2 = (2.0 * DEPTH) ** 0.5
INV_ALPHA = (2.0 * DEPTH) ** -0.25
SCALE = HEAD ** -0.5
NEG = -1e30

CONV_PAIRS, QKV_PAIRS, OUT_PAIRS, DOWN_PAIRS = CT, 3, DT // 2, DT // 2
MIX_PAIRS = CONV_PAIRS + QKV_PAIRS + OUT_PAIRS
MLP_PAIRS = FT + len(GROUP) * DOWN_PAIRS
STAGES = [(l, m, b) for l in range(DEPTH) for m in (0, 1) for b in range(NBLK)]
FIRST = []
_n = 0
for _l, _m, _b in STAGES:
    FIRST.append(_n)
    _n += MLP_PAIRS if _m else MIX_PAIRS
LAST = len(STAGES) - 1

ROWS1 = [("ln1_g", DT), ("ln1_b", DT), ("ln2_g", DT), ("ln2_b", DT), ("conv_b", CT), ("conv_ln_g", CT),
         ("conv_ln_b", CT), ("ffn_conv_b", FT), ("b_ada_mix", 3 * DT), ("b_ada_ffn", 3 * DT)]
N1 = sum(n for _, n in ROWS1)
N2 = CONV_K * CT
N3 = FK * FT
OFF = {}
_n = 0
for _name, _c in ROWS1:
    OFF[_name] = _n
    _n += _c


def chunked(t):
    return t.rearrange("p (n c) -> p n c", c=CHUNK)


class Step:

    def __init__(self, first, i, u):
        self.P = i * 2 + (first + u)
        self.half = i + (first + u) // 2
        self.par = (first + u) % 2
        self.m = i * 2 + u
        self.trip, self.u = (u // 2, u % 2) if isinstance(i, int) else (i, u)


def pairs(eng, first, n, straight=False):
    trips = 0 if straight or n < 4 else n // 2
    if trips:
        with eng.Fori(0, trips) as i:
            for u in (0, 1):
                yield Step(first, i, u)
    for m in range(2 * trips, n):
        yield Step(first, 0, m)


def number(names):
    at = {}
    for n, name in enumerate(names):
        assert name not in at
        at[name] = n + 1
    return at


SMALL = 12
PARTS = ("mean", "var", "read", "small", "rstd", "out")


def both(m):
    return (2 * m, 2 * m + 1)


def sq_tiles(m):
    return range(*((0, 2), (2, 5), (5, DT))[m])


def out_tiles(name, m):
    return range(max(3 * m - 3, 0), min(3 * m, DT)) if under_mixer(name) else both(m)


def under_mixer(name):
    return name[0] == "x" and name[1] < LAST and not STAGES[name[1] + 1][1]




def norm_events():
    stat, dve, act, pool = [], [], [], []

    def init(b):
        for k in range(DT):
            act.extend([("init", b, "u", k), ("init", b, "hi", k)])
            dve.append(("init", b, "lo", k))

    init(0)
    for s, (l, m, b) in enumerate(STAGES):
        x_norm = norm_parts(("x", s - 1), DT) if s else None
        c_norm = norm_parts(("c", s), CT) if not m else None
        if x_norm and c_norm:
            order = [(x_norm, "mean")] + [(c_norm, part) for part in PARTS] + [(x_norm, part) for part in PARTS[1:]]
        else:
            order = [(x_norm or c_norm, part) for part in PARTS]
        for norm, part in order:
            for events, new in zip((stat, dve, act, pool), norm[part]):
                events += new
        if s == 0:
            init(1)
        pool += [("sum", s, k) for k in range(-1, DT)]
    for part in PARTS:
        for events, new in zip((stat, dve, act, pool), norm_parts(("x", LAST), DT)[part]):
            events += new
    return number(stat), number(dve), number(act), number(pool)


def norm_parts(name, n):
    dve_out, act_out = [], []
    if name[0] == "c":
        for k in range(n + 1):
            if k < n:
                act_out += [(name, "z", k), (name, "th", k)]
                dve_out += [(name, "m", k)]
            if k:
                act_out += [(name, "hi", k - 1)]
                dve_out += [(name, "lo", k - 1)]
    elif name[1] < LAST - 1:
        for k in range(n):
            act_out += [(name, "u", k), (name, "hi", k), (name, "x", k)]
    else:
        act_out = [(name, "x", k) for k in range(n)]
    scales = [(name, "scale", k) for k in range(n)]
    if name[0] == "x" and name[1] < LAST - 1:
        dve_out = [(name, what, k) for m in range(n // 2) for what in ("scale", "lo") for k in out_tiles(name, m)]
    else:
        dve_out = scales + dve_out
    return {
        "mean": ([(name, "mean")], [(name, "center", k) for k in range(n)], [(name, "sq", k) for k in range(n)],
                 [(name, what, k) for what in ("pre", "sq")[name[0] == "x":] for k in range(1, n)]),
        "var": ([(name, "var")], [], [], []),
        "read": ([], [(name, "small", 0)], [], []),
        "small": ([], [(name, "small", k) for k in range(1, SMALL)] + [(name, "diag", k) for k in range(T // P)], [], []),
        "rstd": ([(name, "rstd")], [], [], []),
        "out": ([], dve_out, act_out, []),
    }


AT_STAT, AT_DVE, AT_ACT, AT_POOL = norm_events()
MIXERS = [s for s, (_, m, _) in enumerate(STAGES) if not m]


def attention_events():
    dve, act = [], []
    for s in MIXERS:
        for j in range(QT + 1):
            dve += [(s, "sin", j)] + ([(s, "cos", j)] if j == QT else []) + [(s, "rope", j)] + ([(s, "rope2", j)] if j == QT else [])
        for n in range(NCH + 3):
            if n < NCH:
                dve += [(s, "mask", n)] if n == 0 and STAGES[s][2] == 0 else []
                dve += [(s, "max", n), (s, "negmax", n), (s, "sink", n)]
            if 1 <= n <= NCH:
                dve += [(s, e, n - 1) for e in ("den", "inv", "probs")]
            if n >= 3:
                dve += [(s, "lo", n - 3)]
        act += [(s, "v", 0), (s, "v", 1)]
        for n in range(NCH + 2):
            if n < NCH:
                act += [(s, "exp", n, i) for i in range(QT)] + [(s, "esink", n)]
            if 1 <= n <= NCH:
                act += [(s, "probsT", n - 1)]
            if n >= 2:
                act += [(s, "hi", n - 2)]
    return number(dve), number(act)


AT_ADVE, AT_AACT = attention_events()
C_NORM_PE = {2: "var", 3: "rstd"}
C_NORM_ACT = {2: "squares", 5: 0, 6: 1, 7: 2, 8: 3}
C_NORM_DVE = {1: "center", 4: "small", 5: "scale", 6: 0, 7: 1, 8: 2, 9: 3}
POOL_TAPS = 5
TAPS = CONV_K - POOL_TAPS + 2
GATE = 6

NCHUNK = 3 * D // T
CHUNKS_BEFORE = 4
ADA_AT = {(0, "out"): (6, 1), (1, "out"): (10, 0.5)}
for _g in range(6):
    ADA_AT[2 + _g // 4, _g % 4] = (12 + 2 * _g, 0.5)
FOLD_AT = {0: [("ss", 0)], "out of 0": [("gate", 0)], 1: [("ss", 1)], 2: [("gate", 1)], 3: [("ss", 2), ("gate", 2)],
           4: [("ss", 3), ("gate", 3)]}
AT_FOLD = {}
_n = 0
for _s in FOLD_AT:
    for _what, _i in FOLD_AT[_s]:
        _n += 2 if _what == "gate" else 5 if _i else 3
        AT_FOLD[_what, _i] = _n


def ada_steps(s, phase, st_):
    if (s, phase) not in ADA_AT:
        return []
    first, rate = ADA_AT[s, phase]
    if rate == 1:
        return [(first, st_.m, (0, 1))]
    return [(first, st_.trip, (st_.u,))]


OUT_AT = (LAST, LAST_G - 1)


def taps_done(n):
    return 1 + TAPS * n


def build(nc, a):
    ctx = ExitStack()
    with ctx:
        def sb(name, shape, dt=F32, stack=ctx):
            return stack.enter_context(nc.sbuf_tensor(name, shape, dt))

        def sem(name):
            return ctx.enter_context(nc.semaphore(name))

        x = sb("x", [P, DT, SEQ])
        u_hi = [sb(f"u_hi{b}", [P, DT, T], F32R) for b in range(NBLK)]
        u_lo = [sb(f"u_lo{b}", [P, DT, T], F32R) for b in range(NBLK)]
        raw = [[sb(f"raw{r}{s}", [P, DT, P]) for s in (0, 1)] for r in (0, 1)]
        w_hi = [sb(f"w_hi{s}", [P, DT, P], F32R) for s in (0, 1)]
        w_lo = [sb(f"w_lo{s}", [P, DT, P], F32R) for s in (0, 1)]
        ada = [sb(f"ada{i}", [P, DT // 2, T]) for i in (0, 1)]
        ada_acc = sb("ada_acc", [P, T])
        tmp = sb("tmp", [P, 2, T])
        ssum = sb("ssum", [P, T])
        diag = sb("diag", [P, T // P, P])
        small = sb("small", [P, 2, 3, T // P])
        const = sb("const", [P, 5 * P + 1])
        ident, rot, ones_d, ones_c, ones_1 = (const[:, i * P:(i + 1) * P] for i in range(5))
        inv_freq = const[:, 5 * P:5 * P + 1]
        par1 = sb("par1", [P, DEPTH, N1])
        par2 = sb("par2", [P, DEPTH, N2])
        par3 = sb("par3", [P, DEPTH, N3])
        ccol = sb("ccol", [P, DT])
        mod = sb("mod", [P, DEPTH, 2, 3 * DT])
        gain = sb("gain", [P, len(STAGES) // NBLK, DT])
        bias = sb("bias", [P, len(STAGES) // NBLK, DT])
        nsink = sb("nsink", [P, DEPTH, QT])
        ghist = sb("ghist", [P, FT, FK - 1])
        st = sb("st", [P, 2, 7, QT])

        with ExitStack() as region:
            rows1, rows2, rows3 = (sb(f"rows{i}", [P, DEPTH, P], stack=region) for i in (1, 2, 3))
            rowsc = sb("rowsc", [DT, P], stack=region)
            stage_in = [sb(f"stage_in{i}", [P, D], stack=region) for i in (0, 1)]
            pos = sb("pos", [P, SEQ // FBLK], I32, stack=region)
            ang = sb("ang", [P, SEQ // FBLK], stack=region)
            turns = sb("turns", [P, SEQ // FBLK], stack=region)
            tabs = [sb(f"tab{i}", [P, SEQ // FBLK], stack=region) for i in (0, 1)]
        with ExitStack() as region:
            glu = sb("glu", [P, CT, HIST + T], stack=region)
            conv = sb("conv", [P, CT, T], stack=region)
            q = sb("q", [P, NCH, QT, CHUNK], stack=region)
            kz = sb("kz", [P, 2, CHUNK + T], stack=region)
            v_t = sb("v_t", [P, CHUNK + T], stack=region)
            v = sb("v", [P, NCH, P], stack=region)
            probs = sb("probs", [P, 2, QT, P], stack=region)
            probs_t = sb("probs_t", [P, 2, QT * P], stack=region)
            products = probs_t
            rot_part, k_raw = probs_t[:, 0, :], probs[:, 0, :, :].rearrange("p i n -> p (i n)")
            cs = sb("cs", [P, 2, T], stack=region)
        with ExitStack() as region:
            h_hi = sb("h_hi", [P, max(GROUP), T], F32R, stack=region)
            h_lo = sb("h_lo", [P, max(GROUP), T], F32R, stack=region)
            gate = sb("gate", [P, FK - 1 + T], stack=region)
            gacc = sb("gacc", [P, T], stack=region)
            tanh_c = sb("tanh_c", [P, T], stack=region)
        stage_out = [ada[i // 2][:, i % 2 * 2:i % 2 * 2 + 2, :].rearrange("p a b -> p (a b)") for i in range(4)]
        tab_dram = nc.dram_tensor("rope_tables", [2, P, SEQ // FBLK], F32, kind="Internal").ap()

        bank = [[ctx.enter_context(nc.psum_tensor(f"bank{r}{s}", [P, T], F32)) for s in (0, 1)] for r in (0, 1)]
        sbank = [ctx.enter_context(nc.psum_tensor(f"sbank{i}", [P, QT, P], F32)) for i in (0, 1)]
        b6 = ctx.enter_context(nc.psum_tensor("b6", [P, T], F32))
        b7 = ctx.enter_context(nc.psum_tensor("b7", [P, T], F32))

        raw_in = [[sem(f"raw_in{r}{s}") for s in (0, 1)] for r in (0, 1)]
        hi_ready = [sem(f"hi_ready{s}") for s in (0, 1)]
        lo_ready = [sem(f"lo_ready{s}") for s in (0, 1)]
        slab_done = [sem(f"slab_done{s}") for s in (0, 1)]
        bank_free = [[sem(f"bank_free{r}{s}") for s in (0, 1)] for r in (0, 1)]
        stat_done = sem("stat_done")
        norm_dve = sem("norm_dve")
        norm_act = sem("norm_act")
        norm_pool = sem("norm_pool")
        conv_step = sem("conv_step")
        sigmoid_done = sem("sigmoid_done")
        glu_done = sem("glu_done")
        tap_product = sem("tap_product")
        tap_added = sem("tap_added")
        gate_step = sem("gate_step")
        ghist_clear = sem("ghist_clear")
        gate_act = sem("gate_act")
        hist_ready = sem("hist_ready")
        cs_in = sem("cs_in")
        rot_done = sem("rot_done")
        rope_cos = sem("rope_cos")
        v_done = sem("v_done")
        scores_done = sem("scores_done")
        probs_t_done = sem("probs_t_done")
        pv_done = sem("pv_done")
        att_dve = sem("att_dve")
        att_act = sem("att_act")
        in_const = sem("in_const")
        in_sinks = sem("in_sinks")
        in_pos = sem("in_pos")
        in_x = [sem("in_x0"), sem("in_x1")]
        in_ada = [sem("in_ada0"), sem("in_ada1")]
        tab_out = sem("tab_out")
        set_pe = sem("set_pe")
        set_dve = sem("set_dve")
        set_act = sem("set_act")
        x_t_done = sem("x_t_done")
        x_evac = [sem("x_evac0"), sem("x_evac1")]
        ada_add = sem("ada_add")
        ada_sum = sem("ada_sum")
        ada_copied = sem("ada_copied")
        fold_step = sem("fold_step")
        y_t_done = sem("y_t_done")
        y_evac = [sem("y_evac0"), sem("y_evac1")]
        y_out = [sem(f"y_out{i}") for i in range(4)]

        def rot_bank(j):
            return (bank[1][0][:], bank[1][1][:], b6[:], b7[:], sbank[0][:].rearrange("p i n -> p (i n)"))[j]

        def stat_bank(name, what):
            return bank[1][what == "var"] if name[0] == "c" else b7

        def norm_sum(name):
            return diag[:].rearrange("p a b -> p (a b)") if name[0] == "c" else ssum[:]

        def diagonals(name):
            return ada_acc[:].rearrange("p (a b) -> p a b", b=P) if name[0] == "c" else diag[:]

        def qkv_copied(s, j):
            pair = FIRST[s] + CONV_PAIRS + j // 2
            return bank_free[pair % 2][j % 2], pair // 2 + 2

        TT = SEQ // P
        w_ada = {0: a["w_ada_mix"], 1: a["w_ada_ffn"]}

        block = ctx.enter_context(nc.Block())

        @block.sync
        def _(sp):
            def load_ada(base, more, half):
                l, m = base // NCHUNK // 2, base // NCHUNK % 2
                if not isinstance(more, int) or base + more:
                    sp.wait_ge(ada_add, more * DT + DT * (base - 1) + DT // 2 * (half + 1))
                src = w_ada[m][l, half * D // 2:(half + 1) * D // 2, bass.ds((more + base % NCHUNK) * T, T)]
                sp.dma_start(ada[half][:], src.rearrange("(k p) n -> p k n", p=P)).then_inc(in_ada[half], 16)

            def load_adas(s, phase, st_):
                for base, more, halves in ada_steps(s, phase, st_):
                    for half in halves:
                        load_ada(base, more, half)

            def load_x(t):
                if t >= 2:
                    sp.wait_ge(x_t_done, 2 * (t - 1))
                sp.dma_start(stage_in[t % 2][:], a["x"][0, t * P:(t + 1) * P, :]).then_inc(in_x[t % 2], 16)

            def load(step, parts):
                if not isinstance(step.P, int) or step.P >= 2:
                    for s in (0, 1):
                        sp.wait_ge(lo_ready[s], step.P - 1)
                for s in (0, 1):
                    pieces = parts(s)
                    for n, (dst, src) in enumerate(pieces):
                        inc = 48 if len(pieces) == 1 else 16 if len(pieces) == 3 or n == 0 else 32
                        sp.dma_start(dst, src).then_inc(raw_in[step.par][s], inc)

            def columns(w, r0, nk, c0):
                return w[r0:r0 + nk * P, bass.ds(c0, P)].rearrange("(k p) m -> p k m", p=P)

            def mixer(s, l, b):
                first = FIRST[s]
                w = a["w_in"][l]
                for st_ in pairs(sp, first, CONV_PAIRS, straight=s == 0):
                    load(st_, lambda side: [(raw[st_.par][side][:],
                                             columns(w, 0, DT, st_.m * P + (CONV_CH if side == 0 else 0)))])
                    if s == 0 and st_.m < 2:
                        for half in (0, 1):
                            load_ada(CHUNKS_BEFORE + st_.m, 0, half)
                if s == 0:
                    sp.wait_ge(tab_out, 32)
                for i in (0, 1):
                    table = tab_dram[i].rearrange("(f k) n -> f (k n)", k=FBLK)[:, b * T:(b + 1) * T]
                    for r in range(0, P, HEAD):
                        for r0 in (r, r + HALF):
                            sp.dma_start(cs[r0:r0 + HALF, i, :], table).then_inc(cs_in, 16)
                        sp.dma_start(cs[r + ROT:r + HEAD, i, :], a["plain"][i]).then_inc(cs_in, 16)
                for st_ in pairs(sp, first + CONV_PAIRS, QKV_PAIRS):
                    def parts(side):
                        j = 2 * st_.m + side
                        if j >= QT:
                            return [(raw[st_.par][side][:], columns(w, 0, DT, K0 + (j - QT) * P))]
                        return [(raw[st_.par][side][:, :, g * HEAD:(g + 1) * HEAD],
                                 w[:, Q0 + (g * QT + j) * HEAD:Q0 + (g * QT + j + 1) * HEAD].rearrange("(k p) m -> p k m", p=P))
                                for g in (0, 1)]
                    load(st_, parts)
                w = a["w_out"][l]
                for st_ in pairs(sp, first + CONV_PAIRS + QKV_PAIRS, OUT_PAIRS):
                    def parts(side):
                        c0 = (st_.m * 2 + side) * P
                        dst = raw[st_.par][side]
                        return [(dst[:, 0:CT, :], columns(w, 0, CT, c0))] + [
                            (dst[g * HEAD:(g + 1) * HEAD, CT:DT, :],
                             w[CONV_CH + g * QT * HEAD:CONV_CH + (g + 1) * QT * HEAD, bass.ds(c0, P)].rearrange("(j d) m -> d j m", d=HEAD))
                            for g in (0, 1)]
                    load(st_, parts)
                    load_adas(s, "out", st_)

            def mlp(s, l, b):
                first = FIRST[s]
                for g, n in enumerate(GROUP):
                    w = a["w_up"][l]
                    for st_ in pairs(sp, first, n):
                        load(st_, lambda side: [(raw[st_.par][side][:],
                                                 columns(w, 0, DT, (st_.m + START[g]) * P + (F if side == 0 else 0)))])
                    first += n
                    w = a["w_down"][l]
                    for st_ in pairs(sp, first, DOWN_PAIRS):
                        load(st_, lambda side: [(raw[st_.par][side][:, 0:n, :],
                                                 columns(w, START[g] * P, n, (st_.m * 2 + side) * P))])
                        load_adas(s, g, st_)
                    first += DOWN_PAIRS

            for t in range(TT):
                load_x(t)
                if t < CHUNKS_BEFORE:
                    for half in (0, 1):
                        load_ada(t, 0, half)
            sp.wait_ge(set_act, SET_ACT["table", 1])
            for i in (0, 1):
                sp.dma_start(tab_dram[i], tabs[i][:]).then_inc(tab_out, 16)
            for s, (l, m, b) in enumerate(STAGES):
                (mlp if m else mixer)(s, l, b)
            for t in range(TT):
                sp.wait_ge(y_evac[0], t + 1)
                sp.wait_ge(y_evac[1], t + 1)
                sp.dma_start(a["out"][0, t * P:(t + 1) * P, :], stage_out[t % 4]).then_inc(y_out[t % 4], 16)
            for i in range(4):
                sp.wait_ge(y_out[i], 16 * TT // 4)

        @block.tensor
        def _(pe):
            pe.wait_ge(in_const, 16 * IN_CONST)
            srcs = [(rows1[:, l, :], N1) for l in range(DEPTH)] + [(rows2[:, l, :], N2) for l in range(DEPTH)]
            for i, (r, n) in enumerate(srcs):
                ins = pe.transpose(b6[:, i * P:i * P + n], r[0:n, :], ident[0:n, 0:n])
            ins.then_inc(set_pe, 1)
            for i, (r, n) in enumerate([(rows3[:, 0, :], N3), (rows3[:, 1, :], N3), (rowsc, DT)]):
                ins = pe.transpose(b7[:, i * P:i * P + n], r[0:n, :], ident[0:n, 0:n])
            ins.then_inc(set_pe, 1)

            free6 = [set_dve, SET_DVE["par", 0]]
            free7 = [set_dve, SET_DVE["par", 1]]

            def take6(s, v):
                pe.wait_ge(*free6)
                free6[:] = s, v

            def take7(s, v):
                pe.wait_ge(*free7)
                free7[:] = s, v

            def sum_ada(base, more):
                pe.wait_ge(ada_add, more * DT + DT * (base + 1))
                pe.wait_ge(*free6)
                if not isinstance(more, int) or base + more:
                    pe.wait_ge(ada_copied, more + base)
                for i in range(T // P):
                    ins = pe.matmul(b6[:, i:i + 1], ada_acc[:, i * P:(i + 1) * P], ones_1[:, 0:1], start=True, stop=True)
                ins.then_inc(ada_sum, 1)

            def sum_adas(s, phase, st_):
                for base, more, halves in ada_steps(s, phase, st_):
                    if halves[-1] == 1:
                        sum_ada(base, more)

            def adas_summed(s, phase):
                if (s, phase) in ADA_AT:
                    n0, rate = ADA_AT[s, phase]
                    free6[:] = ada_copied, n0 + int(rate * DOWN_PAIRS)

            for t in range(TT):
                pe.wait_ge(in_x[t % 2], 16 * (t // 2 + 1))
                for half in (0, 1):
                    if t >= 2:
                        pe.wait_ge(x_evac[half], t - 1)
                    for k in range(4):
                        ins = pe.transpose(bank[t % 2][half][:, k * P:(k + 1) * P],
                                           stage_in[t % 2][:, (half * 4 + k) * P:(half * 4 + k + 1) * P], ident)
                    ins.then_inc(x_t_done, 1)
                if 1 <= t <= CHUNKS_BEFORE:
                    sum_ada(t - 1, 0)
            free6[:] = ada_copied, CHUNKS_BEFORE

            def slab(step, side, nk, rhs, ready=None):
                pe.wait_ge(lo_ready[side], step.P + 1)
                pe.wait_ge(bank_free[step.par][side], step.half + 1)
                out = bank[step.par][side]
                for k in range(nk):
                    if ready:
                        ready(k)
                    hi, lo = rhs(k)
                    pe.matmul(out[:], w_hi[side][:, k, :], hi, start=k == 0, stop=False)
                    pe.matmul(out[:], w_hi[side][:, k, :], lo, start=False, stop=False)
                    ins = pe.matmul(out[:], w_lo[side][:, k, :], hi, start=False, stop=k == nk - 1)
                ins.then_inc(slab_done[side], 1)

            def stat(name, what):
                n, ones = (DT, ones_d) if name[0] == "x" else (CT, ones_c)
                out = stat_bank(name, what)
                take = take7 if out is b7 else lambda s, v: None
                if what == "mean":
                    if name[0] == "x":
                        pe.wait_ge(norm_pool, AT_POOL["sum", name[1], DT - 1])
                    else:
                        pe.wait_ge(norm_pool, AT_POOL[name, "pre", n - 1])
                    take(norm_dve, AT_DVE[name, "center", n - 1])
                    ins = pe.matmul(out[:], ones, norm_sum(name), start=True, stop=True)
                elif what == "var":
                    pe.wait_ge(norm_pool, AT_POOL[name, "sq", n - 1])
                    take(norm_dve, AT_DVE[name, "small", 0])
                    for i in range(T // P):
                        ins = pe.matmul(out[:, i:i + 1], norm_sum(name)[:, i * P:(i + 1) * P], ones[:, 0:1], start=True, stop=True)
                else:
                    pe.wait_ge(norm_dve, AT_DVE[name, "diag", T // P - 1])
                    take(norm_dve, AT_DVE[name, "scale", n - 1])
                    ins = pe.matmul(out[:], ones_1, diagonals(name).rearrange("p a b -> p (a b)"), start=True, stop=True)
                ins.then_inc(stat_done, 1)

            def mixer(s, l, b):
                first, mi = FIRST[s], MIXERS.index(s)
                for st_ in pairs(pe, first, CONV_PAIRS, straight=True):
                    for side in (0, 1):
                        first_slab = s == 0 and st_.m == 0 and side == 0
                        if s and side == 0:
                            pe.wait_ge(norm_dve, need_u(s, DT - 1))
                        slab(st_, side, DT, lambda k: (u_hi[b][:, k, :], u_lo[b][:, k, :]),
                             (lambda k: pe.wait_ge(norm_dve, need_u(s, k))) if first_slab else None)
                        if s and st_.m == 0 and side == 0:
                            stat(("x", s - 1), "mean")
                    if s == 0 and st_.m < 2:
                        sum_ada(CHUNKS_BEFORE + st_.m, 0)
                if s == 0:
                    free6[:] = ada_copied, NCHUNK
                for st_ in pairs(pe, first + CONV_PAIRS, QKV_PAIRS):
                    for side in (0, 1):
                        slab(st_, side, DT, lambda k: (u_hi[b][:, k, :], u_lo[b][:, k, :]))
                def rotate(j):
                    pe.wait_ge(*qkv_copied(s, j))
                    if j == 2:
                        take6(att_dve, AT_ADVE[s, "sin", j])
                    elif j == 3:
                        take7(att_dve, AT_ADVE[s, "sin", j])
                    elif j == QT:
                        pe.wait_ge(conv_step, taps_done(CT * (mi + 1)))
                    elif j < 2:
                        for i in range(QT + 2):
                            pe.wait_ge(*qkv_copied(s, i))
                    pe.matmul(rot_bank(j), rot, q[:, :, j, :] if j < QT else k_raw,
                              start=True, stop=True).then_inc(rot_done, 1)

                for j in range(QT):
                    rotate(j)
                pe.wait_ge(*qkv_copied(s, QT + 1))
                pe.wait_ge(hist_ready, 2 * (mi + 1))
                for i in (0, 1):
                    for n in range(NCH // 2):
                        c = (i * NCH // 2 + n) * CHUNK
                        ins = pe.transpose(bank[0][i][:, n * P:(n + 1) * P], v_t[:, c:c + P], ident)
                    ins.then_inc(v_done, 1)
                rotate(QT)

                def scores(n):
                    if n == 0:
                        pe.wait_ge(att_dve, AT_ADVE[s, "rope2", QT])
                    if n >= 2:
                        pe.wait_ge(att_act, AT_AACT[s, "exp", n - 2, QT - 1])
                    else:
                        pe.wait_ge(conv_step, taps_done(CT * (mi + 1)))
                    for g in (0, 1):
                        for pr in (0, 1):
                            qq = q[:, n, 2 * pr:2 * pr + 2, :].rearrange("p j t -> p (j t)")
                            ins = pe.matmul(sbank[n % 2][:, 2 * g + pr, :], qq, kz[:, g, n * CHUNK:n * CHUNK + P],
                                            start=True, stop=True)
                    ins.then_inc(scores_done, 1)

                scores(0)
                scores(1)
                stat(("c", s), "mean")
                for n in range(NCH):
                    if n + 2 < NCH:
                        scores(n + 2)
                    pe.wait_ge(att_dve, AT_ADVE[s, "probs", n])
                    (take7 if n % 2 else take6)(att_act, AT_AACT[s, "probsT", n])
                    for i in range(QT):
                        ins = pe.transpose((b7 if n % 2 else b6)[:, i * P:(i + 1) * P], probs[:, n % 2, i, :], ident)
                    ins.then_inc(probs_t_done, 1)
                    pe.wait_ge(att_act, AT_AACT[s, "probsT", n])
                    if n == 0:
                        pe.wait_ge(att_act, AT_AACT[s, "v", 1])
                    if n >= 2:
                        pe.wait_ge(att_dve, AT_ADVE[s, "lo", n - 2])
                    for g in (0, 1):
                        ins = pe.matmul(bank[0][n % 2][g * HEAD:(g + 1) * HEAD, 0:2 * P], v[:, n, g * HEAD:(g + 1) * HEAD],
                                        probs_t[:, n % 2, g * 2 * P:(g + 1) * 2 * P], start=True, stop=True)
                    ins.then_inc(pv_done, 1)
                    if n in C_NORM_PE:
                        stat(("c", s), C_NORM_PE[n])
                if s:
                    stat(("x", s - 1), "var")
                pe.wait_ge(norm_dve, AT_DVE[("c", s), "lo", CT - 1])
                pe.wait_ge(att_dve, AT_ADVE[s, "lo", NCH - 1])
                for st_ in pairs(pe, first + CONV_PAIRS + QKV_PAIRS, OUT_PAIRS, straight=True):
                    for side in (0, 1):
                        slab(st_, side, DT, lambda k: (u_hi[b][:, k, :], u_lo[b][:, k, :]))
                    if s and st_.m == 0:
                        stat(("x", s - 1), "rstd")
                    sum_adas(s, "out", st_)
                adas_summed(s, "out")

            def token_major(out, t, half):
                for k in range(4):
                    ins = pe.transpose(out[:, k * P:(k + 1) * P], x[:, half * 4 + k, t * P:(t + 1) * P], ident)
                ins.then_inc(y_t_done, 1)

            def mlp(s, l, b):
                first = FIRST[s]
                for k in range(DT):
                    pe.wait_ge(norm_dve, need_u(s, k))
                for g, n in enumerate(GROUP):
                    for st_ in pairs(pe, first, n):
                        for side in (0, 1):
                            slab(st_, side, DT, lambda k: (u_hi[b][:, k, :], u_lo[b][:, k, :]))
                    first += n
                    if g < 2:
                        stat(("x", s - 1), ("mean", "rstd")[g])
                    done = hidden(s, START[g])
                    for st_ in pairs(pe, first, DOWN_PAIRS, straight=(s, g) == OUT_AT):
                        for side in (0, 1):
                            slab(st_, side, n, lambda k: (h_hi[:, k, :], h_lo[:, k, :]),
                                 lambda k: pe.wait_ge(gate_step, done + GATE * (k + 1)))
                        sum_adas(s, g, st_)
                        if (s, g) == OUT_AT:
                            pe.wait_ge(norm_act, AT_ACT[("x", LAST - 1), "x", DT - 1])
                            take6(y_evac[0], st_.m + 1)
                            take7(y_evac[1], st_.m + 1)
                            token_major(b6, st_.m, 0)
                            token_major(b7, st_.m, 1)
                    adas_summed(s, g)
                    first += DOWN_PAIRS
                    if g == 0:
                        stat(("x", s - 1), "var")

            for s, (l, m, b) in enumerate(STAGES):
                (mlp if m else mixer)(s, l, b)
            for what in ("mean", "var", "rstd"):
                stat(("x", LAST), what)
            for t in range(TT // 2, TT):
                for half in (0, 1):
                    if t == TT // 2:
                        for k in range(4 * half, 4 * half + 4):
                            pe.wait_ge(norm_act, AT_ACT[("x", LAST), "x", k])
                    if t >= TT // 2 + 2:
                        pe.wait_ge(y_evac[half], t - 1)
                    token_major(bank[t % 2][half], t, half)

        @block.scalar
        def _(act):
            def copy_ada(base, more):
                act.wait_ge(ada_sum, more + base + 1)
                l, m = base // NCHUNK // 2, base // NCHUNK % 2
                n = T // P
                act.activation(mod[:, l, m, bass.ds((more + base % NCHUNK) * n, n)], b6[:, 0:n], ACT.Copy).then_inc(ada_copied, 1)

            def copy_adas(s, phase, st_):
                for base, more, halves in ada_steps(s, phase, st_):
                    if halves[-1] == 1:
                        copy_ada(base, more)

            def load(dst, src):
                act.dma_start(dst, src).then_inc(in_const, 16)

            load(const[:], a["consts"])
            load(rowsc[:], a["c"].rearrange("o (t p) -> (o t) p", p=P))
            for name, n in ROWS1:
                load(rows1[OFF[name]:OFF[name] + n, :, :], a[name].rearrange("l (t p) -> t l p", p=P))
            for l in range(DEPTH):
                load(rows2[0:N2, l, :], a["conv_w"][l].rearrange("k (t p) -> (k t) p", p=P))
                load(rows3[0:N3, l, :], a["ffn_conv_w"][l].rearrange("k (t p) -> (k t) p", p=P))
            for l in range(DEPTH):
                for s in (0, 1):
                    src = a["sinks"][l].rearrange("(o j s) -> s o j", o=1, s=2)[s]
                    with nc.allow_non_contiguous_dma(reason="eight numbers"):
                        act.dma_start(nsink[s * CHUNK:(s + 1) * CHUNK, l, :], src.to_broadcast([CHUNK, QT])).then_inc(in_sinks, 16)
            for f in range(HALF):
                act.dma_start(pos[f * FBLK:(f + 1) * FBLK, :],
                              a["positions"].rearrange("o (k n) -> (o k) n", k=FBLK)).then_inc(in_pos, 16)

            for t in range(TT):
                act.wait_ge(x_t_done, 2 * t + 1)
                act.activation(x[:, 0:4, t * P:(t + 1) * P], bank[t % 2][0][:].rearrange("p (k n) -> p k n", k=4),
                               ACT.Copy).then_inc(x_evac[0], 1)
                if 1 <= t <= CHUNKS_BEFORE:
                    copy_ada(t - 1, 0)
                if t == 2:
                    for i in (0, 1):
                        act.wait_ge(set_dve, SET_DVE["reduced", i])
                        act.activation(tabs[i][:], tabs[i][:], ACT.Sin).then_inc(set_act, 1)
            def split_hi(step, side):
                nxt = Step(0, step.half, step.par + 1)
                act.wait_ge(raw_in[1 - step.par][side], (nxt.half) * 48 + 48)
                act.wait_ge(slab_done[side], step.P + 1)
                act.activation(w_hi[side][:], raw[1 - step.par][side][:], ACT.Copy).then_inc(hi_ready[side], 1)

            def inputs(name, k, b, i, xk):
                act.activation(tmp[:, k % 2, :], xk, ACT.Identity, bias=bias[:, i, k:k + 1],
                               scale=gain[:, i, k:k + 1]).then_inc(norm_act, 1)
                act.wait_ge(norm_act, AT_ACT[(name, "u", k) if name[0] == "x" else (*name, "u", k)])
                act.activation(u_hi[b][:, k, :], tmp[:, k % 2, :], ACT.Copy).then_inc(norm_act, 1)

            for side in (0, 1):
                act.wait_ge(raw_in[0][side], 48)
                act.activation(w_hi[side][:], raw[0][side][:], ACT.Copy).then_inc(hi_ready[side], 1)

            def first_inputs(b, tiles):
                act.wait_ge(x_evac[1], TT)
                act.wait_ge(x_evac[0], TT)
                act.wait_ge(fold_step, AT_FOLD["ss", 0])
                for k in tiles:
                    if k >= 2:
                        act.wait_ge(norm_dve, AT_DVE["init", b, "lo", k - 2])
                    inputs(("init", b), k, b, 0, x[:, k, b * T:(b + 1) * T])

            first_inputs(0, range(DT))

            def squares(name, xk, tiles):
                for k in tiles:
                    act.wait_ge(norm_dve, AT_DVE[name, "center", k])
                    if k >= 2:
                        act.wait_ge(norm_pool, AT_POOL[name, "sq", max(k - 2, 1)])
                    act.activation(tmp[:, k % 2, :], xk(k), ACT.Square).then_inc(norm_act, 1)

            def norm_out(s, tiles):
                l, m, b = STAGES[s]
                name = ("x", s)
                g0 = OFF["ln2_g" if m else "ln1_g"]
                b0 = OFF["ln2_b" if m else "ln1_b"]
                if s < 2 * DEPTH + 1 and ("ss", s // NBLK + 1) in AT_FOLD:
                    act.wait_ge(fold_step, AT_FOLD["ss", s // NBLK + 1])
                for k in tiles:
                    xk = x[:, k, b * T:(b + 1) * T]
                    act.wait_ge(norm_dve, AT_DVE[name, "scale", k])
                    if s < LAST - 1:
                        if k >= 2:
                            act.wait_ge(norm_dve, AT_DVE[name, "lo", k - 2])
                        inputs(name, k, b, s // NBLK + 1, xk)
                    act.activation(xk, xk, ACT.Identity, bias=par1[:, l, b0 + k:b0 + k + 1],
                                   scale=par1[:, l, g0 + k:g0 + k + 1]).then_inc(norm_act, 1)

            def conv_norm_out(s, k):
                l, m, b = STAGES[s]
                name = ("c", s)
                g0, b0 = OFF["conv_ln_g"], OFF["conv_ln_b"]
                if k < CT:
                    act.wait_ge(norm_dve, AT_DVE[name, "scale", k])
                    act.activation(conv[:, k, :], conv[:, k, :], ACT.Identity, bias=par1[:, l, b0 + k:b0 + k + 1],
                                   scale=par1[:, l, g0 + k:g0 + k + 1]).then_inc(norm_act, 1)
                    act.wait_ge(norm_act, AT_ACT[name, "z", k])
                    if k >= 2:
                        act.wait_ge(norm_dve, AT_DVE[name, "lo", k - 2])
                    act.activation(tmp[:, k % 2, :], conv[:, k, :], ACT.Tanh, scale=0.5).then_inc(norm_act, 1)
                if k:
                    act.wait_ge(norm_dve, AT_DVE[name, "m", k - 1])
                    act.activation(u_hi[b][:, k - 1, :], tmp[:, (k - 1) % 2, :], ACT.Copy, scale=0.5).then_inc(norm_act, 1)

            def mixer(s, l, b):
                first, mi = FIRST[s], MIXERS.index(s)
                if s == 0:
                    act.wait_ge(tab_out, 32)
                act.wait_ge(hist_ready, 2 * mi + 1)
                def tap_products(j):
                    act.wait_ge(glu_done, CT * mi + j + 1)
                    for k in range(POOL_TAPS):
                        n = (CT * mi + j) * (POOL_TAPS - 1) + k
                        dst = conv[:, j, :] if k == 0 else products[:, n % 2, :]
                        if k and n > 2:
                            act.wait_ge(tap_added, n - 2)
                        act.activation(dst, glu[:, j, k:k + T], ACT.Copy,
                                       scale=par2[:, l, j + k * CT:j + k * CT + 1]).then_inc(tap_product, 1)

                for st_ in pairs(act, first, CONV_PAIRS, straight=True):
                    j = st_.m
                    act.wait_ge(slab_done[0], st_.P + 1)
                    act.activation(conv[:, j, :], bank[st_.par][0][:], ACT.Tanh, scale=0.5).then_inc(bank_free[st_.par][0], 1)
                    split_hi(st_, 0)
                    act.wait_ge(bank_free[st_.par][0], st_.half + 2)
                    act.activation(conv[:, j, :], conv[:, j, :], ACT.Identity, bias=ones_1[:, 0:1]).then_inc(sigmoid_done, 1)
                    act.wait_ge(slab_done[1], st_.P + 1)
                    act.activation(glu[:, j, HIST:], bank[st_.par][1][:], ACT.Copy).then_inc(bank_free[st_.par][1], 1)
                    split_hi(st_, 1)
                    if s == 0 and j < 2:
                        copy_ada(CHUNKS_BEFORE + j, 0)
                    if j:
                        tap_products(j - 1)
                for st_ in pairs(act, first + CONV_PAIRS, QKV_PAIRS, straight=True):
                    for side in (0, 1):
                        j = 2 * st_.m + side
                        act.wait_ge(slab_done[side], st_.P + 1)
                        if j == QT + 1:
                            act.wait_ge(hist_ready, 2 * (mi + 1))
                        dst = q[:, :, j, :] if j < QT else k_raw if j == QT else v_t[:, CHUNK:]
                        src = chunked(bank[st_.par][side][:]) if j < QT else bank[st_.par][side][:]
                        act.activation(dst, src, ACT.Copy).then_inc(bank_free[st_.par][side], 1)
                        split_hi(st_, side)
                        if j == 1:
                            tap_products(CT - 1)
                    if s:
                        squares(("x", s - 1), lambda k: x[:, k, (1 - b) * T:(2 - b) * T], sq_tiles(st_.m))
                for i in (0, 1):
                    act.wait_ge(v_done, 2 * mi + i + 1)
                    act.activation(v[:, i * NCH // 2:(i + 1) * NCH // 2, :], bank[0][i][:].rearrange("p (n f) -> p n f", f=P),
                                   ACT.Copy).then_inc(att_act, 1)
                for n in range(NCH + 2):
                    if n < NCH:
                        r = n % 2
                        act.wait_ge(att_dve, AT_ADVE[s, "sink", n])
                        for i in range(QT):
                            act.activation(probs[:, r, i, :], sbank[r][:, i, :], ACT.Exp, bias=st[:, r, 1, i:i + 1],
                                           scale=SCALE, accum_out=st[:, r, 3, i:i + 1]).then_inc(att_act, 1)
                        act.activation(st[:, r, 4, :], st[:, r, 2, :], ACT.Exp).then_inc(att_act, 1)
                    if 1 <= n <= NCH:
                        act.wait_ge(probs_t_done, mi * NCH + n)
                        act.activation(probs_t[:, (n - 1) % 2, :], (b6 if n % 2 else b7)[:], ACT.Copy).then_inc(att_act, 1)
                    if n >= 2:
                        act.wait_ge(pv_done, mi * NCH + n - 1)
                        act.activation(u_hi[b][:, CT:DT, (n - 2) * CHUNK:(n - 1) * CHUNK],
                                       bank[0][n % 2][:, 0:QT * CHUNK].rearrange("p (j t) -> p j t", j=QT), ACT.Copy).then_inc(att_act, 1)
                    if n in C_NORM_ACT:
                        if C_NORM_ACT[n] == "squares":
                            squares(("c", s), lambda k: conv[:, k, :], range(CT))
                        else:
                            conv_norm_out(s, C_NORM_ACT[n])
                conv_norm_out(s, CT)
                for st_ in pairs(act, first + CONV_PAIRS + QKV_PAIRS, OUT_PAIRS, straight=True):
                    if s:
                        norm_out(s - 1, out_tiles(("x", s - 1), st_.m))
                    else:
                        act.wait_ge(norm_dve, AT_DVE[("c", s), "lo", CT - 1])
                        first_inputs(1, both(st_.m))
                    split_hi(st_, 0)
                    split_hi(st_, 1)
                    copy_adas(s, "out", st_)

            def stage(t, src):
                act.wait_ge(y_t_done, 2 * t + 1)
                if t >= 4:
                    act.wait_ge(y_out[t % 4], 16 * (t // 4))
                act.activation(stage_out[t % 4][:, 0:D // 2], src[:], ACT.Copy).then_inc(y_evac[0], 1)

            def mlp(s, l, b):
                first = FIRST[s]
                for g, size in enumerate(GROUP):
                    for st_ in pairs(act, first, size):
                        f = st_.m + START[g]
                        n = f + FT * mlp_no(s)
                        act.wait_ge(slab_done[0], st_.P + 1)
                        act.wait_ge(gate_step, n * GATE + 1)
                        ps = bank[st_.par][0]
                        act.activation(gacc[:], ps[:], ACT.Identity, bias=par1[:, l, bass.ds(f + OFF["ffn_conv_b"], 1)],
                                       scale=par3[:, l, bass.ds(f + 2 * FT, 1)]).then_inc(gate_act, 1)
                        act.activation(gate[:, FK - 1:], ps[:], ACT.Copy).then_inc(bank_free[st_.par][0], 1)
                        split_hi(st_, 0)
                        act.wait_ge(gate_step, n * GATE + 5)
                        act.activation(tanh_c[:], gacc[:], ACT.Tanh, scale=0.5).then_inc(gate_act, 1)
                        split_hi(st_, 1)
                        act.wait_ge(bank_free[st_.par][1], st_.half + 2)
                        act.activation(h_hi[:, bass.ds(st_.m, 1), :], gacc[:].rearrange("p (o n) -> p o n", o=1),
                                       ACT.Copy).then_inc(gate_act, 1)
                    first += size
                    last = s == LAST and g == LAST_G
                    for st_ in pairs(act, first, DOWN_PAIRS, straight=g < 2 or last or (s, g) == OUT_AT):
                        if g == 0:
                            squares(("x", s - 1), lambda k: x[:, k, (1 - b) * T:(2 - b) * T], both(st_.m))
                        elif g == 1:
                            norm_out(s - 1, both(st_.m))
                        for side in (0, 1):
                            if not last or st_.m < DOWN_PAIRS - 1:
                                split_hi(st_, side)
                        copy_adas(s, g, st_)
                        if (s, g) == OUT_AT:
                            stage(st_.m, b6)
                    first += DOWN_PAIRS

            for s, (l, m, b) in enumerate(STAGES):
                (mlp if m else mixer)(s, l, b)
            squares(("x", LAST), lambda k: x[:, k, T:], range(DT))
            norm_out(LAST, range(DT))
            for t in range(TT // 2, TT):
                stage(t, bank[t % 2][0])

        @block.vector
        def _(dve):
            setup = [0]

            def step(ins):
                ins.then_inc(set_dve, 1)
                setup[0] += 1
                dve.wait_ge(set_dve, setup[0])

            def done(name):
                assert SET_DVE[name] == setup[0], (name, setup[0])

            dve.wait_ge(set_pe, 1)
            step(dve.tensor_copy(par1[:], b6[:, 0:2 * P].rearrange("p (l n) -> p l n", l=DEPTH)[:, :, 0:N1]))
            step(dve.tensor_scalar(par2[:], b6[:, 2 * P:4 * P].rearrange("p (l n) -> p l n", l=DEPTH)[:, :, 0:N2], 0.5, None, ALU.mult))
            done(("par", 0))
            dve.wait_ge(set_pe, 2)
            step(dve.tensor_copy(par3[:], b7[:, 0:2 * P].rearrange("p (l n) -> p l n", l=DEPTH)[:, :, 0:N3]))
            step(dve.tensor_copy(ccol[:], b7[:, 2 * P:2 * P + DT]))
            done(("par", 1))
            dve.wait_ge(in_sinks, 16 * 2 * DEPTH)
            step(dve.tensor_scalar(nsink[:], nsink[:], -1.0, None, ALU.mult))

            def evac_x(t):
                dve.wait_ge(x_t_done, 2 * t + 2)
                dve.tensor_copy(x[:, 4:8, t * P:(t + 1) * P],
                                bank[t % 2][1][:].rearrange("p (k n) -> p k n", k=4)).then_inc(x_evac[1], 1)

            def add_ada(base, more, half):
                dve.wait_ge(in_ada[half], more * 16 + 16 * (base + 1))
                for k in range(half * DT // 2, (half + 1) * DT // 2):
                    w = ada[half][:, k % (DT // 2), :]
                    if k == 0:
                        if not isinstance(more, int) or base + more:
                            dve.wait_ge(ada_sum, more + base)
                        dve.tensor_scalar(ada_acc[:], w, ccol[:, 0:1], None, ALU.mult).then_inc(ada_add, 1)
                    else:
                        dve.wait_ge(ada_add, more * DT + base * DT + k)
                        dve.scalar_tensor_tensor(out=ada_acc[:], in0=w, scalar=ccol[:, k:k + 1], in1=ada_acc[:],
                                                 op0=ALU.mult, op1=ALU.add).then_inc(ada_add, 1)

            def add_adas(s, phase, st_):
                for base, more, halves in ada_steps(s, phase, st_):
                    for half in halves:
                        add_ada(base, more, half)

            folds = [0]

            def fold(what, i):
                def fold_one(ins):
                    ins.then_inc(fold_step, 1)
                    folds[0] += 1
                    dve.wait_ge(fold_step, folds[0])

                l, m = i // 2, i % 2
                o = OFF["b_ada_ffn" if m else "b_ada_mix"]
                dve.wait_ge(ada_copied, NCHUNK * i + (4 if what == "ss" else 6))
                if what == "gate":
                    g = mod[:, l, m, 2 * DT:]
                    fold_one(dve.tensor_tensor(g, g, par1[:, l, o + 2 * DT:o + 3 * DT], ALU.add))
                    fold_one(dve.tensor_scalar(g, g, 1.0, INV_ALPHA, ALU.add, ALU.mult))
                else:
                    shift, scale = mod[:, l, m, 0:DT], mod[:, l, m, DT:2 * DT]
                    both = mod[:, l, m, 0:2 * DT]
                    fold_one(dve.tensor_tensor(both, both, par1[:, l, o:o + 2 * DT], ALU.add))
                    if i == 0:
                        fold_one(dve.tensor_scalar(gain[:, 0, :], scale, 1.0, None, ALU.add))
                        fold_one(dve.tensor_copy(bias[:, 0, :], shift))
                    else:
                        pl, pm = (i - 1) // 2, (i - 1) % 2
                        g0, b0 = (OFF["ln2_g"], OFF["ln2_b"]) if pm else (OFF["ln1_g"], OFF["ln1_b"])
                        fold_one(dve.tensor_scalar(scale, scale, 1.0, None, ALU.add))
                        fold_one(dve.tensor_tensor(gain[:, i, :], par1[:, pl, g0:g0 + DT], scale, ALU.mult))
                        fold_one(dve.tensor_tensor(bias[:, i, :], par1[:, pl, b0:b0 + DT], scale, ALU.mult))
                        fold_one(dve.tensor_tensor(bias[:, i, :], bias[:, i, :], shift, ALU.add))
                assert AT_FOLD[what, i] == folds[0]

            def angles():
                dve.wait_ge(in_pos, 16 * HALF)
                step(dve.tensor_copy(ang[:], pos[:]))
                step(dve.tensor_scalar(ang[:], ang[:], inv_freq, None, ALU.mult))
                for i, (quarter, shift) in enumerate(((0.25, np.pi / 2), (0.0, 0.0))):
                    step(dve.tensor_scalar(turns[:], ang[:], float(np.float32(0.5 / np.pi)), quarter, ALU.mult, ALU.add))
                    step(dve.tensor_scalar(turns[:], turns[:], MAGIC, None, ALU.add))
                    step(dve.tensor_scalar(turns[:], turns[:], -MAGIC, None, ALU.add))
                    for n, part in enumerate(TWO_PI):
                        step(dve.scalar_tensor_tensor(out=tabs[i][:], in0=turns[:], scalar=-part, in1=(tabs[i] if n else ang)[:],
                                                      op0=ALU.mult, op1=ALU.add))
                    step(dve.tensor_scalar(tabs[i][:], tabs[i][:], shift, PI_DOWN, ALU.add, ALU.min))
                    step(dve.tensor_scalar(tabs[i][:], tabs[i][:], -PI_DOWN, None, ALU.max))
                    done(("reduced", i))

            for t in range(TT):
                evac_x(t)
                if t < CHUNKS_BEFORE:
                    for half in (0, 1):
                        add_ada(t, 0, half)
                if t == 0:
                    angles()
            for r in (0, 1):
                for side in (0, 1):
                    dve.wait_ge(x_evac[side], TT)
                    dve.memset(small[:, 0, 0, 2 * r + side:2 * r + side + 1], 0.0).then_inc(bank_free[r][side], 1)
            dve.memset(ghist[:], 0.0).then_inc(gate_step, 1)
            dve.memset(small[:, 1, 0, 0:1], 0.0).then_inc(conv_step, 1)

            def split_lo(step_, side):
                dve.wait_ge(hi_ready[side], step_.P + 2)
                dve.tensor_tensor(w_lo[side][:], raw[1 - step_.par][side][:], w_hi[side][:].bitcast(F32),
                                  ALU.subtract).then_inc(lo_ready[side], 1)

            def input_lo(b, k, hi_at):
                dve.wait_ge(norm_act, hi_at)
                dve.tensor_tensor(u_lo[b][:, k, :], tmp[:, k % 2, :], u_hi[b][:, k, :].bitcast(F32),
                                  ALU.subtract).then_inc(norm_dve, 1)

            for what in FOLD_AT[0]:
                fold(*what)
            for side in (0, 1):
                dve.wait_ge(hi_ready[side], 1)
                dve.tensor_tensor(w_lo[side][:], raw[0][side][:],
                                  w_hi[side][:].bitcast(F32), ALU.subtract).then_inc(lo_ready[side], 1)
            for k in range(DT):
                input_lo(0, k, AT_ACT["init", 0, "hi", k])

            def center(name, xk, tiles):
                dve.wait_ge(stat_done, AT_STAT[name, "mean"])
                for k in tiles:
                    dve.tensor_tensor(xk(k), xk(k), stat_bank(name, "mean")[:], ALU.subtract).then_inc(norm_dve, 1)

            def small_step(name, n, ins):
                ins.then_inc(norm_dve, 1)
                dve.wait_ge(norm_dve, AT_DVE[name, "small", n])

            def read_var(name):
                eps = EPS / ALPHA2 if name[0] == "x" else EPS
                dve.wait_ge(stat_done, AT_STAT[name, "var"])
                small_step(name, 0, dve.tensor_scalar(small[:, name[0] == "c", 0, :], stat_bank(name, "var")[:, 0:T // P],
                                                      eps, None, ALU.add))

            def rsqrt(name):
                var, y, t = (small[:, name[0] == "c", i, :] for i in range(3))
                small_step(name, 1, dve.tensor_scalar(t.bitcast(I32), var.bitcast(I32), 1, None, ALU.logical_shift_right))
                small_step(name, 2, dve.tensor_scalar(y.bitcast(I32), t.bitcast(I32), -1.0, 1597463007.0, ALU.mult, ALU.add))
                for i in range(3):
                    small_step(name, 3 * i + 3, dve.tensor_tensor(t, y, y, ALU.mult))
                    small_step(name, 3 * i + 4, dve.scalar_tensor_tensor(out=t, in0=t, scalar=-0.5, in1=var, op0=ALU.mult, op1=ALU.mult))
                    small_step(name, 3 * i + 5, dve.scalar_tensor_tensor(out=y, in0=t, scalar=1.5, in1=y, op0=ALU.add, op1=ALU.mult))
                for i in range(T // P):
                    dve.tensor_scalar(diagonals(name)[:, i, :], ident, y[:, i:i + 1], None, ALU.mult).then_inc(norm_dve, 1)

            def rescale(name, xk, tiles):
                dve.wait_ge(stat_done, AT_STAT[name, "rstd"])
                for k in tiles:
                    dve.tensor_tensor(xk(k), xk(k), stat_bank(name, "rstd")[:], ALU.mult).then_inc(norm_dve, 1)

            def inputs_lo(s, tiles):
                if s < LAST - 1:
                    for k in tiles:
                        input_lo(STAGES[s][2], k, AT_ACT[("x", s), "hi", k])

            def residual(l, m, b, st_):
                for side in (0, 1):
                    k = st_.m * 2 + side
                    dve.wait_ge(slab_done[side], st_.P + 1)
                    xk = x[:, bass.ds(k, 1), b * T:(b + 1) * T]
                    dve.scalar_tensor_tensor(out=xk, in0=bank[st_.par][side][:].rearrange("p (o n) -> p o n", o=1),
                                             scalar=mod[:, l, m, bass.ds(k + 2 * DT, 1)],
                                             in1=xk, op0=ALU.mult, op1=ALU.add).then_inc(bank_free[st_.par][side], 1)

            def conv_norm(s, part):
                name, ck = ("c", s), lambda k: conv[:, k, :]
                b = STAGES[s][2]
                if part == "center":
                    center(name, ck, range(CT))
                elif part == "small":
                    read_var(name)
                    rsqrt(name)
                elif part == "scale":
                    rescale(name, ck, range(CT))
                else:
                    k = part
                    if k < CT:
                        dve.wait_ge(norm_act, AT_ACT[name, "th", k])
                        t = tmp[:, k % 2, :]
                        dve.scalar_tensor_tensor(out=t, in0=t, scalar=1.0, in1=conv[:, k, :], op0=ALU.add,
                                                 op1=ALU.mult).then_inc(norm_dve, 1)
                    if k:
                        dve.wait_ge(norm_act, AT_ACT[name, "hi", k - 1])
                        dve.scalar_tensor_tensor(out=u_lo[b][:, k - 1, :], in0=tmp[:, (k - 1) % 2, :], scalar=0.5,
                                                 in1=u_hi[b][:, k - 1, :].bitcast(F32), op0=ALU.mult,
                                                 op1=ALU.subtract).then_inc(norm_dve, 1)

            def mixer(s, l, b):
                first, mi = FIRST[s], MIXERS.index(s)
                other = lambda k: x[:, k, (1 - b) * T:(2 - b) * T]
                if s == 0:
                    for n in (CHUNKS_BEFORE, CHUNKS_BEFORE + 1):
                        for half in (0, 1):
                            add_ada(n, 0, half)
                if s:
                    center(("x", s - 1), other, range(DT))
                dve.wait_ge(hist_ready, 2 * mi + 1)
                for st_ in pairs(dve, first, CONV_PAIRS):
                    j = st_.m
                    before = (j + CT * mi) * TAPS + 1
                    dve.wait_ge(glu_done, j + CT * mi + 1)
                    sums = [sbank[i][:].rearrange("p i (o n) -> p o (i n)", o=1) for i in (0, 1)]
                    for k in range(POOL_TAPS, CONV_K):
                        n = k - POOL_TAPS
                        src = glu[:, bass.ds(j, 1), k:k + T]
                        w = par2[:, l, bass.ds(j + k * CT, 1)]
                        acc = sums[n % 2]
                        if n == 0:
                            dve.wait_ge(conv_step, before)
                            ins = dve.tensor_scalar(acc, src, w, par1[:, l, bass.ds(j + OFF["conv_b"], 1)], ALU.mult, ALU.add)
                        elif n == 1:
                            ins = dve.tensor_scalar(acc, src, w, None, ALU.mult)
                        else:
                            dve.wait_ge(conv_step, before + n - 1)
                            ins = dve.scalar_tensor_tensor(out=acc, in0=src, scalar=w, in1=acc, op0=ALU.mult, op1=ALU.add)
                        ins.then_inc(conv_step, 1)
                    dve.wait_ge(tap_added, (j + CT * mi + 1) * (POOL_TAPS - 1))
                    total = conv[:, bass.ds(j, 1), :]
                    for i in (0, 1):
                        dve.wait_ge(conv_step, before + CONV_K - POOL_TAPS + i)
                        dve.tensor_tensor(total, total, sums[i], ALU.add).then_inc(conv_step, 1)
                dve.wait_ge(cs_in, CS_IN * (mi + 1))
                sin = cs[:, 1, :]
                for j in range(QT + 1):
                    shape = chunked if j < QT else lambda t: t
                    src = q[:, :, j, :] if j < QT else k_raw
                    part = shape(rot_part)
                    if j:
                        dve.wait_ge(att_dve, AT_ADVE[s, "rope", j - 1])
                    dve.wait_ge(rot_done, (QT + 1) * mi + j + 1)
                    dve.tensor_tensor(part, shape(rot_bank(j)), shape(sin), ALU.mult).then_inc(att_dve, 1)
                    dve.wait_ge(att_dve, AT_ADVE[s, "sin", j])
                    if j < QT:
                        dve.wait_ge(rope_cos, QT * mi + j + 1)
                    else:
                        dve.tensor_tensor(k_raw, k_raw, cs[:, 0, :], ALU.mult).then_inc(att_dve, 1)
                        dve.wait_ge(att_dve, AT_ADVE[s, "cos", j])
                    if j < QT:
                        dve.tensor_tensor(src, src, part, ALU.add).then_inc(att_dve, 1)
                    else:
                        dve.wait_ge(hist_ready, 2 * (mi + 1))
                        for g in (0, 1):
                            h = slice(g * HEAD, (g + 1) * HEAD)
                            dve.tensor_tensor(kz[h, g, CHUNK:], k_raw[h, :], rot_part[h, :], ALU.add).then_inc(att_dve, 1)
                for n in range(NCH + 3):
                    if n < NCH:
                        r = n % 2
                        dve.wait_ge(scores_done, mi * NCH + n + 1)
                        if n == 0 and b == 0:
                            dve.memset(sbank[r][:, :, 0:CHUNK], NEG).then_inc(att_dve, 1)
                            dve.wait_ge(att_dve, AT_ADVE[s, "mask", n])
                        dve.tensor_reduce(st[:, r, 0, :], sbank[r][:], AX.X, ALU.max).then_inc(att_dve, 1)
                        dve.wait_ge(att_dve, AT_ADVE[s, "max", n])
                        dve.scalar_tensor_tensor(out=st[:, r, 1, :], in0=st[:, r, 0, :], scalar=-SCALE, in1=nsink[:, l, :],
                                                 op0=ALU.mult, op1=ALU.min).then_inc(att_dve, 1)
                        dve.wait_ge(att_dve, AT_ADVE[s, "negmax", n])
                        dve.tensor_tensor(st[:, r, 2, :], st[:, r, 1, :], nsink[:, l, :], ALU.subtract).then_inc(att_dve, 1)
                    if 1 <= n <= NCH:
                        r = (n - 1) % 2
                        dve.wait_ge(att_act, AT_AACT[s, "esink", n - 1])
                        dve.tensor_tensor(st[:, r, 5, :], st[:, r, 3, :], st[:, r, 4, :], ALU.add).then_inc(att_dve, 1)
                        dve.wait_ge(att_dve, AT_ADVE[s, "den", n - 1])
                        dve.reciprocal(st[:, r, 6, :], st[:, r, 5, :]).then_inc(att_dve, 1)
                        dve.wait_ge(att_dve, AT_ADVE[s, "inv", n - 1])
                        dve.tensor_tensor(probs[:, r, :, :], probs[:, r, :, :],
                                          st[:, r, 6, :].rearrange("p (i o) -> p i o", o=1).to_broadcast([P, QT, P]),
                                          ALU.mult).then_inc(att_dve, 1)
                    if n >= 3:
                        dve.wait_ge(att_act, AT_AACT[s, "hi", n - 3])
                        c = slice((n - 3) * CHUNK, (n - 2) * CHUNK)
                        dve.tensor_tensor(u_lo[b][:, CT:DT, c], bank[0][(n - 3) % 2][:, 0:QT * CHUNK].rearrange("p (j t) -> p j t", j=QT),
                                          u_hi[b][:, CT:DT, c].bitcast(F32), ALU.subtract).then_inc(att_dve, 1)
                    if n in C_NORM_DVE:
                        conv_norm(s, C_NORM_DVE[n])
                conv_norm(s, CT)
                if s == 0:
                    fold("gate", 0)
                if s:
                    read_var(("x", s - 1))
                    rsqrt(("x", s - 1))
                wait_x(dve, s)
                for st_ in pairs(dve, first + CONV_PAIRS + QKV_PAIRS, OUT_PAIRS, straight=True):
                    if s:
                        if st_.m:
                            rescale(("x", s - 1), other, out_tiles(("x", s - 1), st_.m))
                            inputs_lo(s - 1, out_tiles(("x", s - 1), st_.m))
                    else:
                        for k in both(st_.m):
                            input_lo(1, k, AT_ACT["init", 1, "hi", k])
                    add_adas(s, "out", st_)
                    residual(l, 0, b, st_)

            def wait_x(eng, s):
                if s >= 2:
                    eng.wait_ge(norm_act, AT_ACT[("x", s - 2), "x", DT - 1])

            def stage(t, src):
                dve.wait_ge(y_t_done, 2 * t + 2)
                if t >= 4:
                    dve.wait_ge(y_out[t % 4], 16 * (t // 4))
                dve.tensor_copy(stage_out[t % 4][:, D // 2:], src[:]).then_inc(y_evac[1], 1)

            def mlp(s, l, b):
                first = FIRST[s]
                other = lambda k: x[:, k, (1 - b) * T:(2 - b) * T]
                if b == 0 and l:
                    dve.wait_ge(gate_step, hidden(s, 0))
                    dve.memset(ghist[:], 0.0).then_inc(ghist_clear, 1)
                    dve.wait_ge(ghist_clear, l)
                for g, size in enumerate(GROUP):
                    for st_ in pairs(dve, first, size):
                        f = st_.m + START[g]
                        n = f + FT * mlp_no(s)
                        at = n * GATE + 1
                        hist = ghist[:, bass.ds(f, 1), :].rearrange("p o n -> p (o n)")
                        dve.wait_ge(slab_done[0], st_.P + 1)
                        dve.tensor_copy(gate[:, 0:FK - 1], hist).then_inc(gate_step, 1)
                        dve.wait_ge(bank_free[st_.par][0], st_.half + 2)
                        dve.wait_ge(gate_step, at + 1)
                        dve.scalar_tensor_tensor(out=gacc[:], in0=gate[:, 1:1 + T], scalar=par3[:, l, bass.ds(f + FT, 1)],
                                                 in1=gacc[:], op0=ALU.mult, op1=ALU.add).then_inc(gate_step, 1)
                        dve.tensor_copy(hist, gate[:, T:T + FK - 1]).then_inc(gate_step, 1)
                        dve.wait_ge(gate_step, at + 2)
                        dve.scalar_tensor_tensor(out=gacc[:], in0=gate[:, 0:T], scalar=par3[:, l, bass.ds(f, 1)],
                                                 in1=gacc[:], op0=ALU.mult, op1=ALU.add).then_inc(gate_step, 1)
                        split_lo(st_, 0)
                        dve.wait_ge(gate_act, n * 3 + 2)
                        dve.scalar_tensor_tensor(out=tanh_c[:], in0=tanh_c[:], scalar=1.0, in1=gacc[:],
                                                 op0=ALU.add, op1=ALU.mult).then_inc(gate_step, 1)
                        dve.wait_ge(gate_step, at + 5)
                        dve.wait_ge(slab_done[1], st_.P + 1)
                        dve.scalar_tensor_tensor(out=gacc[:], in0=bank[st_.par][1][:], scalar=0.5, in1=tanh_c[:],
                                                 op0=ALU.mult, op1=ALU.mult).then_inc(bank_free[st_.par][1], 1)
                        dve.wait_ge(gate_act, n * 3 + 3)
                        o = lambda t: t.rearrange("p (o n) -> p o n", o=1)
                        dve.tensor_tensor(h_lo[:, bass.ds(st_.m, 1), :], o(gacc[:]),
                                          h_hi[:, bass.ds(st_.m, 1), :].bitcast(F32), ALU.subtract).then_inc(gate_step, 1)
                    first += size
                    if g == 0:
                        wait_x(dve, s)
                    last = s == LAST and g == LAST_G
                    for st_ in pairs(dve, first, DOWN_PAIRS, straight=g < 2 or last or (s, g) == OUT_AT):
                        if g == 0:
                            center(("x", s - 1), other, both(st_.m))
                        elif g == 1:
                            rescale(("x", s - 1), other, both(st_.m))
                            inputs_lo(s - 1, both(st_.m))
                        add_adas(s, g, st_)
                        if not last or st_.m < DOWN_PAIRS - 1:
                            split_lo(st_, 0)
                        residual(l, 1, b, st_)
                        if (s, g) == OUT_AT:
                            stage(st_.m, b7)
                    first += DOWN_PAIRS
                    if g == 0:
                        read_var(("x", s - 1))
                        rsqrt(("x", s - 1))

            for s, (l, m, b) in enumerate(STAGES):
                if s:
                    for what in FOLD_AT.get(s, []):
                        fold(*what)
                (mlp if m else mixer)(s, l, b)
            lastx = lambda k: x[:, k, T:]
            center(("x", LAST), lastx, range(DT))
            read_var(("x", LAST))
            rsqrt(("x", LAST))
            rescale(("x", LAST), lastx, range(DT))
            for t in range(TT // 2, TT):
                stage(t, bank[t % 2][1])

        @block.gpsimd
        def _(pool):
            def split_lo(step_, side):
                pool.wait_ge(hi_ready[side], step_.P + 2)
                pool.tensor_tensor(w_lo[side][:], raw[1 - step_.par][side][:], w_hi[side][:].bitcast(F32),
                                   ALU.subtract).then_inc(lo_ready[side], 1)

            def sum_squares(name, tiles):
                pool.wait_ge(stat_done, AT_STAT[name, "mean"])
                for k in tiles:
                    if k == 0:
                        continue
                    pool.wait_ge(norm_act, AT_ACT[name, "sq", k])
                    if k > 1:
                        pool.wait_ge(norm_pool, AT_POOL[name, "sq", k - 1])
                    total = norm_sum(name)
                    pool.tensor_tensor(total, tmp[:, k % 2, :], tmp[:, 0, :] if k == 1 else total, ALU.add).then_inc(norm_pool, 1)

            def clear_sum(s):
                if s:
                    pool.wait_ge(stat_done, AT_STAT[("x", s - 1), "var"])
                pool.memset(ssum[:], 0.0).then_inc(norm_pool, 1)

            def add_residual(s, st_, side):
                k = st_.m * 2 + side
                b = STAGES[s][2]
                pool.wait_ge(norm_pool, k + AT_POOL["sum", s, -1])
                pool.wait_ge(bank_free[st_.par][side], st_.half + 2)
                pool.tensor_tensor(ssum[:].rearrange("p (o n) -> p o n", o=1), ssum[:].rearrange("p (o n) -> p o n", o=1),
                                   x[:, bass.ds(k, 1), b * T:(b + 1) * T], ALU.add).then_inc(norm_pool, 1)

            def mixer(s, l, b):
                first, mi = FIRST[s], MIXERS.index(s)
                if b == 0:
                    if s == 0:
                        pool.wait_ge(fold_step, AT_FOLD["ss", 0])
                        pool.wait_ge(tab_out, 32)
                    else:
                        for side in (0, 1):
                            pool.wait_ge(slab_done[side], first)
                    pool.memset(glu[:, :, 0:HIST], 0.0).then_inc(hist_ready, 1)
                    pool.memset(v_t[:, 0:CHUNK], 0.0)
                    pool.memset(kz[:], 0.0).then_inc(hist_ready, 1)
                else:
                    pool.wait_ge(conv_step, taps_done(CT * mi))
                    pool.tensor_copy(glu[:, :, 0:HIST], glu[:, :, T:T + HIST]).then_inc(hist_ready, 1)
                    pool.tensor_copy(v_t[:, 0:CHUNK], v_t[:, T:T + CHUNK])
                    pool.tensor_copy(kz[:, :, 0:CHUNK], kz[:, :, T:T + CHUNK]).then_inc(hist_ready, 1)
                def add_taps(j):
                    for k in range(1, POOL_TAPS):
                        n = (CT * mi + j) * (POOL_TAPS - 1) + k
                        pool.wait_ge(tap_product, (CT * mi + j) * POOL_TAPS + k + 1)
                        if k > 1:
                            pool.wait_ge(tap_added, n - 1)
                        pool.tensor_tensor(conv[:, j, :], conv[:, j, :], products[:, n % 2, :], ALU.add).then_inc(tap_added, 1)

                for st_ in pairs(pool, first, CONV_PAIRS, straight=True):
                    j = st_.m
                    split_lo(st_, 0)
                    pool.wait_ge(sigmoid_done, CT * mi + j + 1)
                    pool.wait_ge(bank_free[st_.par][1], st_.half + 2)
                    pool.tensor_tensor(glu[:, j, HIST:], conv[:, j, :], glu[:, j, HIST:], ALU.mult).then_inc(glu_done, 1)
                    split_lo(st_, 1)
                    if j:
                        add_taps(j - 1)
                for st_ in pairs(pool, first + CONV_PAIRS, QKV_PAIRS, straight=True):
                    for side in (0, 1):
                        split_lo(st_, side)
                    if st_.m == 0:
                        add_taps(CT - 1)
                    if s:
                        sum_squares(("x", s - 1), sq_tiles(st_.m))
                pool.wait_ge(cs_in, CS_IN * (mi + 1))
                for j in range(QT):
                    pool.wait_ge(rot_done, (QT + 1) * mi + j + 1)
                    pool.tensor_tensor(q[:, :, j, :], q[:, :, j, :], chunked(cs[:, 0, :]), ALU.mult).then_inc(rope_cos, 1)
                for k in range(1, CT):
                    pool.wait_ge(conv_step, taps_done(CT * mi + k + 1))
                    if k > 1:
                        pool.wait_ge(norm_pool, AT_POOL[("c", s), "pre", k - 1])
                    total = norm_sum(("c", s))
                    pool.tensor_tensor(total, conv[:, k, :], conv[:, 0, :] if k == 1 else total, ALU.add).then_inc(norm_pool, 1)
                sum_squares(("c", s), range(CT))
                clear_sum(s)
                for st_ in pairs(pool, first + CONV_PAIRS + QKV_PAIRS, OUT_PAIRS):
                    for side in (0, 1):
                        split_lo(st_, side)
                    for side in (0, 1):
                        add_residual(s, st_, side)

            def mlp(s, l, b):
                first = FIRST[s]
                for g, size in enumerate(GROUP):
                    for st_ in pairs(pool, first, size):
                        split_lo(st_, 1)
                    first += size
                    if g == LAST_G:
                        clear_sum(s)
                    last = s == LAST and g == LAST_G
                    for st_ in pairs(pool, first, DOWN_PAIRS, straight=g == 0 or last):
                        if g == 0:
                            sum_squares(("x", s - 1), both(st_.m))
                        if not last or st_.m < DOWN_PAIRS - 1:
                            split_lo(st_, 1)
                        if g == LAST_G:
                            for side in (0, 1):
                                add_residual(s, st_, side)
                    first += DOWN_PAIRS

            for s, (l, m, b) in enumerate(STAGES):
                (mlp if m else mixer)(s, l, b)
            sum_squares(("x", LAST), range(DT))


def mlp_no(s):
    return sum(m for _, m, _ in STAGES[:s])


def hidden(s, f):
    return 1 + GATE * (f + FT * mlp_no(s))


def need_u(s, k):
    if s < NBLK:
        return AT_DVE["init", s, "lo", k]
    return AT_DVE[("x", s - 2), "lo", k]


CS_IN = 16 * 2 * 3 * (P // HEAD)
IN_CONST = 2 + len(ROWS1) + 2 * DEPTH
MAGIC = 12582912.0
PI_DOWN = float(np.nextafter(np.float32(np.pi), np.float32(0.0)))


def two_pi_parts():
    rest, parts = 2 * np.pi, []
    for _ in range(3):
        e = 2.0 ** (np.floor(np.log2(rest)) - 7)
        parts.append(float(np.floor(rest / e) * e))
        rest -= parts[-1]
    return parts + [float(np.float32(rest))]


TWO_PI = two_pi_parts()
SET_DVE = {("par", 0): 2, ("par", 1): 4}
for _i in (0, 1):
    SET_DVE["reduced", _i] = 4 + 1 + 2 + (_i + 1) * (3 + len(TWO_PI) + 2)
SET_ACT = {("table", 0): 1, ("table", 1): 2}


def constants():
    ident = np.eye(P, dtype=np.float32)
    rot = np.zeros((P, P), np.float32)
    freq = np.float32(THETA ** (-2.0 * (np.arange(P)[:, None] // FBLK) / ROT))
    for g in range(P // HEAD):
        for j in range(HALF):
            lo, hi = g * HEAD + j, g * HEAD + HALF + j
            rot[hi, lo] = -1.0
            rot[lo, hi] = 1.0
    ones = np.ones((P, P), np.float32)
    return np.concatenate([ident, rot, ones * np.float32(1.0 / D), ones * np.float32(1.0 / CONV_CH), ones, freq], axis=1)


def plain():
    return np.stack([np.full((HEAD - ROT, T), v, np.float32) for v in (1.0, 0.0)])


_INS = ["x", "c", "positions", "w_ada_mix", "b_ada_mix", "w_in", "conv_w", "conv_b", "conv_ln_g", "conv_ln_b",
        "sinks", "w_out", "ln1_g", "ln1_b", "w_ada_ffn", "b_ada_ffn", "w_up", "ffn_conv_w", "ffn_conv_b",
        "w_down", "ln2_g", "ln2_b"]


def kernel(**inputs):
    import concourse.bacc as _bacc
    from concourse.bass_utils import run_bass_kernel_spmd as _run

    nc = _bacc.Bacc("TRN2", target_bir_lowering=False, num_devices=1)
    arrays, args = {}, {}
    made = {"consts": constants(), "plain": plain()}
    for name in _INS + list(made):
        arr = made[name] if name in made else np.ascontiguousarray(inputs[name])
        arrays[f"in_{name}_dram"] = arr
        args[name] = nc.dram_tensor(f"in_{name}_dram", arr.shape, mybir.dt.from_np(arr.dtype), kind="ExternalInput").ap()
    args["out"] = nc.dram_tensor("out_dram", (1, SEQ, D), F32, kind="ExternalOutput").ap()
    build(nc, args)
    r = _run(nc, [arrays], core_ids=[0])
    return r.results[0]["out_dram"]
```
